# Optimizing a Trainium2 kernel written in Bass

```python
import math
import jax
import jax.numpy as jnp
from jax import lax
import numpy as np

D_MODEL = 1024
BATCH = 1
SEQ = 1024
DEPTH = 2
DEC_BATCH = 8
DEC_SEQ = 1
PAST_LEN = 1024
PAGE_SIZE = 128

N_EVEN = (DEPTH + 1) // 2
N_ODD = DEPTH // 2
DH_A = 64
H_A = (D_MODEL // 2) // DH_A
H_IDX = 8
D_IDX = 64
TOPK_MAX = 256
QBLK = 128
NUM_BUCKETS = 32
MAX_DISTANCE = 128
H_R = 4
DV_R = (D_MODEL // 2) // H_R
DK_R = DV_R // 2
RET_CHUNK = 128
ROPE_BASE = 10000.0
D_INNER = 2 * D_MODEL
P_SSM = 64
NH_SSM = D_INNER // P_SSM
G_SSM = 8
HPG = NH_SSM // G_SSM
N_STATE = 128
CONV_W = 4
CONV_DIM = D_INNER + 2 * G_SSM * N_STATE
SSD_CHUNK = 128
D_FF = 4 * D_MODEL
EPS = 1e-6

EVEN_SIZES = (H_A * DH_A, H_A * DH_A, H_A * DH_A, H_IDX * D_IDX, D_IDX, H_IDX,
              H_R * DK_R, H_R * DK_R, H_R * DV_R, H_R * DV_R)
EVEN_IN = sum(EVEN_SIZES)
EVEN_OUT = H_A * DH_A + H_R * DV_R
ODD_SIZES = (D_INNER, CONV_DIM, NH_SSM)
ODD_IN = sum(ODD_SIZES)

kernel_name = 'dsa_retention_ssd_hybrid_step'

def _split(x, sizes):
    return jnp.split(x, np.cumsum(sizes)[:-1].tolist(), axis=-1)

def to_blocks(a, size):
    b, l = a.shape[0], a.shape[1]
    return jnp.moveaxis(a.reshape((b, l // size, size) + a.shape[2:]), 1, 0)

def from_blocks(a):
    a = jnp.moveaxis(a, 0, 1)
    return a.reshape((a.shape[0], a.shape[1] * a.shape[2]) + a.shape[3:])

def rmsnorm(x, g):
    x32 = x.astype(jnp.float32)
    y = x32 * lax.rsqrt(jnp.mean(x32 * x32, axis=-1, keepdims=True) + EPS)
    return (y * g.astype(jnp.float32)).astype(x.dtype)

def mlp(h, w_up, w_down):
    return jnp.square(jax.nn.relu(h @ w_up)) @ w_down

def rotary(x, pos):
    half = x.shape[-1] // 2
    inv = ROPE_BASE ** (-jnp.arange(half, dtype=jnp.float32) / half)
    ang = pos.astype(jnp.float32)[:, None] * inv[None, :]
    cos = jnp.cos(ang)[None, :, None, :]
    sin = jnp.sin(ang)[None, :, None, :]
    x32 = x.astype(jnp.float32)
    x1, x2 = x32[..., :half], x32[..., half:]
    return jnp.concatenate([x1 * cos - x2 * sin, x1 * sin + x2 * cos], axis=-1).astype(x.dtype)

def t5_bucket(dist):
    max_exact = NUM_BUCKETS // 2
    d = jnp.maximum(dist, 0)
    ratio = jnp.log(jnp.maximum(d, max_exact).astype(jnp.float32) / max_exact) / math.log(MAX_DISTANCE / max_exact)
    large = max_exact + (ratio * (NUM_BUCKETS - max_exact)).astype(jnp.int32)
    return jnp.where(d < max_exact, d, jnp.minimum(large, NUM_BUCKETS - 1))

def indexer_topk(iq, iw, ik, tpos, k_sel):
    s = jnp.einsum('bqhd,bld->bqhl', iq, ik) * (D_IDX ** -0.5)
    score = jnp.einsum('bqh,bqhl->bql', iw, jax.nn.relu(s)).astype(jnp.float32)
    keypos = jnp.arange(ik.shape[1])
    score = jnp.where(keypos[None, None, :] <= tpos[None, :, None], score, -jnp.inf)
    return lax.top_k(score, k_sel)[1]

def sparse_attend(q, kg, vg, idx, tpos, rel_bias):
    dist = tpos[None, :, None] - idx
    bias = jnp.moveaxis(rel_bias[t5_bucket(dist)], -1, 2).astype(jnp.float32)
    logits = jnp.einsum('bqhd,bqkhd->bqhk', q, kg).astype(jnp.float32) * (DH_A ** -0.5) + bias
    logits = jnp.where((dist >= 0)[:, :, None, :], logits, -jnp.inf)
    p = jax.nn.softmax(logits, axis=-1).astype(vg.dtype)
    return jnp.einsum('bqhk,bqkhd->bqhd', p, vg)

def even_project(h, w_in, pos):
    b, l, _ = h.shape
    q, k, v, iq, ik, iw, rq, rk, rv, rg = _split(h @ w_in, EVEN_SIZES)
    q = q.reshape(b, l, H_A, DH_A)
    k = k.reshape(b, l, H_A, DH_A)
    v = v.reshape(b, l, H_A, DH_A)
    iq = iq.reshape(b, l, H_IDX, D_IDX)
    iw = iw * (H_IDX ** -0.5)
    rq = rotary(rq.reshape(b, l, H_R, DK_R), pos)
    rk = rotary(rk.reshape(b, l, H_R, DK_R), pos) * (DK_R ** -0.5)
    rv = rv.reshape(b, l, H_R, DV_R)
    return q, k, v, iq, ik, iw, rq, rk, rv, rg

def retention_chunk(state, q, k, v, log_gamma):
    l = q.shape[1]
    q, k, v = q.astype(jnp.float32), k.astype(jnp.float32), v.astype(jnp.float32)
    n = jnp.arange(l, dtype=jnp.float32)
    diff = n[:, None] - n[None, :]
    causal = diff >= 0
    decay = jnp.where(causal[None], jnp.exp(jnp.where(causal, diff, 0.0)[None] * log_gamma[:, None, None]), 0.0)
    scores = jnp.einsum('bthd,bshd->bhts', q, k) * decay[None]
    inner = jnp.einsum('bhts,bshe->bthe', scores, v)
    cross = jnp.einsum('bthd,bhde->bthe', q, state) * jnp.exp((n[:, None] + 1.0) * log_gamma[None, :])[None, :, :, None]
    kdec = k * jnp.exp((l - 1.0 - n)[:, None] * log_gamma[None, :])[None, :, :, None]
    new_state = state * jnp.exp(l * log_gamma)[None, :, None, None] + jnp.einsum('bshd,bshe->bhde', kdec, v)
    return new_state, inner + cross

def retention_scan(state, rq, rk, rv, chunk):
    log_gamma = jnp.log(1.0 - jnp.exp2(-5.0 - jnp.arange(H_R, dtype=jnp.float32)))
    def step(st, xs):
        return retention_chunk(st, xs[0], xs[1], xs[2], log_gamma)
    st, o = lax.scan(step, state.astype(jnp.float32),
                     (to_blocks(rq, chunk), to_blocks(rk, chunk), to_blocks(rv, chunk)))
    return st, from_blocks(o)

def merge_even(att, o, rg, w_out):
    b, l = att.shape[0], att.shape[1]
    mu = jnp.mean(o, axis=-1, keepdims=True)
    var = jnp.mean(jnp.square(o - mu), axis=-1, keepdims=True)
    on = ((o - mu) * lax.rsqrt(var + EPS)).reshape(b, l, H_R * DV_R)
    ret = jax.nn.silu(rg) * on.astype(rg.dtype)
    return jnp.concatenate([att.reshape(b, l, H_A * DH_A), ret], axis=-1) @ w_out

def even_mixer_prompt(h, w_in, w_out, rel_bias):
    b, s, _ = h.shape
    q, k, v, iq, ik, iw, rq, rk, rv, rg = even_project(h, w_in, jnp.arange(s))
    k_sel = min(TOPK_MAX, s // 4)
    bi = jnp.arange(b)[:, None, None]

    def attend_block(args):
        qb, iqb, iwb, start = args
        tpos = start + jnp.arange(QBLK)
        idx = indexer_topk(iqb, iwb, ik, tpos, k_sel)
        return sparse_attend(qb, k[bi, idx], v[bi, idx], idx, tpos, rel_bias)

    starts = jnp.arange(s // QBLK) * QBLK
    att = from_blocks(lax.map(attend_block, (to_blocks(q, QBLK), to_blocks(iq, QBLK), to_blocks(iw, QBLK), starts)))
    st0 = jnp.zeros((b, H_R, DK_R, DV_R), jnp.float32)
    st, o = retention_scan(st0, rq, rk, rv, RET_CHUNK)
    return merge_even(att, o, rg, w_out), k, v, ik, st

def even_mixer_sample(h, ck, cv, cik, page_table, ret_state, w_in, w_out, rel_bias):
    b, l, _ = h.shape
    past = page_table.shape[1] * PAGE_SIZE
    pos = past + jnp.arange(l)
    q, k, v, iq, ik, iw, rq, rk, rv, rg = even_project(h, w_in, pos)
    ik_past = cik[page_table].reshape(b, past, D_IDX)
    ik_all = jnp.concatenate([ik_past.astype(ik.dtype), ik], axis=1)
    k_sel = min(TOPK_MAX, (past + l) // 4)
    idx = indexer_topk(iq, iw, ik_all, pos, k_sel)
    bi = jnp.arange(b)[:, None, None]
    in_past = (idx < past)[..., None, None]
    pidx = jnp.minimum(idx, past - 1)
    page = page_table[bi, pidx // PAGE_SIZE]
    off = pidx % PAGE_SIZE
    nidx = jnp.clip(idx - past, 0, l - 1)
    kg = jnp.where(in_past, ck[page, off], k[bi, nidx])
    vg = jnp.where(in_past, cv[page, off], v[bi, nidx])
    att = sparse_attend(q, kg, vg, idx, pos, rel_bias)
    st, o = retention_scan(ret_state, rq, rk, rv, l)
    return merge_even(att, o, rg, w_out), k, v, ik, st

def causal_dwconv(xpad, w, bias):
    l = xpad.shape[1] - (CONV_W - 1)
    out = bias
    for j in range(CONV_W):
        out = out + xpad[:, j:j + l] * w[j]
    return out

def ssd_chunk(state, x, dt, bm, cm, a):
    l = x.shape[1]
    x, bm, cm = x.astype(jnp.float32), bm.astype(jnp.float32), cm.astype(jnp.float32)
    acs = jnp.cumsum(dt * a, axis=1)
    causal = jnp.tril(jnp.ones((l, l), dtype=bool))
    seg = acs[:, :, None] - acs[:, None, :]
    lmat = jnp.exp(jnp.where(causal[None, :, :, None, None], seg, -jnp.inf))
    xdt = x * dt[..., None]
    cb = jnp.einsum('btgn,bsgn->btsg', cm, bm)
    y_diag = jnp.einsum('btsg,btsgh,bsghp->btghp', cb, lmat, xdt)
    y_off = jnp.einsum('btgn,bghpn->btghp', cm, state) * jnp.exp(acs)[..., None]
    dec_end = jnp.exp(acs[:, -1:] - acs)
    new_state = state * jnp.exp(acs[:, -1])[..., None, None] + jnp.einsum('bsgn,bsgh,bsghp->bghpn', bm, dec_end, xdt)
    return new_state, y_diag + y_off

def mamba_mixer(h, hist, ssm_state, w_in, conv_w, conv_b, dt_bias, a_log, d_skip, norm_w, w_out, chunk):
    b, l, _ = h.shape
    z, xbc, dt = _split(h @ w_in, ODD_SIZES)
    xpad = jnp.concatenate([hist.astype(xbc.dtype), xbc], axis=1)
    new_hist = xpad[:, l:]
    xbc = jax.nn.silu(causal_dwconv(xpad, conv_w, conv_b))
    xs, bm, cm = _split(xbc, (D_INNER, G_SSM * N_STATE, G_SSM * N_STATE))
    xs = xs.reshape(b, l, G_SSM, HPG, P_SSM)
    bm = bm.reshape(b, l, G_SSM, N_STATE)
    cm = cm.reshape(b, l, G_SSM, N_STATE)
    dt = jax.nn.softplus((dt + dt_bias).astype(jnp.float32)).reshape(b, l, G_SSM, HPG)
    a = -jnp.exp(a_log.astype(jnp.float32)).reshape(G_SSM, HPG)

    def step(st, inp):
        return ssd_chunk(st, inp[0], inp[1], inp[2], inp[3], a)

    st0 = ssm_state.astype(jnp.float32).reshape(b, G_SSM, HPG, P_SSM, N_STATE)
    st, y = lax.scan(step, st0, (to_blocks(xs, chunk), to_blocks(dt, chunk), to_blocks(bm, chunk), to_blocks(cm, chunk)))
    y = from_blocks(y) + d_skip.astype(jnp.float32).reshape(G_SSM, HPG)[:, :, None] * xs.astype(jnp.float32)
    g = (y.reshape(b, l, D_INNER) * jax.nn.silu(z.astype(jnp.float32))).reshape(b, l, G_SSM, D_INNER // G_SSM)
    g = g * lax.rsqrt(jnp.mean(g * g, axis=-1, keepdims=True) + EPS)
    out = (g.reshape(b, l, D_INNER) * norm_w.astype(jnp.float32)).astype(h.dtype) @ w_out
    return out, new_hist, st.reshape(b, NH_SSM, P_SSM, N_STATE)

def setup_inputs(seed: int = 0) -> dict:
    key = jax.random.key(seed)
    ks = jax.random.split(key, 32)
    f32 = jnp.float32

    def nrm(k, shape, scale):
        return jax.random.normal(k, shape, f32) * scale

    n_pages = PAST_LEN // PAGE_SIZE
    n_used = DEC_BATCH * n_pages
    n_pool = n_used + max(1, n_used // 4)
    page_table = jax.random.permutation(ks[0], n_pool)[:n_used].reshape(DEC_BATCH, n_pages).astype(jnp.int32)
    dt0 = jnp.exp(jax.random.uniform(ks[1], (N_ODD, NH_SSM), f32, math.log(1e-3), math.log(1e-1)))
    return {
        'x_prompt': nrm(ks[2], (BATCH, SEQ, D_MODEL), 1.0),
        'x_sample': nrm(ks[3], (DEC_BATCH, DEC_SEQ, D_MODEL), 1.0),
        'cache_k': nrm(ks[4], (N_EVEN, n_pool, PAGE_SIZE, H_A, DH_A), 1.0),
        'cache_v': nrm(ks[5], (N_EVEN, n_pool, PAGE_SIZE, H_A, DH_A), 1.0),
        'cache_idx_k': nrm(ks[6], (N_EVEN, n_pool, PAGE_SIZE, D_IDX), 1.0),
        'state_ret': nrm(ks[7], (N_EVEN, DEC_BATCH, H_R, DK_R, DV_R), 0.5),
        'state_conv': nrm(ks[8], (N_ODD, DEC_BATCH, CONV_W - 1, CONV_DIM), 1.0),
        'state_ssm': nrm(ks[9], (N_ODD, DEC_BATCH, NH_SSM, P_SSM, N_STATE), 0.5),
        'page_table': page_table,
        'rel_bias': nrm(ks[10], (NUM_BUCKETS, H_A), 0.5),
        'norm_mix': 1.0 + nrm(ks[11], (DEPTH, D_MODEL), 0.1),
        'norm_mlp': 1.0 + nrm(ks[12], (DEPTH, D_MODEL), 0.1),
        'norm_final': 1.0 + nrm(ks[13], (D_MODEL,), 0.1),
        'w_in_even': nrm(ks[14], (N_EVEN, D_MODEL, EVEN_IN), D_MODEL ** -0.5),
        'w_out_even': nrm(ks[15], (N_EVEN, EVEN_OUT, D_MODEL), EVEN_OUT ** -0.5),
        'w_in_odd': nrm(ks[16], (N_ODD, D_MODEL, ODD_IN), D_MODEL ** -0.5),
        'conv_w': nrm(ks[17], (N_ODD, CONV_W, CONV_DIM), CONV_W ** -0.5),
        'conv_b': nrm(ks[18], (N_ODD, CONV_DIM), 0.01),
        'dt_bias': dt0 + jnp.log(-jnp.expm1(-dt0)),
        'a_log': jnp.log(jax.random.uniform(ks[19], (N_ODD, NH_SSM), f32, 1.0, 16.0)),
        'd_skip': 1.0 + nrm(ks[20], (N_ODD, NH_SSM), 0.1),
        'ssm_norm': 1.0 + nrm(ks[21], (N_ODD, D_INNER), 0.1),
        'w_out_odd': nrm(ks[22], (N_ODD, D_INNER, D_MODEL), D_INNER ** -0.5),
        'w_up': nrm(ks[23], (DEPTH, D_MODEL, D_FF), D_MODEL ** -0.5),
        'w_down': nrm(ks[24], (DEPTH, D_FF, D_MODEL), D_FF ** -0.5),
    }

def reference(x_prompt, x_sample, cache_k, cache_v, cache_idx_k, state_ret, state_conv, state_ssm, page_table,
              rel_bias, norm_mix, norm_mlp, norm_final, w_in_even, w_out_even, w_in_odd, conv_w, conv_b,
              dt_bias, a_log, d_skip, ssm_norm, w_out_odd, w_up, w_down):
    xp, xs = x_prompt, x_sample
    bp = xp.shape[0]
    k_p, v_p, ik_p, k_s, v_s, ik_s, ret_p, ret_s = [], [], [], [], [], [], [], []
    conv_p, conv_s, ssm_p, ssm_s = [], [], [], []
    for layer in range(DEPTH):
        hp = rmsnorm(xp, norm_mix[layer])
        hs = rmsnorm(xs, norm_mix[layer])
        if layer % 2 == 0:
            e = layer // 2
            yp, kk, vv, ik, st = even_mixer_prompt(hp, w_in_even[e], w_out_even[e], rel_bias)
            k_p.append(kk); v_p.append(vv); ik_p.append(ik); ret_p.append(st)
            ys, kk, vv, ik, st = even_mixer_sample(hs, cache_k[e], cache_v[e], cache_idx_k[e], page_table,
                                                   state_ret[e], w_in_even[e], w_out_even[e], rel_bias)
            k_s.append(kk); v_s.append(vv); ik_s.append(ik); ret_s.append(st)
        else:
            o = layer // 2
            hist0 = jnp.zeros((bp, CONV_W - 1, CONV_DIM), hp.dtype)
            st0 = jnp.zeros((bp, NH_SSM, P_SSM, N_STATE), jnp.float32)
            yp, hc, st = mamba_mixer(hp, hist0, st0, w_in_odd[o], conv_w[o], conv_b[o], dt_bias[o], a_log[o],
                                     d_skip[o], ssm_norm[o], w_out_odd[o], SSD_CHUNK)
            conv_p.append(hc); ssm_p.append(st)
            ys, hc, st = mamba_mixer(hs, state_conv[o], state_ssm[o], w_in_odd[o], conv_w[o], conv_b[o],
                                     dt_bias[o], a_log[o], d_skip[o], ssm_norm[o], w_out_odd[o], xs.shape[1])
            conv_s.append(hc); ssm_s.append(st)
        xp = xp + yp
        xs = xs + ys
        xp = xp + mlp(rmsnorm(xp, norm_mlp[layer]), w_up[layer], w_down[layer])
        xs = xs + mlp(rmsnorm(xs, norm_mlp[layer]), w_up[layer], w_down[layer])
    y_prompt = rmsnorm(xp, norm_final)
    y_sample = rmsnorm(xs, norm_final)
    return (y_prompt, y_sample, jnp.stack(k_p), jnp.stack(v_p), jnp.stack(ik_p), jnp.stack(k_s), jnp.stack(v_s),
            jnp.stack(ik_s), jnp.stack(ret_p), jnp.stack(ret_s), jnp.stack(conv_p), jnp.stack(conv_s),
            jnp.stack(ssm_p), jnp.stack(ssm_s))


_drawn_inputs = setup_inputs


def setup_inputs(seed=0):
    import zlib

    import numpy as np

    out = dict(_drawn_inputs(seed))
    spreads = {}
    factors = {'conv_b': 3.226}
    for name, (base, spread) in spreads.items():
        noise = np.random.default_rng([zlib.crc32(name.encode()), seed]).standard_normal(out[name].shape)
        drawn = base * np.exp(spread * noise) if base else spread * noise
        out[name] = jnp.asarray(drawn.astype(out[name].dtype))
    for name, factor in factors.items():
        out[name] = (out[name] * factor).astype(out[name].dtype)
    return out
```

```python
from contextlib import ExitStack, contextmanager

import numpy as np

import concourse.bass as bass
from concourse import mybir

F32 = mybir.dt.float32
F32R = mybir.dt.float32r
I32 = mybir.dt.int32
ALU = mybir.AluOpType
ACT = mybir.ActivationFunctionType
AX_X = mybir.AxisListType.X

P = 128
D_MODEL = 1024
KT = D_MODEL // P
SEQ = 1024
NBLK = SEQ // P
NS = 8
TOK = SEQ + NS
TT = 344
NT = TOK // TT
PAGES = 8
NPOOL = 80
DH = 64
HA = 8
HIDX = 8
TOPK = 256
NB = 32
HR = 4
DKR = 64
DVR = 128
D_INNER = 2048
PS = 64
NH = 32
G = 8
HPG = NH // G
NST = 128
CW = 4
CONV_DIM = 4096
EPS = 1e-6
BIG = 1e30
TAKEN = -3e38
COL_Q, COL_K, COL_V, COL_IQ, COL_IK, COL_IW, COL_R = 0, 512, 1024, 1536, 2048, 2112, 2120
COL_Z, COL_X, COL_B, COL_C, COL_DT = 0, 2048, 4096, 5120, 6144


class Tally:

    def __init__(self, sem, count=0):
        self.sem, self.count, self.reg = sem, count, None

    def value(self):
        return self.count if self.reg is None else self.reg + self.count

    def up(self, ins, by=1):
        ins.then_inc(self.sem, by)
        self.count += by


def done(eng, ins, tally):
    tally.up(ins)
    eng.wait_ge(tally.sem, tally.value())


@contextmanager
def counted(eng, trips, *tallies):
    kept = [(t, t.count, t.reg) for t, _ in tallies]
    with eng.Fori(0, trips) as i:
        for t, n in tallies:
            t.reg = i * n if t.reg is None else t.reg + i * n
        yield i
    for (t, n), (_, c0, r0) in zip(tallies, kept):
        assert t.count - c0 == n, (t.count - c0, n)
        t.count, t.reg = c0 + n * trips, r0


def shape_constants():
    f = np.float32
    c = {}
    c["ident"] = np.eye(P, dtype=f)
    k = np.arange(P)
    c["future"] = (k[None, :] > k[:, None]).astype(f)
    c["upto"] = (k[:, None] <= k[None, :]).astype(f)
    def bucket(d):
        d = np.maximum(d, 0)
        ratio = np.log(np.maximum(d, 16).astype(f) / f(16)) / f(np.log(8.0))
        large = 16 + (ratio * f(16)).astype(np.int32)
        return np.where(d < 16, d, np.minimum(large, 31))
    x = np.arange(384)
    oh = np.zeros((NB, 384 + P + NS), f)
    oh[bucket(255 - x), x] += 1
    oh[bucket(P - k), 384 + k] += 1
    oh[bucket(0), 384 + P:] += 1
    oh[NB - 1, :] -= 1
    c["buckets"] = oh
    inv = (f(10000.0) ** (-np.arange(32, dtype=f) / f(32))).astype(f)
    pos = np.concatenate([np.arange(SEQ), np.full(NS, SEQ)]).astype(f)
    ang = (pos[None, :] * inv[:, None]).astype(f)
    cos, sin = np.cos(ang).astype(f), np.sin(ang).astype(f)
    c["cos"] = np.tile(cos, (4, 1))
    c["sin"] = np.concatenate([-sin, sin, -sin, sin], 0)
    lg = np.log(1.0 - np.exp2(-5.0 - np.arange(HR, dtype=np.float64)))
    n = np.arange(P)
    dec = np.where(n[None, :] >= n[:, None], np.exp((n[None, :] - n[:, None])[None] * lg[:, None, None]), 0.0)
    c["decay"] = np.ascontiguousarray(dec.transpose(1, 0, 2)).reshape(P, HR * P).astype(f)
    head = lambda pair: np.repeat([2 * pair, 2 * pair + 1], 64)
    c["qdecay"] = np.concatenate([np.exp((n[None, :] + 1) * lg[head(p)][:, None]) for p in range(2)], 1).astype(f)
    c["kdecay"] = np.exp((P - 1 - n)[:, None] * lg[None, :]).astype(f)
    c["sdecay"] = np.concatenate([np.exp(P * lg[head(p)])[:, None] for p in range(2)]
                                 + [np.exp(lg[head(p)])[:, None] for p in range(2)], 1).astype(f)
    pick = np.zeros((NS, NS, P), f)
    for b in range(NS):
        pick[b, b] = 1
    c["pick"] = pick.reshape(NS, NS * P)
    expand = np.zeros((NH, 16, P), f)
    for h in range(NH):
        expand[h, h // 2, (h % 2) * 64:(h % 2) * 64 + 64] = 1
    c["expand"] = expand.reshape(NH, 16 * P)
    return c


CONSTS = {k: v.shape for k, v in shape_constants().items()}


class Build:

    def __init__(self, nc, ctx, ins, outs, stop):
        self.nc, self.ctx, self.stop = nc, ctx, stop
        self.i, self.o = ins, outs
        self.top = (nc.sbuf_base + 63) // 64 * 64
        self.end = nc.sbuf_top
        self.names = 0
        self.stage_sems = []
        self.psum = ctx.enter_context(nc.psum_tensor("psum", [P, 8, 512], F32))
        self.ident = self.take("ident_sb", [P, P])
        self.upto = self.take("upto_sb", [P, P])
        self.ones = self.take("ones_sb", [P, P])
        self.gains = self.take("gains_sb", [P, 5, KT])
        self.eps = self.take("eps_sb", [P, 1])
        self.x = None
        self.wf = self.take("w_loaded_sb", [P, 2, KT, P])
        self.wh = self.take("w_high_sb", [P, 2, KT, P], F32R)
        self.wl = self.take("w_low_sb", [P, 2, KT, P], F32R)
        self.hh = self.take("act_high_sb", [P, KT, TOK], F32R)
        self.hl = self.take("act_low_sb", [P, KT, TOK], F32R)
        self.s_w_loaded = [self.sem("w_loaded_even"), self.sem("w_loaded_odd")]
        self.s_w_high = self.sem("w_high")
        self.s_w_low = self.sem("w_low")
        self.s_tile = self.sem("tile_summed")
        self.s_tile_free = self.sem("tile_free")
        self.s_held = {e.engine: self.sem(f"held_{n}") for n, e in
                       (("sync", nc.sync), ("act", nc.scalar), ("pool", nc.gpsimd))}
        self.stage_sems = []
        self.unit = 0
        self.stored = 0

    def sem(self, name):
        self.names += 1
        sem = self.nc.alloc_semaphore(name=f"{name}_{self.names}")
        self.stage_sems.append(sem)
        return sem

    def recycle(self):
        self.nc.clear_and_free_semaphores(self.stage_sems)
        self.stage_sems = []
        self.nc.all_engine_barrier()

    def hold(self, eng):
        eng.sem_inc(self.s_held[eng.engine], 1)

    def tally(self, name):
        return Tally(self.sem(name))

    def take(self, name, shape, dt=F32):
        n = 4
        for s in shape[1:]:
            n *= s
        self.names += 1
        t = self.nc.alloc_sbuf_tensor_at(f"{name}_{self.names}", shape, dt, offset=self.top)
        self.top += (n + 31) // 32 * 32
        assert self.top <= self.end, (name, self.top, self.end)
        return t

    def bank(self, n, rows=P, cols=512):
        return self.psum[0:rows, n, 0:cols]


    def load_weights(self, sp, u, par, src, width=P, held=False):
        sp.wait_ge(self.s_w_low, u + 1)
        if held:
            self.hold(sp)
        sp.dma_start(self.wf[:, par, :, 0:width], src).then_inc(self.s_w_loaded[par], 16)

    def split_high(self, act, u, par, width=P):
        act.wait_ge(self.s_w_loaded[par], u * 8 + (16 - 8 * par))
        act.wait_ge(self.s_tile, u * 3 + 3)
        self.nc.scalar.copy(self.wh[:, par, :, 0:width], self.wf[:, par, :, 0:width]).then_inc(self.s_w_high, 1)

    def split_low(self, pool, u, par, width=P):
        pool.wait_ge(self.s_w_high, u + 1)
        pool.wait_ge(self.s_tile, u * 3 + 3)
        self.nc.gpsimd.tensor_tensor(self.wl[:, par, :, 0:width], self.wf[:, par, :, 0:width],
                                     self.wh[:, par, :, 0:width].bitcast(F32), ALU.subtract).then_inc(self.s_w_low, 1)

    def multiply(self, pe, u, par, high, low, width=P, last_k=None):
        nc = self.nc
        pe.wait_ge(self.s_w_high, u + 1)
        pe.wait_ge(self.s_w_low, u + 3)
        for t in range(NT):
            out = self.psum[0:width, 3 * par + t, 0:TT]
            pe.wait_ge(self.s_tile_free, u * 3 + t + 1)
            n = 0
            cols = slice(t * TT, (t + 1) * TT)
            for k in range(KT):
                if k == KT - 1 and t == 0 and last_k is not None:
                    last_k()
                for w, a in ((self.wh, high), (self.wh, low), (self.wl, high)):
                    ins = nc.tensor.matmul(out, w[:, par, k, 0:width], a[:, k, cols],
                                           start=n == 0, stop=n == 3 * KT - 1)
                    n += 1
            ins.then_inc(self.s_tile, 1)

    def await_tile(self, eng, u, t):
        eng.wait_ge(self.s_tile, u * 3 + t + 7)

    def tile(self, par, t, rows=P):
        return self.psum[0:rows, 3 * par + t, 0:TT]


def tcols(t):
    return slice(t * TT, (t + 1) * TT)


def load_inputs(B):
    nc = B.nc
    mark = B.top
    B.x_base = B.top
    B.x = B.take("x_sb", [P, KT, TOK])
    x_end = B.top
    nat = B.take("x_rows_sb", [P, NBLK, D_MODEL])
    nats = B.take("x_sample_rows_sb", [NS, D_MODEL])
    s_const, s_rows = B.sem("const_loaded"), B.sem("rows_loaded")
    s_turned, s_kept = B.sem("block_turned"), B.sem("block_kept")
    s_set = B.sem("constants_set")
    with nc.Block() as block:
        @block.sync
        def _(sp):
            sp.dma_start(nat[:], B.i["x_prompt"].rearrange("o (n p) d -> p (o n) d", p=P)).then_inc(s_rows, 16)
            sp.dma_start(nats[:], B.i["x_sample"].rearrange("b o d -> (b o) d")).then_inc(s_rows, 16)
            sp.dma_start(B.ident[:], B.i["ident"]).then_inc(s_const, 16)
            sp.dma_start(B.upto[:], B.i["upto"]).then_inc(s_const, 16)
            with nc.allow_non_contiguous_dma("norm gains, once"):
                for n, g in enumerate((B.i["norm_mix"][0], B.i["norm_mlp"][0], B.i["norm_mix"][1],
                                       B.i["norm_mlp"][1], B.i["norm_final"])):
                    sp.dma_start(B.gains[:, n, :], g.rearrange("(k p) -> p k", p=P)).then_inc(s_const, 16)
            sp.wait_ge(s_const, 7 * 16)

        @block.gpsimd
        def _(pool):
            nc.gpsimd.memset(B.ones[:], 1.0).then_inc(s_set, 1)
            nc.gpsimd.memset(B.eps[:], EPS).then_inc(s_set, 1)

        @block.tensor
        def _(pe):
            pe.sem_inc(B.s_w_low, 2)
            pe.sem_inc(B.s_tile, 6)
            pe.sem_inc(B.s_tile_free, 6)
            pe.wait_ge(s_const, 7 * 16)
            pe.wait_ge(s_rows, 32)
            for n in range(2 * (NBLK + 1)):
                blk, half = n // 2, n % 2
                if n >= 4:
                    pe.wait_ge(s_kept, n - 3)
                rows = P if blk < NBLK else NS
                src = nat[:, blk, :] if blk < NBLK else nats[:]
                for j in range(4):
                    k = 4 * half + j
                    ins = nc.tensor.transpose(B.psum[:, n % 4, j * P:j * P + rows], src[:, k * P:(k + 1) * P],
                                              B.ident[0:rows, 0:rows])
                ins.then_inc(s_turned, 1)

        @block.vector
        def _(dve):
            for n in range(2 * (NBLK + 1)):
                blk, half = n // 2, n % 2
                rows = P if blk < NBLK else NS
                dve.wait_ge(s_turned, n + 1)
                nc.vector.tensor_copy(
                    B.x[:, 4 * half:4 * half + 4, blk * P:blk * P + rows],
                    B.psum[:, n % 4, :].rearrange("p (j c) -> p j c", j=4)[:, :, 0:rows]).then_inc(s_kept, 1)
    B.top = x_end
    return mark


def normalize(B, gain, final=False, keep=None):
    nc = B.nc
    mark = B.top
    sq = B.take("square_sb", [P, 2, TOK])
    acc = B.take("square_sum_sb", [P, TOK])
    rstd = B.take("rstd_sb", [P, TOK])
    tmp = B.take("normed_sb", [P, 2, TOK])
    s_sq, s_acc, s_sum, s_rstd = B.sem("squared"), B.sem("square_added"), B.sem("square_summed"), B.sem("rstd")
    s_tmp, s_high, s_low = B.sem("normed"), B.sem("normed_high"), B.sem("normed_low")
    s_keep = B.sem("x_kept")
    with nc.Block() as block:
        @block.sync
        def _(sp):
            if keep is not None:
                sp.dma_start(keep, B.x[:]).then_inc(s_keep, 16)
                sp.wait_ge(s_keep, 16)

        @block.scalar
        def _(act):
            for k in range(KT):
                if k >= 2:
                    act.wait_ge(s_acc, k - 1)
                nc.scalar.activation(sq[:, k % 2, :], B.x[:, k, :], ACT.Square).then_inc(s_sq, 1)
            for t in range(NT):
                act.wait_ge(s_sum, t + 1)
                nc.scalar.activation(rstd[:, tcols(t)], B.psum[:, t, 0:TT], ACT.Ln, bias=B.eps[:, 0:1],
                                     scale=1.0 / D_MODEL).then_inc(s_rstd, 1)
            act.wait_ge(s_rstd, NT)
            nc.scalar.activation(rstd[:], rstd[:], ACT.Exp, scale=-0.5).then_inc(s_rstd, 1)
            if not final:
                for k in range(KT):
                    act.wait_ge(s_tmp, k + 1)
                    nc.scalar.copy(B.hh[:, k, :], tmp[:, k % 2, :]).then_inc(s_high, 1)

        @block.tensor
        def _(pe):
            pe.wait_ge(s_acc, KT)
            for t in range(NT):
                nc.tensor.matmul(B.psum[:, t, 0:TT], B.ones[:], acc[:, tcols(t)], start=True, stop=True).then_inc(s_sum, 1)

        @block.vector
        def _(dve):
            for k in range(KT):
                dve.wait_ge(s_sq, k + 1)
                if k == 0:
                    nc.vector.tensor_copy(acc[:], sq[:, 0, :]).then_inc(s_acc, 1)
                else:
                    dve.wait_ge(s_acc, k)
                    nc.vector.tensor_tensor(acc[:], acc[:], sq[:, k % 2, :], ALU.add).then_inc(s_acc, 1)
            dve.wait_ge(s_rstd, NT + 1)
            for k in range(KT):
                if k >= 2 and not final:
                    dve.wait_ge(s_low, k - 1)
                out = B.x[:, k, :] if final else tmp[:, k % 2, :]
                nc.vector.scalar_tensor_tensor(out=out, in0=B.x[:, k, :], scalar=B.gains[:, gain, k:k + 1],
                                               in1=rstd[:], op0=ALU.mult, op1=ALU.mult).then_inc(s_tmp, 1)

        @block.gpsimd
        def _(pool):
            if not final:
                for k in range(KT):
                    pool.wait_ge(s_high, k + 1)
                    nc.gpsimd.tensor_tensor(B.hl[:, k, :], tmp[:, k % 2, :], B.hh[:, k, :].bitcast(F32),
                                            ALU.subtract).then_inc(s_low, 1)
    B.top = mark


def mlp(B, layer):
    nc = B.nc
    mark = B.top
    uh = B.take("hidden_high_sb", [P, KT, TOK], F32R)
    ul = B.take("hidden_low_sb", [P, KT, TOK], F32R)
    relu = B.take("relu_sb", [P, 2, TT])
    sq = B.take("relu_square_sb", [P, 2, TT])
    GROUPS = 4
    U0 = B.unit
    w_up = B.i["w_up"][layer].rearrange("(k p) (c m) -> c p k m", p=P, m=P)
    w_down = B.i["w_down"][layer].rearrange("(g k p) (c m) -> g c p k m", k=KT, p=P, m=P)
    s_relu, s_square, s_high, s_low, s_added = (B.sem("relu"), B.sem("squared"), B.sem("hidden_high"),
                                                B.sem("hidden_low"), B.sem("down_added"))

    def up_unit(g, j, e):
        return g * 16 + j * 2 + (U0 + e)

    with nc.Block() as block:
        @block.sync
        def _(sp):
            with sp.Fori(0, GROUPS) as g:
                with sp.Fori(0, 4) as j:
                    for e in range(2):
                        B.load_weights(sp, up_unit(g, j, e), (U0 + e) % 2,
                                       w_up[bass.ds(g * 8 + j * 2 + e, 1)].rearrange("o p k m -> p (o k) m"))
                wd = w_down[bass.ds(g, 1)].rearrange("o c p k m -> (o c) p k m")
                with sp.Fori(0, 4) as j:
                    for e in range(2):
                        B.load_weights(sp, up_unit(g, j, 8 + e), (U0 + e) % 2,
                                       wd[bass.ds(j * 2 + e, 1)].rearrange("o p k m -> p (o k) m"))

        @block.gpsimd
        def _(pool):
            with pool.Fori(0, GROUPS * 8) as j:
                for e in range(2):
                    B.split_low(pool, j * 2 + (U0 + e), (U0 + e) % 2)

        @block.tensor
        def _(pe):
            with pe.Fori(0, GROUPS) as g:
                with pe.Fori(0, 4) as j:
                    for e in range(2):
                        B.multiply(pe, up_unit(g, j, e), (U0 + e) % 2, B.hh, B.hl)
                pe.wait_ge(s_low, g * 24 + 21)
                for e in range(2):
                    B.multiply(pe, up_unit(g, 0, 8 + e), (U0 + e) % 2, uh, ul,
                               last_k=(lambda: pe.wait_ge(s_low, g * 24 + 24)) if e == 0 else None)
                with pe.Fori(1, 4) as j:
                    for e in range(2):
                        B.multiply(pe, up_unit(g, j, 8 + e), (U0 + e) % 2, uh, ul)

        @block.scalar
        def _(act):
            def high(u, e):
                B.split_high(act, u, (U0 + e) % 2)

            with act.Fori(0, GROUPS) as g:
                high(up_unit(g, 0, 0), 0)
                with act.Fori(0, 4) as j:
                    for e in range(2):
                        high(up_unit(g, j, e + 1), e + 1)
                        for t in range(NT):
                            n = g * 24 + j * 6 + (3 * e + t)
                            s = (3 * e + t) % 2
                            act.wait_ge(s_relu, n + 1)
                            nc.scalar.activation(sq[:, s, :], relu[:, s, :], ACT.Square).then_inc(s_square, 1)
                            act.wait_ge(s_square, n + 1)
                            nc.scalar.copy(uh[:, bass.ds(j * 2 + e, 1), tcols(t)].rearrange("p o c -> p (o c)"),
                                           sq[:, s, :]).then_inc(s_high, 1)
                with act.Fori(0, 3) as j:
                    for e in range(2):
                        high(up_unit(g, j, 9 + e), e + 1)
                high(up_unit(g, 3, 9), 1)

        @block.vector
        def _(dve):
            with dve.Fori(0, GROUPS) as g:
                with dve.Fori(0, 4) as j:
                    for e in range(2):
                        for t in range(NT):
                            n = g * 24 + j * 6 + (3 * e + t)
                            s = (3 * e + t) % 2
                            B.await_tile(dve, up_unit(g, j, e), t)
                            nc.vector.tensor_scalar(relu[:, s, :], B.tile((U0 + e) % 2, t), 0.0, None,
                                                    ALU.max).then_inc(s_relu, 1)
                            dve.wait_ge(s_high, n + 1)
                            nc.vector.tensor_tensor(
                                ul[:, bass.ds(j * 2 + e, 1), tcols(t)].rearrange("p o c -> p (o c)"), sq[:, s, :],
                                uh[:, bass.ds(j * 2 + e, 1), tcols(t)].rearrange("p o c -> p (o c)").bitcast(F32),
                                ALU.subtract).then_inc(s_low, 1)
                            dve.wait_ge(s_low, n + 1)
                            dve.sem_inc(B.s_tile_free, 1)
                with dve.Fori(0, 4) as j:
                    for e in range(2):
                        for t in range(NT):
                            B.await_tile(dve, up_unit(g, j, 8 + e), t)
                            xs = B.x[:, bass.ds(j * 2 + e, 1), tcols(t)].rearrange("p o c -> p (o c)")
                            nc.vector.tensor_tensor(xs, xs, B.tile((U0 + e) % 2, t), ALU.add).then_inc(B.s_tile_free, 1)
    B.unit += GROUPS * 16
    B.top = mark


def write_outputs(B):
    nc = B.nc
    rows_sb = B.take("y_rows_sb", [P, 2, D_MODEL])
    s_turned, s_kept, s_out = (B.sem("row_block_turned"), B.sem("row_block_kept"),
                               [B.sem("y_stored_even"), B.sem("y_stored_odd")])
    with nc.Block() as block:
        @block.tensor
        def _(pe):
            for n in range(2 * (NBLK + 1)):
                blk, half = n // 2, n % 2
                rows = P if blk < NBLK else NS
                if n >= 4:
                    pe.wait_ge(s_kept, n - 3)
                for j in range(4):
                    ins = nc.tensor.transpose(B.psum[0:rows, n % 4, j * P:(j + 1) * P],
                                              B.x[:, 4 * half + j, blk * P:blk * P + rows], B.ident[:])
                ins.then_inc(s_turned, 1)

        @block.vector
        def _(dve):
            for n in range(2 * (NBLK + 1)):
                blk, half = n // 2, n % 2
                rows = P if blk < NBLK else NS
                dve.wait_ge(s_turned, n + 1)
                if blk >= 2:
                    dve.wait_ge(s_out[blk % 2], 16 * (blk // 2))
                nc.vector.tensor_copy(rows_sb[0:rows, blk % 2, half * 512:half * 512 + 512],
                                      B.psum[0:rows, n % 4, :]).then_inc(s_kept, 1)

        @block.sync
        def _(sp):
            for blk in range(NBLK + 1):
                sp.wait_ge(s_kept, 2 * blk + 2)
                if blk < NBLK:
                    sp.dma_start(B.o["y_prompt"][0, blk * P:(blk + 1) * P, :], rows_sb[:, blk % 2, :]).then_inc(s_out[blk % 2], 16)
                else:
                    sp.dma_start(B.o["y_sample"].rearrange("b o d -> (b o) d"), rows_sb[0:NS, blk % 2, :]).then_inc(s_out[blk % 2], 16)
            sp.wait_ge(s_out[0], 16 * 5)
            sp.wait_ge(s_out[1], 16 * 4)



LATE = NBLK - 3


def score_offset(i):
    return sum((j + 1) * P for j in range(2, i))


SCORE_COLS = score_offset(NBLK)
KEYS_S = PAGES * P + 1


def indexer(B):
    nc = B.nc
    B.retention_base = B.top
    B.scores_s = B.take("sample_scores_sb", [NS, KEYS_S + 7])
    B.pages = B.take("page_table_sb", [1, NS * PAGES], I32)
    B.qkv_s = B.take("sample_qkv_rows_sb", [NS, 3, 512])
    B.bias_s = B.take("sample_bias_sb", [P, 2, HA])
    B.even_top = B.top
    B.future = B.take("future_sb", [P, P])
    B.scores = B.take("scores_sb", [P, SCORE_COLS])
    mark = B.top
    iq = B.take("index_q_sb", [P, 4, TOK])
    ikw = B.take("index_k_w_sb", [P, TOK])
    ik2 = B.take("index_k_again_sb", [P, TOK])
    ikn = B.take("index_k_rows_sb", [P, NBLK + 1, DH + HIDX])
    iwn = B.take("index_w_rows_sb", [P, NBLK, HIDX])
    relu = B.take("relu_scores_sb", [P, 2, 1024])
    iqs = B.take("sample_index_q_sb", [DH, NS, HIDX])
    iws = B.take("sample_index_w_sb", [HIDX, NS, NS])
    pk = B.take("index_pages_sb", [P, NS * PAGES, DH])
    ikt = B.take("index_pages_turned_sb", [DH, 2, KEYS_S + 7])
    rs = B.take("sample_relu_sb", [HIDX, 2, KEYS_S + 7])
    U0 = B.unit
    w_in = B.i["w_in_even"][0].rearrange("(k p) n -> p k n", p=P)
    WSCALE = HIDX ** -0.5 * DH ** -0.5
    N = (NBLK - 2) * HIDX
    s_table, s_page, s_out = B.sem("page_table_loaded"), B.sem("index_page_loaded"), B.sem("index_k_stored")
    s_turned, s_rows, s_w = B.sem("index_k_turned"), B.sem("index_k_rows"), B.sem("index_w_scaled")
    s_dot, s_relu, s_add = B.sem("index_products"), B.sem("index_relu"), B.sem("index_added")
    s_fut = B.sem("future_loaded")
    s_small = B.tally("sample_index_ready")
    s_pt, s_pc, s_sdot, s_srelu, s_sacc, s_fin = (B.sem("pages_turned"), B.sem("pages_copied"), B.sem("sample_products"),
                                                  B.sem("sample_relu"), B.sem("sample_weighted"), B.sem("sample_scores"))
    TILES_DONE = 6 + 3 * (U0 + 5)
    with nc.Block() as block:
        @block.sync
        def _(sp):
            for e in range(5):
                c0, w = (COL_IQ + e * P, P) if e < 4 else (COL_IK, DH + HIDX)
                B.load_weights(sp, U0 + e, (U0 + e) % 2, w_in[:, :, c0:c0 + w], w)
            sp.dma_start(B.future[:], B.i["future"]).then_inc(s_fut, 16)
            sp.dma_start(B.pages[:], B.i["page_table"].rearrange("(o b) n -> o (b n)", o=1)).then_inc(s_table, 16)
            sp.wait_ge(s_table, 16)
            with sp.Fori(0, NS * PAGES) as n:
                page = sp.value_load(B.pages[0:1, bass.ds(n, 1)], min_val=0, max_val=NPOOL - 1)
                sp.dma_start(pk[:, bass.ds(n, 1), :],
                             B.i["cache_idx_k"][0][bass.ds(page, 1)].rearrange("o p d -> p o d")).then_inc(s_page, 16)
            sp.wait_ge(s_rows, 3)
            sp.dma_start(B.o["idx_k_prompt"][0, 0].rearrange("(n p) d -> p n d", p=P), ikn[:, 0:NBLK, 0:DH]).then_inc(s_out, 16)
            sp.dma_start(B.o["idx_k_sample"][0].rearrange("b o d -> (b o) d"), ikn[0:NS, NBLK, 0:DH]).then_inc(s_out, 16)
            sp.wait_ge(s_out, 32)

        @block.gpsimd
        def _(pool):
            nc.gpsimd.memset(iws[:], 0.0).then_inc(s_w, 1)
            for e in range(5):
                B.split_low(pool, U0 + e, (U0 + e) % 2, P if e < 4 else DH + HIDX)

        @block.tensor
        def _(pe):
            for e in range(5):
                B.multiply(pe, U0 + e, (U0 + e) % 2, B.hh, B.hl, P if e < 4 else DH + HIDX)
            pe.wait_ge(B.s_tile_free, TILES_DONE)
            for n in range(NBLK + 1):
                w = P if n < NBLK else NS
                ins = nc.tensor.transpose(B.psum[0:w, n // 4, (n % 4) * P:(n % 4) * P + DH + HIDX],
                                          ikw[0:DH + HIDX, n * P:n * P + w], B.ident[0:DH + HIDX, 0:DH + HIDX])
                if n % 4 == 3 or n == NBLK:
                    ins.then_inc(s_turned, 1)
            pe.wait_ge(s_rows, 3)
            n = 0
            for i in range(2, NBLK):
                L = (i + 1) * P
                for h in range(HIDX):
                    if n >= 3:
                        pe.wait_ge(s_relu, n - 2)
                    r = slice(64 * (h % 2), 64 * (h % 2) + 64)
                    keys = ikw if h % 2 == 0 else ik2
                    for c in range(0, L, 512):
                        w = min(512, L - c)
                        ins = nc.tensor.matmul(B.psum[:, 2 * (n % 3) + c // 512, 0:w], iq[r, h // 2, i * P:(i + 1) * P],
                                               keys[r, c:c + w], start=True, stop=True)
                    ins.then_inc(s_dot, 1)
                    n += 1
            pe.wait_ge(s_relu, N)
            pe.wait_ge(s_small.sem, 4)
            pe.wait_ge(s_page, 16 * NS * PAGES)

            def turn_pages(b):
                if b >= 1:
                    pe.wait_ge(s_pc, 2 * b)
                for j in range(PAGES):
                    ins = nc.tensor.transpose(B.psum[0:DH, 6 + j // 4, (j % 4) * P:(j % 4 + 1) * P],
                                              pk[:, b * PAGES + j, :], B.ident[:])
                ins.then_inc(s_pt, 1)

            turn_pages(0)
            for b in range(NS):
                if b + 1 < NS:
                    turn_pages(b + 1)
                pe.wait_ge(s_pc, 2 * b + 2)
                if b >= 1:
                    pe.wait_ge(s_srelu, 2 * b)
                for bank, c, w in ((0, 0, 512), (1, 512, 512), (2, 1024, 1)):
                    ins = nc.tensor.matmul(B.psum[0:HIDX, bank, 0:w], iqs[:, b, :], ikt[:, b % 2, c:c + w],
                                           start=True, stop=True)
                ins.then_inc(s_sdot, 1)
                pe.wait_ge(s_srelu, 2 * b + 2)
                for bank, c, w in ((3, 0, 512), (4, 512, 512), (5, 1024, 1)):
                    ins = nc.tensor.matmul(B.psum[0:NS, bank, 0:w], iws[:, b, :], rs[:, b % 2, c:c + w],
                                           start=b == 0, stop=b == NS - 1)
                ins.then_inc(s_sacc, 1)

        @block.scalar
        def _(act):
            for e in range(5):
                B.split_high(act, U0 + e, (U0 + e) % 2, P if e < 4 else DH + HIDX)
                if e >= 1:
                    for t in range(NT):
                        B.await_tile(act, U0 + e - 1, t)
                        nc.scalar.copy(iq[:, e - 1, tcols(t)], B.tile((U0 + e - 1) % 2, t)).then_inc(B.s_tile_free, 1)
            for t in range(NT):
                B.await_tile(act, U0 + 4, t)
                nc.scalar.copy(ikw[0:DH + HIDX, tcols(t)], B.tile((U0 + 4) % 2, t, DH + HIDX)).then_inc(s_small.sem, 1)
                nc.scalar.copy(ik2[64:128, tcols(t)], B.tile((U0 + 4) % 2, t, DH)).then_inc(B.s_tile_free, 1)
            act.wait_ge(s_small.sem, 3)
            act.wait_ge(B.s_tile_free, TILES_DONE)
            s_small.count = 3
            for par in range(2):
                nc.scalar.copy(iqs[:].rearrange("p b (c two) -> p two c b", two=2)[:, par],
                               iq[64 * par:64 * par + 64, :, SEQ:TOK]).then_inc(s_w, 1)
            act.wait_ge(s_w, 3)
            nc.scalar.mul(iws[:].rearrange("h a b -> h (a b)")[:, 0:NS * NS:NS + 1], ikw[64:64 + HIDX, SEQ:TOK],
                          WSCALE).then_inc(s_small.sem, 1)
            n = 0
            for i in range(2, NBLK):
                L = (i + 1) * P
                for h in range(HIDX):
                    act.wait_ge(s_dot, n + 1)
                    if n >= 2:
                        act.wait_ge(s_add, n - 1)
                    nc.scalar.activation(relu[:, n % 2, 0:L],
                                         B.psum[:, 2 * (n % 3):2 * (n % 3) + 2, :].rearrange("p b c -> p (b c)")[:, 0:L],
                                         ACT.Relu).then_inc(s_relu, 1)
                    n += 1
            for b in range(NS):
                act.wait_ge(s_sdot, b + 1)
                if b >= 2:
                    act.wait_ge(s_sacc, b - 1)
                nc.scalar.activation(rs[:, b % 2, 0:1024], B.psum[0:HIDX, 0:2, :].rearrange("p b c -> p (b c)"),
                                     ACT.Relu).then_inc(s_srelu, 1)
                nc.scalar.activation(rs[:, b % 2, 1024:1025], B.psum[0:HIDX, 2, 0:1], ACT.Relu).then_inc(s_srelu, 1)

        @block.vector
        def _(dve):
            for n in range(3):
                dve.wait_ge(s_turned, n + 1)
                if n < 2:
                    nc.vector.tensor_copy(ikn[:, 4 * n:4 * n + 4, :],
                                          B.psum[:, n, :].rearrange("p (j c) -> p j c", j=4)[:, :, 0:DH + HIDX]).then_inc(s_rows, 1)
                else:
                    nc.vector.tensor_copy(ikn[0:NS, NBLK, :], B.psum[0:NS, 2, 0:DH + HIDX]).then_inc(s_rows, 1)
            dve.wait_ge(s_rows, 2)
            s_iw = B.sem("index_w_rows")
            nc.vector.tensor_scalar(iwn[:], ikn[:, 0:NBLK, DH:DH + HIDX], WSCALE, None, ALU.mult).then_inc(s_iw, 1)
            dve.wait_ge(s_iw, 1)
            dve.wait_ge(s_fut, 16)
            n = 0
            s_diag = B.sem("diagonal_masked")
            for i in range(2, NBLK):
                L = (i + 1) * P
                S = B.scores[:, score_offset(i):score_offset(i) + L]
                for h in range(HIDX):
                    dve.wait_ge(s_relu, n + 1)
                    w = iwn[:, i, h:h + 1]
                    if h == 0:
                        nc.vector.tensor_scalar(S, relu[:, n % 2, 0:L], w, None, ALU.mult).then_inc(s_add, 1)
                    else:
                        dve.wait_ge(s_add, n)
                        nc.vector.scalar_tensor_tensor(out=S, in0=relu[:, n % 2, 0:L], scalar=w, in1=S,
                                                       op0=ALU.mult, op1=ALU.add).then_inc(s_add, 1)
                    n += 1
                dve.wait_ge(s_add, n)
                D = S[:, i * P:L]
                nc.vector.scalar_tensor_tensor(out=D, in0=B.future[:], scalar=-BIG, in1=D,
                                               op0=ALU.mult, op1=ALU.add).then_inc(s_diag, 1)
            for b in range(NS):
                dve.wait_ge(s_pt, b + 1)
                if b >= 2:
                    dve.wait_ge(s_sdot, b - 1)
                nc.vector.tensor_copy(ikt[:, b % 2, 0:1024],
                                      B.psum[0:DH, 6:8, :].rearrange("p b c -> p (b c)")).then_inc(s_pc, 1)
                nc.vector.tensor_copy(ikt[:, b % 2, 1024:1025], ikw[0:DH, SEQ + b:SEQ + b + 1]).then_inc(s_pc, 1)
            dve.wait_ge(s_sacc, NS)
            nc.vector.tensor_copy(B.scores_s[:, 0:1024], B.psum[0:NS, 3:5, :].rearrange("p b c -> p (b c)")).then_inc(s_fin, 1)
            nc.vector.tensor_copy(B.scores_s[:, 1024:1025], B.psum[0:NS, 5, 0:1]).then_inc(s_fin, 1)
    B.unit += 5
    B.top = mark


def project_and_choose(B):
    nc = B.nc
    B.qkv = B.take("qkv_sb", [P, 12, TOK])
    mark = B.top
    stage = B.take("stage_sb", [P, 2, TOK])
    left = B.take("scores_left_sb", [P, 2, KEYS_S + 7])
    best = B.take("best_sb", [P, 2, 8])
    U0 = B.unit
    par = lambda e: (U0 + e) % 2
    B.r_scratch = nc.dram_tensor("retention_scratch", (12, P, TOK), F32, kind="Internal").ap()
    w_in = B.i["w_in_even"][0].rearrange("(k p) n -> p k n", p=P)
    w_qkv = w_in[:, :, 0:12 * P].rearrange("p k (c m) -> c p k m", m=P)
    w_r = w_in[:, :, COL_R:COL_R + 12 * P].rearrange("p k (c m) -> c p k m", m=P)
    s_stage, s_spill = B.sem("unit_staged"), [B.sem("unit_spilled_even"), B.sem("unit_spilled_odd")]
    s_step = [B.tally("choosing_step_a"), B.tally("choosing_step_b")]
    s_round = B.sem("choosing_round")
    with nc.Block() as block:
        @block.sync
        def _(sp):
            for base, src in ((0, w_qkv), (12, w_r)):
                with sp.Fori(0, 6) as j:
                    for e in range(2):
                        B.load_weights(sp, j * 2 + (U0 + base + e), par(e),
                                       src[bass.ds(j * 2 + e, 1)].rearrange("o p k m -> p (o k) m"))

        @block.gpsimd
        def _(pool):
            with pool.Fori(0, 12) as j:
                for e in range(2):
                    B.split_low(pool, j * 2 + (U0 + e), par(e))

        @block.tensor
        def _(pe):
            with pe.Fori(0, 12) as j:
                for e in range(2):
                    B.multiply(pe, j * 2 + (U0 + e), par(e), B.hh, B.hl)

        @block.scalar
        def _(act):
            B.split_high(act, U0, par(0))
            with act.Fori(0, 6) as j:
                for e in range(2):
                    B.split_high(act, j * 2 + (U0 + e + 1), par(e + 1))
                    for t in range(NT):
                        B.await_tile(act, j * 2 + (U0 + e), t)
                        nc.scalar.copy(B.qkv[:, bass.ds(j * 2 + e, 1), tcols(t)].rearrange("p o c -> p (o c)"),
                                       B.tile(par(e), t)).then_inc(B.s_tile_free, 1)

            def spill(j, last=False):
                for e in range(2):
                    u = j * 2 + (U0 + 12 + e)
                    if not (last and e == 1):
                        B.split_high(act, u + 1, par(e + 1))
                    act.wait_ge(s_spill[e], j * 16 + 16)
                    for t in range(NT):
                        B.await_tile(act, u, t)
                        nc.scalar.copy(stage[:, e, tcols(t)], B.tile(par(e), t)).then_inc(B.s_tile_free, 1)
                    act.wait_ge(B.s_tile_free, u * 3 + 9)
                    act.dma_start(B.r_scratch[bass.ds(j * 2 + e, 1)].rearrange("o p c -> p (o c)"),
                                  stage[:, e, :]).then_inc(s_spill[e], 16)

            for e in range(2):
                act.sem_inc(s_spill[e], 16)
            with act.Fori(0, 5) as j:
                spill(j)
            spill(5, last=True)
            for e in range(2):
                act.wait_ge(s_spill[e], 16 * 7)

        @block.vector
        def _(dve):
            def choose(*chains):
                def each(step):
                    for c, (S, rows, L) in enumerate(chains):
                        step(s_step[c], S, left[0:rows, c, 0:L], best[0:rows, c, :])

                def largest(source):
                    def step(tally, S, W, m8):
                        if tally.count:
                            dve.wait_ge(tally.sem, tally.value())
                        if source is None:
                            dve.sem_inc(s_round, 1)
                        tally.up(nc.vector.max(m8, W if source is None else S))
                    return step

                def take(tally, S, W, m8):
                    dve.wait_ge(tally.sem, tally.value())
                    dve.sem_inc(s_round, 1)
                    tally.up(nc.vector.match_replace(W, m8, W, TAKEN))

                def take_first(tally, S, W, m8):
                    dve.wait_ge(tally.sem, tally.value())
                    tally.up(nc.vector.match_replace(W, m8, S, TAKEN))

                def mark(tally, S, W, m8):
                    dve.wait_ge(tally.sem, tally.value())
                    tally.up(nc.vector.scalar_tensor_tensor(out=S, in0=W, scalar=1.0, in1=S, op0=ALU.mult, op1=ALU.is_equal))

                each(largest("scores"))
                each(take_first)
                with counted(dve, TOPK // 8 - 1, *((t, 2) for t in s_step)):
                    each(largest(None))
                    each(take)
                each(mark)

            block_scores = lambda i: (B.scores[:, score_offset(i):score_offset(i) + (i + 1) * P], P, (i + 1) * P)
            choose((B.scores_s[:, 0:KEYS_S], NS, KEYS_S), block_scores(LATE - 1))
            choose(block_scores(2), block_scores(3))
    B.unit += 24
    B.top = mark


def keys_and_values(B):
    nc = B.nc
    B.vn = B.take("v_rows_sb", [P, NBLK, 512])
    B.bias = B.take("bias_sb", [P, HA, 2 * P])
    mark = B.top
    kn = B.take("k_rows_sb", [P, 2, 512])
    buckets = B.take("buckets_sb", [NB, 384 + P + NS])
    rel = B.take("rel_bias_sb", [NB, HA])
    line = B.take("bias_line_sb", [HA, 384])
    b_scratch = nc.dram_tensor("bias_scratch", (HA, 384), F32, kind="Internal").ap()
    b_rows = nc.dram_tensor("bias_rows_scratch", (P, HA, 384), F32, kind="Internal").ap()
    s_in, s_bias, s_biasc = B.sem("bias_loaded"), B.sem("bias_products"), B.sem("bias_copied")
    s_line, s_biast = B.sem("bias_line_stored"), B.sem("bias_tiles_loaded")
    s_turned, s_kept = B.sem("rows_turned"), B.sem("rows_kept")
    s_k, s_v = [B.sem("k_stored_even"), B.sem("k_stored_odd")], B.sem("v_stored")
    steps = [(0, NBLK)] + [(1, b) for b in range(NBLK + 1)] + [(2, b) for b in range(NBLK + 1)]
    with nc.Block() as block:
        @block.sync
        def _(sp):
            sp.dma_start(buckets[:], B.i["buckets"]).then_inc(s_in, 16)
            sp.dma_start(rel[:], B.i["rel_bias"]).then_inc(s_in, 16)
            sp.wait_ge(s_biasc, 1)
            sp.dma_start(b_scratch, line[:]).then_inc(s_line, 16)
            sp.wait_ge(s_line, 16)
            sp.dma_start(b_rows, bass.AP(tensor=b_scratch.tensor, offset=0,
                                         ap=[[0, P], [384, HA], [1, 384]])).then_inc(s_line, 16)
            sp.wait_ge(s_line, 32)
            sp.dma_start(B.bias[:], bass.AP(tensor=b_rows.tensor, offset=P - 1,
                                            ap=[[HA * 384 - 1, P], [384, HA], [1, 2 * P]])).then_inc(s_biast, 16)
            for n, (part, b) in enumerate(steps):
                if part == 1 and b < NBLK:
                    sp.wait_ge(s_kept, n + 1)
                    sp.dma_start(B.o["k_prompt"][0, 0, b * P:(b + 1) * P].rearrange("p h d -> p (h d)"),
                                 kn[:, b % 2, :]).then_inc(s_k[b % 2], 16)
            sp.wait_ge(s_kept, len(steps))
            sp.dma_start(B.o["v_prompt"][0, 0].rearrange("(n p) h d -> p n (h d)", p=P), B.vn[:]).then_inc(s_v, 16)
            sp.dma_start(B.o["k_sample"][0].rearrange("b o h d -> (b o) (h d)"), B.qkv_s[:, 1, :]).then_inc(s_v, 16)
            sp.dma_start(B.o["v_sample"][0].rearrange("b o h d -> (b o) (h d)"), B.qkv_s[:, 2, :]).then_inc(s_v, 16)
            sp.wait_ge(s_v, 48)
            sp.wait_ge(s_biast, 16)
            for e in range(2):
                sp.wait_ge(s_k[e], 64)

        @block.tensor
        def _(pe):
            pe.wait_ge(s_in, 32)
            nc.tensor.matmul(B.psum[0:HA, 0, 0:384], rel[:], buckets[:, 0:384], start=True, stop=True)
            nc.tensor.matmul(B.psum[:, 1, 0:HA], buckets[:, 384:384 + P], rel[:], start=True, stop=True)
            nc.tensor.matmul(B.psum[0:NS, 2, 0:HA], buckets[:, 384 + P:384 + P + NS], rel[:], start=True,
                             stop=True).then_inc(s_bias, 1)
            for n, (part, b) in enumerate(steps):
                w = P if b < NBLK else NS
                if n >= 4:
                    pe.wait_ge(s_kept, n - 3)
                for j in range(4):
                    ins = nc.tensor.transpose(B.psum[0:w, 4 + n % 4, j * P:(j + 1) * P],
                                              B.qkv[:, 4 * part + j, b * P:b * P + w], B.ident[:])
                ins.then_inc(s_turned, 1)

        @block.vector
        def _(dve):
            dve.wait_ge(s_bias, 1)
            nc.vector.tensor_scalar(line[:], B.psum[0:HA, 0, 0:384], DH ** 0.5, None, ALU.mult).then_inc(s_biasc, 1)
            nc.vector.tensor_copy(B.bias_s[:, 0, :], B.psum[:, 1, 0:HA]).then_inc(s_biasc, 1)
            nc.vector.tensor_copy(B.bias_s[0:NS, 1, :], B.psum[0:NS, 2, 0:HA]).then_inc(s_biasc, 1)
            for n, (part, b) in enumerate(steps):
                dve.wait_ge(s_turned, n + 1)
                if b == NBLK:
                    out, rows = B.qkv_s[:, part, :], NS
                elif part == 1:
                    out, rows = kn[:, b % 2, :], P
                    if b >= 2:
                        dve.wait_ge(s_k[b % 2], 16 * (b // 2))
                else:
                    out, rows = B.vn[:, b, :], P
                nc.vector.tensor_copy(out, B.psum[0:rows, 4 + n % 4, :]).then_inc(s_kept, 1)
    B.top = mark


def attend(B):
    nc = B.nc
    mark = B.top
    spare = B.qkv[:, 8:12, :].rearrange("p k c -> p (k c)")
    logit = spare[:, 0:2048].rearrange("p (s c) -> p s c", s=2)
    pt = spare[:, 2048:4096].rearrange("p (s c) -> p s c", s=2)
    first = B.take("first_blocks_mask_sb", [P, 2 * P])
    near = B.take("near_mask_sb", [P, 2, 2 * P])
    mx = B.take("row_max_sb", [P, 2, 2])
    nm = B.take("minus_max_sb", [P, 2])
    total = B.take("prob_sum_sb", [P, 2, HA])
    rden = B.take("prob_sum_inverse_sb", [P, HA])
    o = B.take("att_rows_sb", [P, 512])
    left = B.take("scores_left_sb", [P, NBLK * P])
    best = B.take("best_sb", [P, 8])
    s_choice, s_chosen = B.tally("choosing_step"), B.sem("block_chosen")
    ROUNDS = TOPK // 8
    seq = [(i, h) for i in range(NBLK) for h in range(HA)]
    N = len(seq)
    (s_mask, s_near, s_dot, s_log, s_max, s_prob, s_turned, s_pt, s_pv, s_o, s_ot, s_hi, s_lo, s_far, s_rden) = (
        B.sem(x) for x in ("mask_scaled", "near_mask", "logit_products", "logits", "row_max", "probs", "probs_turned",
                           "probs_copied", "values_weighted", "att_rows", "att_turned", "att_high", "att_low",
                           "far_logits", "sum_inverse"))
    width = lambda i: (i + 1) * P

    def mask(i):
        if i == 0:
            return first[:, P:2 * P]
        if i == 1:
            return first[:]
        return B.scores[:, score_offset(i):score_offset(i) + width(i)]

    with nc.Block() as block:
        @block.gpsimd
        def _(pool):
            nc.gpsimd.memset(first[:, 0:P], 0.0).then_inc(s_mask, 1)
            nc.gpsimd.tensor_scalar(first[:, P:2 * P], B.future[:], -BIG, None, ALU.mult).then_inc(s_mask, 1)
            n = 0
            for i in range(NBLK):
                M, L = mask(i), width(i)
                if i >= 2:
                    if i >= LATE:
                        pool.wait_ge(s_chosen, i - LATE + 1)
                    nc.gpsimd.tensor_scalar(M, M, -BIG, None, ALU.mult).then_inc(s_mask, 1)
                pool.wait_ge(s_mask, max(2, i + 1))
                w = min(L, 2 * P)
                for h in range(HA):
                    if n >= 2:
                        pool.wait_ge(s_log, n - 1)
                    nc.gpsimd.tensor_tensor(near[:, n % 2, 0:w], M[:, L - w:L], B.bias[:, h, 2 * P - w:2 * P],
                                            ALU.add).then_inc(s_near, 1)
                    n += 1

        @block.tensor
        def _(pe):
            def dot(n):
                i, h = seq[n]
                L = width(i)
                if n >= 2:
                    pe.wait_ge(s_log, n - 1)
                r = slice(64 * (h % 2), 64 * (h % 2) + 64)
                for c in range(0, L, 512):
                    w = min(512, L - c)
                    ins = nc.tensor.matmul(B.psum[:, 2 * (n % 2) + c // 512, 0:w], B.qkv[r, h // 2, i * P:(i + 1) * P],
                                           B.qkv[r, 4 + h // 2, c:c + w], start=True, stop=True)
                ins.then_inc(s_dot, 1)

            def turn(n):
                i, h = seq[n]
                pe.wait_ge(s_prob, n + 1)
                if n >= 1:
                    pe.wait_ge(s_pt, n)
                for j in range(i + 1):
                    ins = nc.tensor.transpose(B.psum[:, 4 + j // 4, (j % 4) * P:(j % 4 + 1) * P],
                                              logit[:, n % 2, j * P:(j + 1) * P], B.ident[:])
                ins.then_inc(s_turned, 1)

            def weigh(n):
                i, h = seq[n]
                pe.wait_ge(s_pt, n + 1)
                if h == 0 and i >= 1:
                    pe.wait_ge(s_o, i)
                for j in range(i + 1):
                    ins = nc.tensor.matmul(B.psum[:, 6, h * DH:(h + 1) * DH], pt[:, n % 2, j * P:(j + 1) * P],
                                           B.vn[:, j, h * DH:(h + 1) * DH], start=j == 0, stop=j == i)
                ins.then_inc(s_pv, 1)

            def turn_rows(i):
                pe.wait_ge(s_o, i + 1)
                if i >= 1:
                    pe.wait_ge(s_lo, i)
                for j in range(4):
                    ins = nc.tensor.transpose(B.psum[:, 7, j * P:(j + 1) * P], o[:, j * P:(j + 1) * P], B.ident[:])
                ins.then_inc(s_ot, 1)

            dot(0)
            for n in range(N + 1):
                if n + 1 < N:
                    dot(n + 1)
                if n < N:
                    turn(n)
                if n >= 1:
                    weigh(n - 1)
                if n >= 1 and n % HA == 1 and n > 1:
                    turn_rows(n // HA - 1)
            turn_rows(NBLK - 1)

        @block.vector
        def _(dve):
            def logits(n):
                i, h = seq[n]
                L = width(i)
                w = min(L, 2 * P)
                far = L - w
                ps = B.psum[:, 2 * (n % 2):2 * (n % 2) + 2, :].rearrange("p b c -> p (b c)")
                dve.wait_ge(s_dot, n + 1)
                dve.wait_ge(s_near, n + 1)
                if n >= 2:
                    dve.wait_ge(s_turned, n - 1)
                    dve.wait_ge(s_prob, n - 1)
                start = TAKEN
                if far:
                    nc.vector.tensor_tensor_reduce(out=logit[:, n % 2, 0:far], in0=ps[:, 0:far], in1=mask(i)[:, 0:far],
                                                   scale=DH ** -0.5, scalar=TAKEN, op0=ALU.add, op1=ALU.max,
                                                   accum_out=mx[:, n % 2, 0:1]).then_inc(s_far, 1)
                    dve.wait_ge(s_far, n + 1 - 2 * HA)
                    start = mx[:, n % 2, 0:1]
                nc.vector.tensor_tensor_reduce(out=logit[:, n % 2, far:L], in0=ps[:, far:L], in1=near[:, n % 2, 0:w],
                                               scale=DH ** -0.5, scalar=start, op0=ALU.add, op1=ALU.max,
                                               accum_out=mx[:, n % 2, 1:2]).then_inc(s_log, 1)
                dve.wait_ge(s_log, n + 1)
                nc.vector.tensor_scalar(nm[:, n % 2:n % 2 + 1], mx[:, n % 2, 1:2], -1.0, None, ALU.mult).then_inc(s_max, 1)
                dve.wait_ge(s_max, n + 1)

            def rows(i):
                dve.wait_ge(s_pv, HA * (i + 1))
                dve.wait_ge(s_prob, HA * (i + 1))
                if i >= 1:
                    dve.wait_ge(s_ot, i)
                    dve.wait_ge(s_o, i)
                nc.vector.reciprocal(rden[:], total[:, i % 2, :]).then_inc(s_rden, 1)
                dve.wait_ge(s_rden, i + 1)
                nc.vector.tensor_tensor(o[:].rearrange("p (h d) -> p h d", h=HA),
                                        B.psum[:, 6, :].rearrange("p (h d) -> p h d", h=HA),
                                        rden[:].unsqueeze(2).to_broadcast([P, HA, DH]), ALU.mult).then_inc(s_o, 1)

            def low(i):
                dve.wait_ge(s_hi, i + 1)
                out = B.hl[:, 0:4, i * P:(i + 1) * P]
                nc.vector.tensor_tensor(out, B.psum[:, 7, :].rearrange("p (k c) -> p k c", k=4),
                                        B.hh[:, 0:4, i * P:(i + 1) * P].bitcast(F32), ALU.subtract).then_inc(s_lo, 1)

            def choose_step(i, r, half):
                S, W, m8 = mask(i), left[:, 0:width(i)], best[:]
                source = S if r == 0 else W
                if s_choice.count:
                    dve.wait_ge(s_choice.sem, s_choice.value())
                if half == 0:
                    s_choice.up(nc.vector.max(m8, source))
                elif half == 1:
                    s_choice.up(nc.vector.match_replace(W, m8, source, TAKEN))
                if r == ROUNDS - 1 and half == 1:
                    dve.wait_ge(s_choice.sem, s_choice.value())
                    nc.vector.scalar_tensor_tensor(out=S, in0=W, scalar=1.0, in1=S, op0=ALU.mult,
                                                   op1=ALU.is_equal).then_inc(s_chosen, 1)
                    dve.wait_ge(s_chosen, i - LATE + 1)

            steps, heads_work = 0, sum(width(i) for i, h in seq if i < NBLK - 1)
            all_steps = (NBLK - LATE) * ROUNDS * 2
            work = 0
            for n in range(N):
                logits(n)
                work += width(seq[n][0])
                while steps < all_steps and steps * heads_work < work * all_steps:
                    choose_step(LATE + steps // (2 * ROUNDS), steps // 2 % ROUNDS, steps % 2)
                    steps += 1
                if n >= HA and n % HA == 1:
                    rows(n // HA - 1)
                if n >= HA and n % HA == 3:
                    low(n // HA - 1)
            rows(NBLK - 1)
            low(NBLK - 1)

        @block.scalar
        def _(act):
            def high(i):
                act.wait_ge(s_ot, i + 1)
                nc.scalar.copy(B.hh[:, 0:4, i * P:(i + 1) * P],
                               B.psum[:, 7, :].rearrange("p (k c) -> p k c", k=4)).then_inc(s_hi, 1)

            def copy_turned(n):
                i, h = seq[n]
                L = width(i)
                act.wait_ge(s_turned, n + 1)
                if n >= 2:
                    act.wait_ge(s_pv, n - 1)
                nc.scalar.copy(pt[:, n % 2, 0:L], B.psum[:, 4:6, :].rearrange("p b c -> p (b c)")[:, 0:L]).then_inc(s_pt, 1)

            for n in range(N):
                i, h = seq[n]
                L = width(i)
                act.wait_ge(s_max, n + 1)
                if h == 0 and i >= 2:
                    act.wait_ge(s_rden, i - 1)
                nc.scalar.activation(logit[:, n % 2, 0:L], logit[:, n % 2, 0:L], ACT.Exp, bias=nm[:, n % 2:n % 2 + 1],
                                     accum_out=total[:, i % 2, h:h + 1]).then_inc(s_prob, 1)
                if n >= 1:
                    copy_turned(n - 1)
                if n >= HA and n % HA == 2:
                    high(n // HA - 1)
            copy_turned(N - 1)
            high(NBLK - 1)
    B.top = mark


def attend_samples(B):
    nc = B.nc
    mark = B.top
    KS, VS = 3, 3
    kp = B.take("k_pages_sb", [P, KS, PAGES, 512])
    vp = B.take("v_pages_sb", [P, VS, PAGES, 512])
    pick = B.take("pick_sb", [NS, NS, P])
    maskt = B.take("sample_mask_sb", [P, PAGES, NS])
    logit = B.take("sample_logits_sb", [P, NS, PAGES, HA])
    own_prod = B.take("own_product_sb", [NS, 512])
    own = B.take("own_logit_sb", [NS, HA])
    owned = B.take("own_logit_diagonal_sb", [NS, NS, HA])
    pmax = B.take("page_max_sb", [P, NS * HA])
    hmax = B.take("head_max_sb", [NS * HA, 1])
    dmax = B.take("head_max_diagonal_sb", [NS * HA, NS * HA])
    pown = B.take("own_prob_sb", [P, NS * HA])
    pownd = B.take("own_prob_diagonal_sb", [NS, NS, HA])
    den = B.take("denominator_sb", [P, NS * HA])
    att = B.take("sample_att_sb", [P, 4, NS])
    kept = pick[:].rearrange("p (s b) c -> p s (b c)", s=2)
    s_kept, s_col = B.sem("own_columns_kept"), B.sem("columns_summed")
    s_k, s_v = [B.sem(f"k_pages_{b}") for b in range(NS)], [B.sem(f"v_pages_{b}") for b in range(NS)]
    s_pick = B.sem("pick_loaded")
    (s_mt, s_q, s_prod, s_dots, s_ob, s_mxt, s_mb, s_sub, s_exp, s_sum, s_den, s_pvd, s_fin, s_hi, s_owned, s_pmax,
     s_dmax, s_pownd) = (B.sem(x) for x in (
         "mask_turned", "q_spread", "k_times_q", "dots", "own_spread", "max_turned", "max_spread", "max_subtracted",
         "sample_probs", "probs_summed", "denominators", "sample_values", "sample_att", "sample_att_high",
         "own_logits", "page_max", "max_diagonal", "own_probs_diagonal"))
    s_step = B.tally("sample_step")
    eye8 = B.ident[0:NS, 0:NS].unsqueeze(2).to_broadcast([NS, NS, HA])

    def load(eng, cache, place, b, sem):
        with eng.Fori(0, PAGES) as j:
            page = eng.value_load(B.pages[0:1, bass.ds(j + b * PAGES, 1)], min_val=0, max_val=NPOOL - 1)
            eng.dma_start(place[:, bass.ds(j, 1), :],
                          B.i[cache][0][bass.ds(page, 1)].rearrange("o p h d -> p o (h d)")).then_inc(sem, 16)

    def load_keys(eng, parity):
        for b in range(parity, NS, 2):
            if b >= KS:
                eng.wait_ge(s_dots, b - KS + 1)
            load(eng, "cache_k", kp[:, b % KS], b, s_k[b])

    def key_place(b):
        return (NS - KS + b - VS) % KS

    def v_place(b):
        return vp[:, b] if b < VS else kp[:, key_place(b)] if b < VS + KS else vp[:, b - VS - KS]

    with nc.Block() as block:
        @block.sync
        def _(sp):
            sp.dma_start(pick[:].rearrange("p b c -> p (b c)"), B.i["pick"]).then_inc(s_pick, 16)
            load_keys(sp, 0)

        @block.gpsimd
        def _(pool):
            load_keys(pool, 1)

        @block.tensor
        def _(pe):
            def to_columns(b):
                pe.wait_ge(s_kept, b + 1)
                for t in range(4):
                    ins = nc.tensor.matmul(B.psum[:, 7, b * 4 + t:b * 4 + t + 1], kept[:, b % 2, t * P:(t + 1) * P],
                                           B.ones[0:HA, 0:1], start=True, stop=True)
                ins.then_inc(s_col, 1)

            for j in range(PAGES):
                ins = nc.tensor.transpose(B.psum[:, 0, j * NS:(j + 1) * NS], B.scores_s[:, j * P:(j + 1) * P],
                                          B.ident[0:NS, 0:NS])
            ins.then_inc(s_mt, 1)
            pe.wait_ge(s_pick, 16)
            for b in range(NS):
                if b >= 2:
                    pe.wait_ge(s_prod, b - 1)
                nc.tensor.matmul(B.psum[:, 1 + b % 2, :], pick[:, b, :], B.qkv_s[:, 0, :], start=True, stop=True).then_inc(s_q, 1)
            pe.wait_ge(s_owned, 1)
            nc.tensor.matmul(B.psum[:, 3, 0:NS * HA], B.ones[0:NS, :], owned[:].rearrange("p b h -> p (b h)"),
                             start=True, stop=True).then_inc(s_ob, 1)
            pe.wait_ge(s_pmax, 2)
            nc.tensor.transpose(B.psum[0:NS * HA, 4, 0:P], pmax[:], B.ident[:]).then_inc(s_mxt, 1)
            pe.wait_ge(s_dmax, 1)
            nc.tensor.matmul(B.psum[:, 5, 0:NS * HA], B.ones[0:NS * HA, :], dmax[:], start=True, stop=True).then_inc(s_mb, 1)
            pe.wait_ge(s_exp, 2)
            nc.tensor.matmul(B.psum[:, 6, :], B.ones[:], logit[:].rearrange("p b g h -> p (b g h)"),
                             start=True, stop=True).then_inc(s_sum, 1)
            pe.wait_ge(s_pownd, 1)
            for b in range(NS):
                pe.wait_ge(s_v[b], 16 * PAGES)
                if b >= 2:
                    pe.wait_ge(s_kept, b - 1)
                out = B.psum[0:HA, 1 + b % 2, :]
                for j in range(PAGES):
                    nc.tensor.matmul(out, logit[:, b, j, :], v_place(b)[:, j, :], start=j == 0, stop=False)
                nc.tensor.matmul(out, pownd[:, b, :], B.qkv_s[:, 2, :], start=False, stop=True).then_inc(s_pvd, 1)
                if b >= 1:
                    to_columns(b - 1)
            to_columns(NS - 1)

        @block.vector
        def _(dve):
            def step(ins):
                done(dve, ins, s_step)

            dve.wait_ge(s_mt, 1)
            step(nc.vector.tensor_scalar(maskt[:].rearrange("p g b -> p (g b)"), B.psum[:, 0, 0:PAGES * NS], -BIG, None, ALU.mult))
            step(nc.vector.tensor_tensor(own_prod[:], B.qkv_s[:, 0, :], B.qkv_s[:, 1, :], ALU.mult))
            step(nc.vector.tensor_reduce(own[:], own_prod[:].rearrange("p (h d) -> p h d", h=HA), AX_X, ALU.add))
            step(nc.vector.scalar_tensor_tensor(out=own[:], in0=own[:], scalar=DH ** -0.5, in1=B.bias_s[0:NS, 1, :],
                                                op0=ALU.mult, op1=ALU.add))
            step(nc.vector.tensor_scalar(hmax[0:NS, :], B.scores_s[:, KEYS_S - 1:KEYS_S], -BIG, None, ALU.mult))
            step(nc.vector.tensor_scalar(own[:], own[:], hmax[0:NS, 0:1], None, ALU.add))
            nc.vector.tensor_tensor(owned[:], own[:].unsqueeze(1).to_broadcast([NS, NS, HA]), eye8,
                                    ALU.mult).then_inc(s_owned, 1)
            for b in range(NS):
                dve.wait_ge(s_k[b], 16 * PAGES)
                dve.wait_ge(s_q, b + 1)
                nc.vector.tensor_tensor(kp[:, b % KS], kp[:, b % KS],
                                        B.psum[:, 1 + b % 2, :].unsqueeze(1).to_broadcast([P, PAGES, 512]),
                                        ALU.mult).then_inc(s_prod, 1)
                dve.wait_ge(s_prod, b + 1)
                nc.vector.tensor_reduce(logit[:, b].rearrange("p g h -> p (g h)"),
                                        kp[:, b % KS].rearrange("p g (h d) -> p (g h) d", d=DH), AX_X, ALU.add).then_inc(s_dots, 1)
            dve.wait_ge(s_dots, NS)
            flat = logit[:].rearrange("p b g h -> p (b g h)")
            step(nc.vector.tensor_scalar(flat, flat, DH ** -0.5, None, ALU.mult))
            step(nc.vector.tensor_tensor(logit[:], logit[:],
                                         maskt[:].rearrange("p g b -> p b g").unsqueeze(3).to_broadcast([P, NS, PAGES, HA]), ALU.add))
            step(nc.vector.tensor_tensor(logit[:, :, PAGES - 1, :], logit[:, :, PAGES - 1, :],
                                         B.bias_s[:, 0, :].unsqueeze(1).to_broadcast([P, NS, HA]), ALU.add))
            nc.vector.tensor_reduce(pmax[:].rearrange("p (b h) -> p b h", b=NS),
                                    logit[:].rearrange("p b g h -> p b h g"), AX_X, ALU.max).then_inc(s_pmax, 1)
            dve.wait_ge(s_pmax, 1)
            dve.wait_ge(s_ob, 1)
            nc.vector.tensor_tensor(pmax[:], pmax[:], B.psum[:, 3, 0:NS * HA], ALU.max).then_inc(s_pmax, 1)
            dve.wait_ge(s_mxt, 1)
            step(nc.vector.tensor_reduce(hmax[:], B.psum[0:NS * HA, 4, 0:P], AX_X, ALU.max))
            nc.vector.tensor_scalar(dmax[:], B.ident[0:NS * HA, 0:NS * HA], hmax[:, 0:1], None, ALU.mult).then_inc(s_dmax, 1)
            dve.wait_ge(s_mb, 1)
            step(nc.vector.tensor_copy(den[:], B.psum[:, 5, 0:NS * HA]))
            nc.vector.tensor_tensor(logit[:], logit[:], den[:].rearrange("p (b h) -> p b h", b=NS).unsqueeze(2)
                                    .to_broadcast([P, NS, PAGES, HA]), ALU.subtract).then_inc(s_sub, 1)
            nc.vector.tensor_tensor(pown[:], B.psum[:, 3, 0:NS * HA], den[:], ALU.subtract).then_inc(s_sub, 1)
            dve.wait_ge(s_exp, 2)
            nc.vector.tensor_tensor(pownd[:], pown[0:NS, :].rearrange("p (b h) -> p b h", b=NS), eye8, ALU.mult).then_inc(s_pownd, 1)
            dve.wait_ge(s_sum, 1)
            dve.wait_ge(s_sub, 2)
            step(nc.vector.tensor_reduce(den[:].rearrange("p (b h) -> p b h", b=NS),
                                         B.psum[:, 6, :].rearrange("p (b g h) -> p b h g", b=NS, g=PAGES), AX_X, ALU.add))
            step(nc.vector.tensor_tensor(den[:], den[:], pown[:], ALU.add))
            step(nc.vector.reciprocal(den[:], den[:]))
            for b in range(NS):
                dve.wait_ge(s_pvd, b + 1)
                if b >= 2:
                    dve.wait_ge(s_col, b - 1)
                nc.vector.tensor_tensor(kept[:, b % 2, :].rearrange("h (g d) -> h g d", g=HA),
                                        B.psum[0:HA, 1 + b % 2, :].rearrange("h (g d) -> h g d", g=HA),
                                        B.ident[0:HA, 0:HA].unsqueeze(2).to_broadcast([HA, HA, DH]), ALU.mult).then_inc(s_kept, 1)
            dve.wait_ge(s_col, NS)
            for e in range(2):
                r = slice(64 * e, 64 * e + 64)
                nc.vector.tensor_tensor(
                    att[r, :, :], B.psum[r, 7, 0:NS * 4].rearrange("p (b t) -> p t b", b=NS),
                    den[r, :].rearrange("p (b t e) -> p e t b", b=NS, e=2)[:, e], ALU.mult).then_inc(s_fin, 1)
            dve.wait_ge(s_fin, 2)
            dve.wait_ge(s_hi, 1)
            step(nc.vector.tensor_tensor(B.hl[:, 0:4, SEQ:TOK], att[:], B.hh[:, 0:4, SEQ:TOK].bitcast(F32), ALU.subtract))

        @block.scalar
        def _(act):
            for b in range(VS + KS):
                act.wait_ge(s_dots, 2 * b + 1 if b < VS else NS - KS + 1 + b - VS)
                load(act, "cache_v", v_place(b), b, s_v[b])
            act.wait_ge(s_sub, 2)
            nc.scalar.activation(logit[:].rearrange("p b g h -> p (b g h)"), logit[:].rearrange("p b g h -> p (b g h)"),
                                 ACT.Exp).then_inc(s_exp, 1)
            nc.scalar.activation(pown[:], pown[:], ACT.Exp).then_inc(s_exp, 1)
            for b in range(VS + KS, NS):
                act.wait_ge(s_pvd, b - VS - KS + 1)
                load(act, "cache_v", v_place(b), b, s_v[b])
            act.wait_ge(s_fin, 2)
            nc.scalar.copy(B.hh[:, 0:4, SEQ:TOK], att[:]).then_inc(s_hi, 1)
    B.top = mark


def retention(B):
    nc = B.nc
    mark = B.top
    r = B.take("retention_parts_sb", [P, 12, TOK])
    o = B.take("retention_out_sb", [P, HR, TOK])
    sw = B.take("halves_swapped_sb", [P, 4, TOK])
    vrow = sw[:].rearrange("p k c -> p (k c)")[:, 0:4096].rearrange("p (n c) -> p n c", c=512)
    cs = B.take("cos_sin_sb", [P, 2, TOK])
    kdec = cs[:].rearrange("p k c -> p (k c)")[:, 0:2048].rearrange("p (n c) -> p n c", c=256)
    tab = B.take("retention_tables_sb", [P, HR * P + 2 * P + HR + 4])
    decay, qdecay = tab[:, 0:512].rearrange("p (h t) -> p h t", h=HR), tab[:, 512:768].rearrange("p (c t) -> p c t", c=2)
    kdecay, sdecay = tab[:, 768:772], tab[:, 772:776]
    srow = B.take("sample_kv_rows_sb", [NS, 256 + 512])
    scd = B.take("decayed_scores_sb", [P, 2, HR, P])
    by_parity = lambda a: a.rearrange("p (c two) t -> p two c t", two=2)
    pairs = lambda bank: B.psum[:, bank:bank + 2, 0:2 * P].rearrange("p two (c t) -> p two c t", c=2)
    state = B.take("retention_state_sb", [P, 2, 2, P])
    s_load, s_tab = B.sem("parts_loaded"), B.sem("tables_loaded")
    s_swap, s_rot, s_sin, s_gate = B.sem("halves_swapped"), B.sem("rotated"), B.sem("sin_part"), B.sem("gates")
    s_turned, s_kept, s_qd = B.sem("kv_turned"), B.sem("kv_rows"), B.sem("q_decayed")
    s_sc, s_scd, s_o, s_okept, s_st, s_state = (B.sem(x) for x in (
        "chunk_scores", "chunk_scores_decayed", "chunk_out", "chunk_out_kept", "chunk_state", "state_updated"))
    s_out, s_kd = B.sem("prompt_state_stored"), B.sem("k_rows_decayed")
    qdb = B.take("q_decayed_sb", [P, 2, 2, P])
    with nc.Block() as block:
        @block.sync
        def _(sp):
            sp.dma_start(r[:], B.r_scratch.rearrange("k p c -> p k c")).then_inc(s_load, 16)
            for dst, name in ((cs[:, 0, :], "cos"), (cs[:, 1, :], "sin"), (tab[:, 0:512], "decay"), (tab[:, 512:768], "qdecay"),
                              (kdecay, "kdecay"), (sdecay, "sdecay")):
                sp.dma_start(dst, B.i[name]).then_inc(s_tab, 16)
            sp.wait_ge(s_state, 2 * NBLK)
            sp.dma_start(B.o["ret_prompt"][0, 0].rearrange("(c two) k v -> (two k) c v", two=2),
                         state[:, (NBLK - 1) % 2]).then_inc(s_out, 16)
            sp.wait_ge(s_out, 16)

        @block.scalar
        def _(act):
            act.wait_ge(s_load, 16)
            for a in range(4):
                src = a ^ 1
                nc.scalar.copy(sw[32 * a:32 * a + 32, :, :], r[32 * src:32 * src + 32, 0:4, :]).then_inc(s_swap, 1)
            act.wait_ge(s_rot, 2)
            nc.scalar.mul(r[:, 2:4, :], r[:, 2:4, :], DKR ** -0.5).then_inc(s_rot, 1)
            nc.scalar.activation(r[:, 8:12, :], r[:, 8:12, :], ACT.Silu).then_inc(s_gate, 1)
            for n in range(NBLK + 1):
                act.wait_ge(s_turned, 2 * n + 1)
                if n < NBLK:
                    nc.scalar.copy(vrow[:, n, :], B.psum[:, 2 * (n % 2), :]).then_inc(s_kept, 1)
                else:
                    nc.scalar.copy(srow[:, 256:768], B.psum[0:NS, 2 * (n % 2), :]).then_inc(s_kept, 1)
                    act.wait_ge(s_turned, 2 * n + 2)
                    nc.scalar.copy(srow[:, 0:256], B.psum[0:NS, 2 * (n % 2) + 1, 0:256]).then_inc(s_kept, 1)
            for n in range(NBLK):
                act.wait_ge(s_o, n + 1)
                nc.scalar.copy(by_parity(o[:, :, n * P:(n + 1) * P]), pairs(2 + 2 * (n % 2))).then_inc(s_okept, 1)

        @block.gpsimd
        def _(pool):
            pool.wait_ge(s_tab, 16 * 6)
            pool.wait_ge(s_swap, 4)
            nc.gpsimd.tensor_tensor(sw[:], sw[:], cs[:, 1, :].unsqueeze(1).to_broadcast([P, 4, TOK]), ALU.mult).then_inc(s_sin, 1)
            for n in range(NBLK):
                if n == 0:
                    pool.wait_ge(s_rot, 2)
                if n >= 2:
                    pool.wait_ge(s_o, n - 1)
                nc.gpsimd.tensor_tensor(qdb[:, n % 2], r[:, 0:2, n * P:(n + 1) * P], qdecay, ALU.mult).then_inc(s_qd, 1)

        @block.vector
        def _(dve):
            dve.wait_ge(s_tab, 16 * 6)
            dve.wait_ge(s_load, 16)
            dve.wait_ge(s_swap, 4)
            nc.vector.tensor_tensor(r[:, 0:4, :], r[:, 0:4, :], cs[:, 0, :].unsqueeze(1).to_broadcast([P, 4, TOK]),
                                    ALU.mult).then_inc(s_rot, 1)
            dve.wait_ge(s_rot, 1)
            dve.wait_ge(s_sin, 1)
            nc.vector.tensor_tensor(r[:, 0:4, :], r[:, 0:4, :], sw[:], ALU.add).then_inc(s_rot, 1)
            dve.wait_ge(s_rot, 2)
            for n in range(NBLK):
                dve.wait_ge(s_turned, 2 * n + 2)
                nc.vector.tensor_tensor(kdec[:, n, :].rearrange("p (h d) -> p h d", h=HR),
                                        B.psum[:, 2 * (n % 2) + 1, 0:256].rearrange("p (h d) -> p h d", h=HR),
                                        kdecay.unsqueeze(2).to_broadcast([P, HR, DKR]), ALU.mult).then_inc(s_kd, 1)
            for n in range(NBLK):
                dve.wait_ge(s_sc, n + 1)
                if n >= 2:
                    dve.wait_ge(s_o, n - 1)
                nc.vector.tensor_tensor(by_parity(scd[:, n % 2]), pairs(0), by_parity(decay), ALU.mult).then_inc(s_scd, 1)
                dve.wait_ge(s_st, n + 1)
                for c in range(2):
                    ps = B.psum[:, 7, c * P:(c + 1) * P]
                    new = state[:, n % 2, c, :]
                    if n == 0:
                        nc.vector.tensor_copy(new, ps).then_inc(s_state, 1)
                    else:
                        dve.wait_ge(s_state, 2 * n)
                        nc.vector.scalar_tensor_tensor(out=new, in0=state[:, (n - 1) % 2, c, :], scalar=sdecay[:, c:c + 1],
                                                       in1=ps, op0=ALU.mult, op1=ALU.add).then_inc(s_state, 1)

        @block.tensor
        def _(pe):
            pe.wait_ge(s_rot, 3)
            for n in range(NBLK + 1):
                w = P if n < NBLK else NS
                if n >= 2:
                    pe.wait_ge(s_kept, n - 1)
                    pe.wait_ge(s_kd, n - 1)
                for j in range(4):
                    ins = nc.tensor.transpose(B.psum[0:w, 2 * (n % 2), j * P:(j + 1) * P], r[:, 4 + j, n * P:n * P + w], B.ident[:])
                ins.then_inc(s_turned, 1)
                for j in range(2):
                    ins = nc.tensor.transpose(B.psum[0:w, 2 * (n % 2) + 1, j * P:(j + 1) * P], r[:, 2 + j, n * P:n * P + w], B.ident[:])
                ins.then_inc(s_turned, 1)
            pe.wait_ge(s_kept, NBLK + 2)

            def scores(n):
                if n >= 1:
                    pe.wait_ge(s_scd, n)
                for h in range(HR):
                    q = slice(64 * (h % 2), 64 * (h % 2) + 64)
                    ins = nc.tensor.matmul(B.psum[:, h % 2, (h // 2) * P:(h // 2 + 1) * P], r[q, 2 + h // 2, n * P:(n + 1) * P],
                                           r[q, h // 2, n * P:(n + 1) * P], start=True, stop=True)
                ins.then_inc(s_sc, 1)

            for n in range(NBLK):
                scores(n)
                if n >= 1:
                    pe.wait_ge(s_state, 2 * n)
                for h in range(HR):
                    q = slice(64 * (h % 2), 64 * (h % 2) + 64)
                    ins = nc.tensor.matmul(B.psum[q, 7, (h // 2) * P:(h // 2 + 1) * P], kdec[:, n, h * DKR:(h + 1) * DKR],
                                           vrow[:, n, h * P:(h + 1) * P], start=True, stop=True)
                ins.then_inc(s_st, 1)
                pe.wait_ge(s_scd, n + 1)
                pe.wait_ge(s_qd, n + 1)
                if n >= 2:
                    pe.wait_ge(s_okept, n - 1)
                for h in range(HR):
                    q = slice(64 * (h % 2), 64 * (h % 2) + 64)
                    out = B.psum[:, 2 + 2 * (n % 2) + h % 2, (h // 2) * P:(h // 2 + 1) * P]
                    ins = nc.tensor.matmul(out, vrow[:, n, h * P:(h + 1) * P], scd[:, n % 2, h, :],
                                           start=True, stop=n == 0)
                    if n >= 1:
                        ins = nc.tensor.matmul(out, state[q, (n - 1) % 2, h // 2, :], qdb[q, n % 2, h // 2, :],
                                               start=False, stop=True)
                ins.then_inc(s_o, 1)

    flat = sw[:].rearrange("p k c -> p (k c)")
    st = flat[:, 0:2048].rearrange("p (b c v) -> p b c v", b=NS, c=2)
    kd = flat[0:NS, 2048:4096].rearrange("p (b n) -> p b n", b=NS)
    s_stl, s_sto = B.sem("sample_state_loaded"), B.sem("sample_state_stored")
    s_kd2, s_outer, s_new, s_os, s_ok = (B.sem(x) for x in ("sample_k_diagonal", "sample_outer", "sample_state_new",
                                                           "sample_out", "sample_out_kept"))
    with nc.Block() as block:
        @block.sync
        def _(sp):
            for b in range(NS):
                sp.dma_start(st[:, b], B.i["state_ret"][0, b].rearrange("(c two) k v -> (two k) c v", two=2)).then_inc(s_stl, 16)
            sp.wait_ge(s_new, 2)
            for b in range(NS):
                sp.dma_start(B.o["ret_sample"][0, b].rearrange("(c two) k v -> (two k) c v", two=2), st[:, b]).then_inc(s_sto, 16)
            sp.wait_ge(s_sto, 16 * NS)

        @block.vector
        def _(dve):
            nc.vector.tensor_tensor(kd, srow[:, 0:256].unsqueeze(1).to_broadcast([NS, NS, 256]),
                                    B.ident[0:NS, 0:NS].unsqueeze(2).to_broadcast([NS, NS, 256]), ALU.mult).then_inc(s_kd2, 1)
            dve.wait_ge(s_stl, 16 * NS)
            dve.wait_ge(s_outer, 1)
            for c in range(2):
                nc.vector.scalar_tensor_tensor(
                    out=st[:, :, c, :], in0=st[:, :, c, :], scalar=sdecay[:, 2 + c:3 + c],
                    in1=B.psum[:, 0:4, :].rearrange("p a (b c v) -> p c (a b) v", c=2, b=2)[:, c],
                    op0=ALU.mult, op1=ALU.add).then_inc(s_new, 1)
            dve.wait_ge(s_os, 1)
            nc.vector.tensor_copy(by_parity(o[:, :, SEQ:TOK]),
                                  B.psum[:, 4:6, 0:2 * NS].rearrange("p two (c b) -> p two c b", c=2)).then_inc(s_ok, 1)

        @block.tensor
        def _(pe):
            pe.wait_ge(s_kd2, 1)
            for b in range(NS):
                for h in range(HR):
                    q = slice(64 * (h % 2), 64 * (h % 2) + 64)
                    c0 = (b % 2) * 256 + (h // 2) * P
                    ins = nc.tensor.matmul(B.psum[q, b // 2, c0:c0 + P], kd[:, b, h * DKR:(h + 1) * DKR],
                                           srow[:, 256 + h * P:256 + (h + 1) * P], start=True, stop=True)
            ins.then_inc(s_outer, 1)
            pe.wait_ge(s_new, 2)
            for b in range(NS):
                for h in range(HR):
                    q = slice(64 * (h % 2), 64 * (h % 2) + 64)
                    ins = nc.tensor.matmul(B.psum[:, 4 + h % 2, (h // 2) * NS + b:(h // 2) * NS + b + 1], st[q, b, h // 2, :],
                                           r[q, h // 2, SEQ + b:SEQ + b + 1], start=True, stop=True)
            ins.then_inc(s_os, 1)

    oc = r[:, 0:4, :]
    sq = sw
    s_sum, s_oc, s_sq, s_sum2, s_rs, s_on, s_hi, s_lo = (B.sem(x) for x in (
        "head_summed", "centred", "centred_square", "square_summed", "inverse_deviation", "gated", "ret_high", "ret_low"))
    wide = lambda a: a.rearrange("p (t c) -> p t c", t=NT)
    with nc.Block() as block:
        @block.tensor
        def _(pe):
            def total(h):
                if h >= 1:
                    pe.wait_ge(s_oc, h)
                for t in range(NT):
                    ins = nc.tensor.matmul(B.psum[:, t, 0:TT], B.ones[:], o[:, h, tcols(t)], start=True, stop=True)
                ins.then_inc(s_sum, 1)

            total(0)
            for h in range(HR):
                if h + 1 < HR:
                    total(h + 1)
                pe.wait_ge(s_sq, h + 1)
                if h >= 1:
                    pe.wait_ge(s_rs, 2 * h - 1)
                for t in range(NT):
                    ins = nc.tensor.matmul(B.psum[:, 3 + t, 0:TT], B.ones[:], sq[:, h, tcols(t)], start=True, stop=True)
                ins.then_inc(s_sum2, 1)

        @block.vector
        def _(dve):
            for h in range(HR):
                dve.wait_ge(s_sum, h + 1)
                nc.vector.scalar_tensor_tensor(out=wide(oc[:, h, :]), in0=B.psum[:, 0:3, 0:TT], scalar=-1.0 / DVR,
                                               in1=wide(o[:, h, :]), op0=ALU.mult, op1=ALU.add).then_inc(s_oc, 1)
            for h in range(HR):
                dve.wait_ge(s_oc, h + 1)
                dve.wait_ge(s_rs, 2 * h + 2)
                nc.vector.tensor_tensor(o[:, h, :], oc[:, h, :], sq[:, h, :], ALU.mult).then_inc(s_on, 1)
                dve.wait_ge(s_on, 2 * h + 1)
                nc.vector.tensor_tensor(o[:, h, :], o[:, h, :], r[:, 8 + h, :], ALU.mult).then_inc(s_on, 1)

        @block.scalar
        def _(act):
            for h in range(HR):
                act.wait_ge(s_oc, h + 1)
                nc.scalar.activation(sq[:, h, :], oc[:, h, :], ACT.Square).then_inc(s_sq, 1)
                act.wait_ge(s_sum2, h + 1)
                nc.scalar.activation(wide(sq[:, h, :]), B.psum[:, 3:6, 0:TT], ACT.Ln, bias=B.eps[:, 0:1], scale=1.0 / DVR).then_inc(s_rs, 1)
                act.wait_ge(s_rs, 2 * h + 1)
                nc.scalar.activation(sq[:, h, :], sq[:, h, :], ACT.Exp, scale=-0.5).then_inc(s_rs, 1)
            for h in range(HR):
                act.wait_ge(s_on, 2 * h + 2)
                nc.scalar.copy(B.hh[:, 4 + h, :], o[:, h, :]).then_inc(s_hi, 1)

        @block.gpsimd
        def _(pool):
            for h in range(HR):
                pool.wait_ge(s_hi, h + 1)
                nc.gpsimd.tensor_tensor(B.hl[:, 4 + h, :], o[:, h, :], B.hh[:, 4 + h, :].bitcast(F32), ALU.subtract).then_inc(s_lo, 1)
    B.top = mark


def project_add(B, w, load_x=True):
    nc = B.nc
    U0 = B.unit
    par = lambda e: (U0 + e) % 2
    s_x = B.sem("x_loaded")
    with nc.Block() as block:
        @block.sync
        def _(sp):
            B.load_weights(sp, U0, par(0), w[0])
            B.load_weights(sp, U0 + 1, par(1), w[1])
            if load_x:
                sp.dma_start(B.x[:], B.x_scratch).then_inc(s_x, 16)
            with sp.Fori(1, 4) as j:
                for e in range(2):
                    B.load_weights(sp, j * 2 + (U0 + e), par(e), w[bass.ds(j * 2 + e, 1)].rearrange("o p k m -> p (o k) m"))

        @block.gpsimd
        def _(pool):
            with pool.Fori(0, 4) as j:
                for e in range(2):
                    B.split_low(pool, j * 2 + (U0 + e), par(e))

        @block.scalar
        def _(act):
            with act.Fori(0, 4) as j:
                for e in range(2):
                    B.split_high(act, j * 2 + (U0 + e), par(e))

        @block.tensor
        def _(pe):
            with pe.Fori(0, 4) as j:
                for e in range(2):
                    B.multiply(pe, j * 2 + (U0 + e), par(e), B.hh, B.hl)

        @block.vector
        def _(dve):
            if load_x:
                dve.wait_ge(s_x, 16)
            with dve.Fori(0, 4) as j:
                for e in range(2):
                    for t in range(NT):
                        B.await_tile(dve, j * 2 + (U0 + e), t)
                        xs = B.x[:, bass.ds(j * 2 + e, 1), tcols(t)].rearrange("p o c -> p (o c)")
                        nc.vector.tensor_tensor(xs, xs, B.tile(par(e), t), ALU.add).then_inc(B.s_tile_free, 1)
    B.unit += 8



def time_steps(B):
    nc = B.nc
    HC = NBLK * NH
    B.cw = B.take("conv_weights_sb", [P, 32, CW + 1])
    B.nw = B.take("ssm_norm_sb", [P, 16])
    B.dskip = B.take("d_skip_sb", [P, NH])
    B.dt = B.take("dt_rows_sb", [P, HC])
    B.acs = B.take("decay_sum_rows_sb", [P, HC])
    B.eacs = B.take("decay_rows_sb", [P, HC])
    B.dend = B.take("decay_to_end_sb", [P, HC])
    B.etot = B.take("chunk_decay_sb", [P, HC])
    B.chs = B.take("sample_channel_values_sb", [P, 16, 2 * NS + 1])
    B.hist = B.take("conv_history_sb", [P, 32, NS * (CW - 1)])
    mark = B.top
    raw = B.take("dt_raw_sb", [NH, TOK])
    dtt = B.take("dt_sb", [NH, TOK])
    dta = B.take("dt_a_sb", [NH, TOK])
    sm = B.take("head_values_sb", [NH, 4])
    dar = B.take("dt_a_rows_sb", [P, HC])
    expand = B.take("expand_sb", [NH, 16, P])
    srhs = B.take("sample_head_values_sb", [NH, 2 * NS + 1])
    hrow = B.take("history_rows_sb", [NS * (CW - 1), CONV_DIM])
    acst = B.take("decay_sum_sb", [NH, SEQ])
    tot = B.take("chunk_sum_sb", [P, HC])
    B.acs_scratch = nc.dram_tensor("decay_sum_scratch", (NH, SEQ), F32, kind="Internal").ap()
    U0 = B.unit
    par = U0 % 2
    w_in = B.i["w_in_odd"][0].rearrange("(k p) n -> p k n", p=P)
    (s_raw, s_act, s_rows, s_t, s_sums, s_sumc, s_exp, s_h, s_hc, s_ch, s_chc) = (B.sem(x) for x in (
        "dt_copied", "dt_exp", "dt_rows", "dt_turned", "sums", "sums_kept", "decays", "history_turned", "history_kept",
        "channels", "channels_kept"))
    s_ld, s_hl, s_acst, s_dt = B.sem("head_values_loaded"), B.sem("history_loaded"), B.sem("decay_sum_stored"), B.tally("dt_step")
    with nc.Block() as block:
        @block.sync
        def _(sp):
            B.load_weights(sp, U0, par, w_in[:, :, COL_DT:COL_DT + NH], NH)
            with nc.allow_non_contiguous_dma("small per-head and per-channel values, once"):
                for n, name in enumerate(("dt_bias", "a_log", "d_skip")):
                    sp.dma_start(sm[:, n:n + 1], B.i[name].rearrange("o h -> h o")).then_inc(s_ld, 16)
                for j in range(CW):
                    sp.dma_start(B.cw[:, :, j], B.i["conv_w"][0, j].rearrange("(c p) -> p c", p=P)).then_inc(s_ld, 16)
                sp.dma_start(B.cw[:, :, CW], B.i["conv_b"][0].rearrange("(c p) -> p c", p=P)).then_inc(s_ld, 16)
                sp.dma_start(B.nw[:], B.i["ssm_norm"][0].rearrange("(c p) -> p c", p=P)).then_inc(s_ld, 16)
                sp.dma_start(B.dskip[:], B.i["d_skip"].to_broadcast([P, NH])).then_inc(s_ld, 16)
            sp.dma_start(expand[:].rearrange("h c p -> h (c p)"), B.i["expand"]).then_inc(s_ld, 16)
            sp.dma_start(hrow[:], B.i["state_conv"][0].rearrange("b j c -> (b j) c")).then_inc(s_hl, 16)
            sp.dma_start(B.o["conv_sample"][0, :, 0:CW - 2, :], B.i["state_conv"][0, :, 1:CW - 1, :]).then_inc(s_hl, 16)
            sp.wait_ge(s_sumc, 2)
            sp.dma_start(B.acs_scratch, acst[:]).then_inc(s_acst, 16)
            sp.wait_ge(s_acst, 16)
            sp.wait_ge(s_hl, 32)

        @block.gpsimd
        def _(pool):
            B.split_low(pool, U0, par, NH)

        @block.tensor
        def _(pe):
            B.multiply(pe, U0, par, B.hh, B.hl, NH)
            pe.wait_ge(s_ld, 16 * 11)
            pe.wait_ge(s_hl, 32)
            for n in range(8):
                if n >= 2:
                    pe.wait_ge(s_hc, n - 1)
                for j in range(4):
                    ins = nc.tensor.transpose(B.psum[:, 6 + n % 2, j * 24:(j + 1) * 24], hrow[:, (4 * n + j) * P:(4 * n + j + 1) * P],
                                              B.ident[0:24, 0:24])
                ins.then_inc(s_h, 1)
            pe.wait_ge(s_act, 3)
            for n in range(NBLK):
                nc.tensor.transpose(B.psum[:, 3, n * NH:(n + 1) * NH], dtt[:, n * P:(n + 1) * P], B.ident[0:NH, 0:NH])
                ins = nc.tensor.transpose(B.psum[:, 4, n * NH:(n + 1) * NH], dta[:, n * P:(n + 1) * P], B.ident[0:NH, 0:NH])
            ins.then_inc(s_t, 1)
            pe.wait_ge(s_rows, 2)
            nc.tensor.matmul(B.psum[:, 5, 0:HC], B.upto[:], dar[:], start=True, stop=True)
            nc.tensor.matmul(B.psum[:, 0, 0:HC], B.ones[:], dar[:], start=True, stop=True)
            for n in range(NBLK):
                ins = nc.tensor.matmul(B.psum[0:NH, 1 + n // 4, (n % 4) * P:(n % 4 + 1) * P], dar[:, n * NH:(n + 1) * NH],
                                       B.upto[:], start=True, stop=True)
            ins.then_inc(s_sums, 1)
            pe.wait_ge(s_chc, 1)
            for c in range(16):
                ins = nc.tensor.matmul(B.psum[:, 3, c * 17:c * 17 + 17], expand[:, c, :], srhs[:], start=True, stop=True)
            ins.then_inc(s_ch, 1)

        @block.scalar
        def _(act):
            B.split_high(act, U0, par, NH)
            act.wait_ge(s_ld, 16 * 11)
            for t in range(NT):
                B.await_tile(act, U0, t)
                nc.scalar.activation(raw[:, tcols(t)], B.tile(par, t, NH), ACT.Identity, bias=sm[:, 0:1]).then_inc(B.s_tile_free, 1)
            act.wait_ge(B.s_tile_free, 6 + 3 * (U0 + 1))
            s_soft = B.sem("softplus_step")
            nc.scalar.activation(dtt[:], raw[:], ACT.Abs).then_inc(s_soft, 1)
            act.wait_ge(s_soft, 1)
            nc.scalar.activation(dtt[:], dtt[:], ACT.Exp, scale=-1.0).then_inc(s_soft, 1)
            nc.scalar.activation(sm[:, 3:4], sm[:, 1:2], ACT.Exp).then_inc(s_soft, 1)
            act.wait_ge(s_soft, 3)
            nc.scalar.activation(dtt[:], dtt[:], ACT.Ln, bias=B.ones[0:NH, 0:1]).then_inc(s_raw, 1)
            act.wait_ge(s_sumc, 5)
            nc.scalar.activation(B.eacs[:], B.acs[:], ACT.Exp).then_inc(s_exp, 1)
            nc.scalar.activation(B.etot[:], tot[:], ACT.Exp).then_inc(s_exp, 1)
            nc.scalar.activation(B.dend[:], B.dend[:], ACT.Exp).then_inc(s_exp, 1)
            act.wait_ge(s_chc, 2)
            nc.scalar.activation(B.chs[:, :, NS:2 * NS], B.chs[:, :, NS:2 * NS], ACT.Exp).then_inc(s_exp, 1)

        @block.vector
        def _(dve):
            for n in range(8):
                dve.wait_ge(s_h, n + 1)
                nc.vector.tensor_copy(B.hist[:, 4 * n:4 * n + 4, :], B.psum[:, 6 + n % 2, 0:96].rearrange("p (j c) -> p j c", j=4)).then_inc(s_hc, 1)
            dve.wait_ge(s_raw, 1)
            done(dve, nc.vector.scalar_tensor_tensor(out=dtt[:], in0=raw[:], scalar=0.0, in1=dtt[:], op0=ALU.max, op1=ALU.add), s_dt)
            done(dve, nc.vector.tensor_scalar(dta[:], dtt[:], sm[:, 3:4], -1.0, ALU.mult, ALU.mult), s_dt)
            nc.vector.tensor_copy(srhs[:, 0:NS], dtt[:, SEQ:TOK]).then_inc(s_act, 1)
            nc.vector.tensor_copy(srhs[:, NS:2 * NS], dta[:, SEQ:TOK]).then_inc(s_act, 1)
            nc.vector.tensor_copy(srhs[:, 2 * NS:2 * NS + 1], sm[:, 2:3]).then_inc(s_act, 1)
            dve.wait_ge(s_act, 3)
            dve.sem_inc(s_chc, 1)
            dve.wait_ge(s_t, 1)
            nc.vector.tensor_copy(B.dt[:], B.psum[:, 3, 0:HC]).then_inc(s_rows, 1)
            nc.vector.tensor_copy(dar[:], B.psum[:, 4, 0:HC]).then_inc(s_rows, 1)
            dve.wait_ge(s_sums, 1)
            nc.vector.tensor_copy(acst[:, 0:512], B.psum[0:NH, 1, :]).then_inc(s_sumc, 1)
            nc.vector.tensor_copy(acst[:, 512:1024], B.psum[0:NH, 2, :]).then_inc(s_sumc, 1)
            nc.vector.tensor_copy(B.acs[:], B.psum[:, 5, 0:HC]).then_inc(s_sumc, 1)
            nc.vector.tensor_copy(tot[:], B.psum[:, 0, 0:HC]).then_inc(s_sumc, 1)
            dve.wait_ge(s_sumc, 4)
            nc.vector.tensor_tensor(B.dend[:], tot[:], B.acs[:], ALU.subtract).then_inc(s_sumc, 1)
            dve.wait_ge(s_ch, 1)
            nc.vector.tensor_copy(B.chs[:].rearrange("p c n -> p (c n)"), B.psum[:, 3, 0:16 * 17]).then_inc(s_chc, 1)
            dve.wait_ge(s_exp, 3)
            done(dve, nc.vector.tensor_tensor(B.dend[:], B.dend[:], B.dt[:], ALU.mult), s_dt)
    B.unit += 1
    B.top = mark


def mamba_groups(B):
    nc = B.nc
    mark = B.top
    PAD = CW - 1
    pre = B.take("conv_in_sb", [P, 4, PAD + TOK])
    post = B.take("conv_out_sb", [P, 4, TOK])
    z = B.take("z_sb", [P, 2, TOK])
    bc = B.take("decay_sum_spread_sb", [P, HPG, SEQ])
    acc = B.take("conv_sum_sb", [P, 2, TOK])
    tmp = acc[:].rearrange("p s c -> p (s c)")[:, 0:2048].rearrange("p (c b n) -> p c b n", c=2, b=NS)
    rows = B.take("x_b_rows_sb", [P, 2, 384])
    xdt = B.take("x_dt_sb", [P, 2, 256])
    xdec = B.take("x_decayed_sb", [P, 2, 256])
    xd = B.take("x_d_sb", [P, 2, 256])
    cbm = B.take("cb_masked_sb", [P, 2, P])
    state = B.take("scan_state_sb", [P, 2, 256])
    ste = B.take("scan_state_decayed_sb", [P, 256])
    yb = B.take("y_sb", [P, 256])
    gz = B.take("gated_rows_sb", [P, NBLK, 256])
    ss = B.take("square_sums_sb", [P, NBLK])
    st = B.take("sample_ssm_state_sb", [P, NS, 2, P])
    dg = B.take("diagonals_sb", [P, NS, P])
    gst = B.take("gated_sb", [P, 2, TOK])
    sml = B.take("sample_small_sb", [P, 8, 16])
    cst = gz[0:PAD + NS, 0:2, :].rearrange("p n (j c) -> p (n j) c", j=2)
    sst = xd[:, 0, :].rearrange("p (c n) -> p c n", c=2)
    B.g_scratch = nc.dram_tensor("gated_scratch", (16, P, TOK), F32, kind="Internal").ap()
    U0 = B.unit
    par = lambda e: (U0 + e) % 2
    w_in = B.i["w_in_odd"][0].rearrange("(k p) n -> p k n", p=P)
    w_pair = lambda c0: w_in[:, :, c0:c0 + G * 256].rearrange("p k (g e m) -> e g p k m", e=2, m=P)
    w_one = lambda c0: w_in[:, :, c0:c0 + G * P].rearrange("p k (g m) -> g p k m", m=P)
    w_of = [w_pair(COL_X)[0], w_pair(COL_X)[1], w_one(COL_B), w_one(COL_C), w_pair(COL_Z)[0], w_pair(COL_Z)[1]]
    names = ("conv_sum", "conv_out", "chunk_turned", "chunk_y", "chunk_state_sum", "rows_copied", "differences",
             "exps", "cb_masked", "scores", "x_dt", "x_decayed", "x_d", "state_decayed", "state", "y_parts", "gated",
             "square_sums", "rstd", "gated_scaled", "gated_turned", "gated_stored_col", "diagonal", "spread", "outer",
             "sample_state", "sample_gated", "sample_sum", "conv_rows_turned", "conv_rows_kept", "state_turned",
             "state_rows", "pad_set", "sample_scaled", "sample_decayed", "sample_mean", "column_half")
    S = {n: B.sem(n) for n in names}
    s_bc, s_st, s_sto = B.sem("spread_loaded"), B.sem("sample_ssm_loaded"), B.sem("sample_ssm_stored")
    s_gout, s_cout, s_sout = B.sem("gated_stored"), B.sem("conv_rows_stored"), B.sem("state_stored")
    s_dv = B.tally("vector_step")
    SLOT = {0: [0], 1: [1], 2: [2], 4: [3], 5: [4], 7: [5], 8: [6], 9: [7], 11: [8]}

    def unit(g, e):
        return g * 6 + (U0 + e)

    def await_group(eng, sem, g, per, n):
        eng.wait_ge(sem, g * per + n)

    def head_cols(a, g, n):
        return a[:, bass.ds(g * HPG + n * NH, HPG)]

    def rounds(eng, part, *tallies):
        part(None, 0)
        if tallies:
            with counted(eng, G - 1, *tallies) as g:
                part(g, g + 1)
        else:
            with eng.Fori(0, G - 1) as g:
                part(g, g + 1)
        part(G - 1, None)

    with nc.Block() as block:
        @block.sync
        def _(sp):
            def part(g, nx):
                if g is not None:
                    sp.wait_ge(S["chunk_y"], g * NBLK)
                    B.hold(sp)
                    sp.dma_start(bc[:], bass.AP(tensor=B.acs_scratch.tensor, offset=g * (HPG * SEQ),
                                                ap=[[0, P], [SEQ, HPG], [1, SEQ]])).then_inc(s_bc, 16)
                    sp.wait_ge(s_sto, g * (16 * NS))
                    sp.wait_ge(S["sample_gated"], g)
                    B.hold(sp)
                    for b in range(NS):
                        sp.dma_start(st[:, b], B.i["state_ssm"][0, b].rearrange("(g c two) q n -> g (two q) c n", g=G, two=2)
                                     [bass.ds(g, 1)].rearrange("o p c n -> p (o c) n")).then_inc(s_st, 16)
                if nx is not None:
                    for e in range(6):
                        B.load_weights(sp, unit(nx, e), par(e),
                                       w_of[e][bass.ds(nx, 1)].rearrange("o p k m -> p (o k) m"), held=True)
            rounds(sp, part)

        @block.gpsimd
        def _(pool):
            def out_states(g):
                pool.wait_ge(S["sample_state"], g + 1)
                B.hold(pool)
                for b in range(NS):
                    pool.dma_start(B.o["ssm_sample"][0, b].rearrange("(g c two) q n -> g (two q) c n", g=G, two=2)
                                   [bass.ds(g, 1)].rearrange("o p c n -> p (o c) n"), st[:, b]).then_inc(s_sto, 16)

            def store_conv_rows(g):
                pool.wait_ge(S["conv_rows_kept"], g + 1)
                B.hold(pool)
                for j0, n, c0, w in ((0, 2, g * 256, 256), (2, 1, g * P + D_INNER, P), (3, 1, g * P + (D_INNER + G * NST), P)):
                    src = cst[:, j0:j0 + n, :].rearrange("p j c -> p (j c)")
                    pool.dma_start(B.o["conv_prompt"][0, 0][:, bass.ds(c0, w)], src[0:PAD]).then_inc(s_cout, 16)
                    pool.dma_start(B.o["conv_sample"][0, :, CW - 2, :][:, bass.ds(c0, w)], src[PAD:PAD + NS]).then_inc(s_cout, 16)

            def finish(g):
                pool.wait_ge(S["state_rows"], g + 1)
                B.hold(pool)
                pool.dma_start(B.o["ssm_prompt"][0, 0].rearrange("(g c two) q n -> g (two q) c n", g=G, two=2)
                               [bass.ds(g, 1)].rearrange("o p c n -> p (o c) n"), sst).then_inc(s_sout, 16)
                pool.wait_ge(S["gated_stored_col"], g * 8 + 8)
                pool.wait_ge(S["sample_scaled"], g + 1)
                B.hold(pool)
                pool.dma_start(B.g_scratch.rearrange("(g e) p c -> g p e c", e=2)[bass.ds(g, 1)].rearrange("o p e c -> p (o e) c"),
                               gst[:]).then_inc(s_gout, 16)

            def part(g, nx):
                splits = [] if nx is None else list(range(4))
                if g is not None:
                    pool.wait_ge(S["conv_out"], g * 4 + 4)
                    pool.wait_ge(S["sample_gated"], g)
                    nc.gpsimd.tensor_tensor(dg[:], B.ident[:].unsqueeze(1).to_broadcast([P, NS, P]),
                                            post[:, 2, SEQ:TOK].unsqueeze(2).to_broadcast([P, NS, P]), ALU.mult).then_inc(S["diagonal"], 1)
                for k in range(9):
                    if splits and k % 2 == 0:
                        e = splits.pop(0)
                        B.split_low(pool, unit(nx, e), par(e))
                    if g is None:
                        continue
                    if k == 0:
                        store_conv_rows(g)
                    if k < NBLK:
                        n = k
                        await_group(pool, S["rows_copied"], g, NBLK, n + 1)
                        await_group(pool, S["square_sums"], g, NBLK, max(n - 1, 0))
                        if n == 0:
                            pool.wait_ge(s_sout, g * 16)
                        B.hold(pool)
                        nc.gpsimd.tensor_tensor(xd[:, n % 2, :].rearrange("p (h q) -> p h q", h=HPG),
                                                rows[:, n % 2, 0:256].rearrange("p (h q) -> p h q", h=HPG),
                                                B.dskip[:, bass.ds(g * HPG, HPG)].unsqueeze(2).to_broadcast([P, HPG, PS]),
                                                ALU.mult).then_inc(S["x_d"], 1)
                        nc.gpsimd.tensor_tensor(xdec[:, n % 2, :].rearrange("p (h q) -> p h q", h=HPG),
                                                rows[:, n % 2, 0:256].rearrange("p (h q) -> p h q", h=HPG),
                                                head_cols(B.dend, g, n).unsqueeze(2).to_broadcast([P, HPG, PS]),
                                                ALU.mult).then_inc(S["x_decayed"], 1)
                        if n >= 1:
                            await_group(pool, S["state"], g, NBLK, n)
                            B.hold(pool)
                            nc.gpsimd.tensor_tensor(ste[:].rearrange("p (h q) -> p h q", h=HPG),
                                                    state[:, (n - 1) % 2, :].rearrange("p (h q) -> p h q", h=HPG),
                                                    head_cols(B.etot, g, n).unsqueeze(2).to_broadcast([P, HPG, PS]),
                                                    ALU.mult).then_inc(S["state_decayed"], 1)
                    if k == 1:
                        pool.wait_ge(s_st, g * (16 * NS) + 16 * NS)
                        B.hold(pool)
                        nc.gpsimd.tensor_tensor(st[:], st[:], B.chs[:, bass.ds(g * 2, 2), NS:2 * NS].rearrange("p c b -> p b c")
                                                .unsqueeze(3).to_broadcast([P, NS, 2, P]), ALU.mult).then_inc(S["sample_decayed"], 1)
                    if k == 3:
                        pool.wait_ge(S["outer"], g + 1)
                        pool.wait_ge(S["sample_decayed"], g + 1)
                        nc.gpsimd.tensor_tensor(dg[:], B.ident[:].unsqueeze(1).to_broadcast([P, NS, P]),
                                                post[:, 3, SEQ:TOK].unsqueeze(2).to_broadcast([P, NS, P]), ALU.mult).then_inc(S["diagonal"], 1)
                        nc.gpsimd.tensor_tensor(st[:], st[:], tmp.rearrange("p c b n -> p b c n"), ALU.add).then_inc(S["sample_state"], 1)
                    if k == 4:
                        out_states(g)
                if splits:
                    raise AssertionError(splits)
                for e in ((4, 5) if nx is not None else ()):
                    B.split_low(pool, unit(nx, e), par(e))
                if g is not None:
                    finish(g)
            rounds(pool, part)
            pool.wait_ge(s_sto, 16 * NS * G)
            pool.wait_ge(s_gout, 16 * G)
            pool.wait_ge(s_sout, 16 * G)
            pool.wait_ge(s_cout, 16 * 6 * G)

        @block.tensor
        def _(pe):
            def tile(nx, e, t):
                u = unit(nx, e)
                if t == 0:
                    pe.wait_ge(B.s_w_high, u + 1)
                    pe.wait_ge(B.s_w_low, u + 3)
                pe.wait_ge(B.s_tile_free, u * 3 + t + 4)
                m = 0
                for k in range(KT):
                    for w, a in ((B.wh, B.hh), (B.wh, B.hl), (B.wl, B.hh)):
                        ins = nc.tensor.matmul(B.psum[:, t, 0:TT], w[:, par(e), k, :], a[:, k, tcols(t)], start=m == 0,
                                               stop=m == 3 * KT - 1)
                        m += 1
                ins.then_inc(B.s_tile, 1)

            def turn(g, n):
                if n == 0:
                    pe.wait_ge(S["conv_out"], g * 4 + 4)
                    pe.wait_ge(S["gated_stored_col"], g * 8)
                await_group(pe, S["rows_copied"], g, NBLK, n)
                await_group(pe, S["cb_masked"], g, NBLK, n)
                c = slice(n * P, (n + 1) * P)
                for j in range(3):
                    nc.tensor.transpose(B.psum[:, 3, j * P:(j + 1) * P], post[:, j, c], B.ident[:])
                nc.tensor.matmul(B.psum[:, 3, 384:512], post[:, 2, c], post[:, 3, c], start=True, stop=True).then_inc(S["chunk_turned"], 1)

            def scan(g, n):
                if n == 0:
                    pe.wait_ge(B.s_tile_free, unit(g, 5) * 3 + 9)
                    pe.wait_ge(S["conv_rows_kept"], g + 1)
                await_group(pe, S["scores"], g, NBLK, n + 1)
                await_group(pe, S["gated"], g, NBLK, n)
                await_group(pe, S["state"], g, NBLK, n)
                c = slice(n * P, (n + 1) * P)
                for j in range(2):
                    nc.tensor.transpose(B.psum[:, 5, 256 + j * P:256 + (j + 1) * P], z[:, j, c], B.ident[:])
                for h in range(HPG):
                    ins = nc.tensor.matmul(B.psum[:, 4, h * PS:(h + 1) * PS], bc[:, h, c], xdt[:, n % 2, h * PS:(h + 1) * PS],
                                           start=True, stop=True)
                if n >= 1:
                    ins = nc.tensor.matmul(B.psum[:, 4, 256:512], post[:, 3, c], state[:, (n - 1) % 2, :], start=True, stop=True)
                ins.then_inc(S["chunk_y"], 1)
                await_group(pe, S["x_decayed"], g, NBLK, n + 1)
                nc.tensor.matmul(B.psum[:, 5, 0:256], rows[:, n % 2, 256:384], xdec[:, n % 2, :], start=True,
                                 stop=True).then_inc(S["chunk_state_sum"], 1)

            def spread(g, m):
                await_group(pe, S["diagonal"], g, 2, m + 1)
                if m == 0:
                    pe.wait_ge(S["state_rows"], g)
                    pe.wait_ge(S["sample_scaled"], g)
                for a in range(2):
                    ins = nc.tensor.matmul(B.psum[:, 6 + a, :], B.ones[:],
                                           dg[:, 4 * a:4 * a + 4, :].rearrange("p b n -> p (b n)"), start=True, stop=True)
                ins.then_inc(S["spread"], 1)

            def slot(g, k):
                if k < NBLK:
                    turn(g, k)
                if k >= 1:
                    scan(g, k - 1)
                if k == 2:
                    spread(g, 0)
                if k == 5:
                    spread(g, 1)

            def sample_sum(g):
                pe.wait_ge(S["sample_gated"], g + 1)
                nc.tensor.matmul(B.psum[:, 6, 0:16], B.ones[:], sml[:, 3, :], start=True, stop=True).then_inc(S["sample_sum"], 1)

            def finish(g, n):
                pe.wait_ge(S["gated_scaled"], g * 8 + n + 1)
                if n >= 2:
                    pe.wait_ge(S["gated_stored_col"], g * 8 + n - 1)
                for j in range(2):
                    ins = nc.tensor.transpose(B.psum[:, 3 + n % 2, j * P:(j + 1) * P], gz[:, n, j * P:(j + 1) * P], B.ident[:])
                ins.then_inc(S["gated_turned"], 1)

            def part(g, nx):
                for i in range(12):
                    if nx is not None:
                        tile(nx, i // 3, i % 3)
                    if g is not None:
                        for k in SLOT.get(i, []):
                            slot(g, k)
                if nx is not None:
                    tile(nx, 4, 0)
                if g is not None:
                    sample_sum(g)
                    await_group(pe, S["state"], g, NBLK, NBLK)
                    for j in range(2):
                        ins = nc.tensor.transpose(B.psum[:, 7, j * P:(j + 1) * P], state[:, (NBLK - 1) % 2, j * P:(j + 1) * P], B.ident[:])
                    ins.then_inc(S["state_turned"], 1)
                    pe.wait_ge(S["gated"], g * 8 + 8)
                for i in range(5):
                    if nx is not None:
                        tile(nx, 4 + (i + 1) // 3, (i + 1) % 3)
                    if g is not None:
                        for n in ((0, 1), (2, 3), (4, 5), (6, 7), ())[i]:
                            finish(g, n)
                if nx is not None:
                    pe.wait_ge(B.s_tile_free, unit(nx, 3) * 3 + 9)
                    if g is not None:
                        pe.wait_ge(S["chunk_state_sum"], g * 8 + 8)
                        pe.wait_ge(S["gated"], g * 8 + 8)
                        pe.wait_ge(S["state"], g * 8 + 8)
                    for j in range(4):
                        ins = nc.tensor.transpose(B.psum[0:PAD + NS, 5, j * P:(j + 1) * P], pre[:, j, SEQ:SEQ + PAD + NS], B.ident[:])
                    ins.then_inc(S["conv_rows_turned"], 1)
            rounds(pe, part)

        @block.scalar
        def _(act):
            def evacuate(nx, e, t):
                B.await_tile(act, unit(nx, e), t)
                ps = B.psum[:, t, 0:TT]
                if e < 4:
                    nc.scalar.copy(pre[:, e, PAD + t * TT:PAD + (t + 1) * TT], ps).then_inc(B.s_tile_free, 1)
                else:
                    nc.scalar.activation(z[:, e - 4, tcols(t)], ps, ACT.Silu).then_inc(B.s_tile_free, 1)

            def slot(g, k):
                if k < NBLK:
                    n = k
                    await_group(act, S["chunk_turned"], g, NBLK, n + 1)
                    await_group(act, S["cb_masked"], g, NBLK, n + 1)
                    if n >= 2:
                        await_group(act, S["chunk_state_sum"], g, NBLK, n - 1)
                        await_group(act, S["x_dt"], g, NBLK, n - 1)
                        await_group(act, S["x_decayed"], g, NBLK, n - 1)
                    nc.scalar.copy(rows[:, n % 2, :], B.psum[:, 3, 0:384]).then_inc(S["rows_copied"], 1)
                    await_group(act, S["differences"], g, NBLK, n + 1)
                    e = bc[:, :, n * P:(n + 1) * P]
                    nc.scalar.activation(e, e, ACT.Exp).then_inc(S["exps"], 1)
                if k >= 2:
                    square(g, k - 2)

            def square(g, n):
                await_group(act, S["gated"], g, NBLK, n + 1)
                nc.scalar.activation(xd[:, n % 2, :], gz[:, n, :], ACT.Square, accum_out=ss[:, n:n + 1]).then_inc(S["square_sums"], 1)

            def finish(g, n):
                act.wait_ge(S["gated_turned"], g * 8 + n + 1)
                B.hold(act)
                for e in range(2):
                    nc.scalar.activation(gst[:, e, n * P:(n + 1) * P], B.psum[:, 3 + n % 2, e * P:(e + 1) * P], ACT.Copy,
                                         scale=B.nw[:, bass.ds(g * 2 + e, 1)]).then_inc(
                        S["gated_stored_col"] if e == 1 else S["column_half"], 1)

            def silu(nx, j):
                act.wait_ge(S["conv_sum"], nx * 4 + j + 1)
                nc.scalar.activation(post[:, j, :], acc[:, j % 2, :], ACT.Silu).then_inc(S["conv_out"], 1)

            def part(g, nx):
                if nx is not None:
                    B.split_high(act, unit(nx, 0), par(0))
                    if g is not None:
                        act.wait_ge(S["conv_sum"], g * 4 + 4)
                        act.wait_ge(S["conv_rows_turned"], g + 1)
                for i in range(12):
                    if nx is not None:
                        if i % 3 == 0:
                            B.split_high(act, unit(nx, i // 3 + 1), par(i // 3 + 1))
                        evacuate(nx, i // 3, i % 3)
                    if g is not None:
                        for k in SLOT.get(i, []):
                            slot(g, k)
                if g is not None:
                    square(g, NBLK - 1)
                    act.wait_ge(S["square_sums"], g * 8 + 8)
                    nc.scalar.activation(ss[:], ss[:], ACT.Ln, bias=B.eps[:, 0:1], scale=1.0 / 256).then_inc(S["rstd"], 1)
                    act.wait_ge(S["rstd"], g * 4 + 1)
                    nc.scalar.activation(ss[:], ss[:], ACT.Exp, scale=-0.5).then_inc(S["rstd"], 1)
                    act.wait_ge(S["sample_mean"], g + 1)
                    nc.scalar.activation(sml[:, 4, 0:8], sml[:, 4, 0:8], ACT.Ln, bias=B.eps[:, 0:1], scale=1.0 / 256).then_inc(S["rstd"], 1)
                    act.wait_ge(S["rstd"], g * 4 + 3)
                    nc.scalar.activation(sml[:, 4, 0:8], sml[:, 4, 0:8], ACT.Exp, scale=-0.5).then_inc(S["rstd"], 1)
                    act.wait_ge(S["rstd"], g * 4 + 4)
                    act.wait_ge(s_gout, g * 16)
                    for n in range(NBLK):
                        nc.scalar.activation(gz[:, n, :], gz[:, n, :], ACT.Copy, scale=ss[:, n:n + 1]).then_inc(S["gated_scaled"], 1)
                if nx is not None:
                    if g is not None:
                        act.wait_ge(S["chunk_turned"], g * 8 + 8)
                        act.wait_ge(S["sample_gated"], g + 1)
                    silu(nx, 0)
                for i in range(6):
                    if nx is not None:
                        if i == 0:
                            B.split_high(act, unit(nx, 5), par(5))
                        evacuate(nx, 4 + i // 3, i % 3)
                    if g is not None and 1 <= i <= 4:
                        finish(g, 2 * i - 2)
                        finish(g, 2 * i - 1)
                    if nx is not None and i in (0, 3, 5):
                        if i == 3 and g is not None:
                            act.wait_ge(S["chunk_state_sum"], g * 8 + 8)
                        silu(nx, {0: 1, 3: 2, 5: 3}[i])
            rounds(act, part)

        @block.vector
        def _(dve):
            def step(ins):
                done(dve, ins, s_dv)

            def start(g, n):
                if n == 0:
                    dve.wait_ge(s_bc, g * 16 + 16)
                for h in range(HPG):
                    e = bc[:, h, n * P:(n + 1) * P]
                    ins = nc.vector.tensor_scalar(e, e, B.acs[:, bass.ds(g * HPG + (n * NH + h), 1)], 0.0, ALU.subtract, ALU.min)
                ins.then_inc(S["differences"], 1)

            def scores(g, n):
                await_group(dve, S["chunk_turned"], g, NBLK, n + 1)
                nc.vector.tensor_tensor(cbm[:, n % 2, :], B.psum[:, 3, 384:512], B.upto[:], ALU.mult).then_inc(S["cb_masked"], 1)
                await_group(dve, S["rows_copied"], g, NBLK, n + 1)
                nc.vector.tensor_tensor(xdt[:, n % 2, :].rearrange("p (h q) -> p h q", h=HPG),
                                        rows[:, n % 2, 0:256].rearrange("p (h q) -> p h q", h=HPG),
                                        head_cols(B.dt, g, n).unsqueeze(2).to_broadcast([P, HPG, PS]), ALU.mult).then_inc(S["x_dt"], 1)
                await_group(dve, S["exps"], g, NBLK, n + 1)
                await_group(dve, S["cb_masked"], g, NBLK, n + 1)
                e = bc[:, :, n * P:(n + 1) * P]
                await_group(dve, S["x_dt"], g, NBLK, n + 1)
                nc.vector.tensor_tensor(e, e, cbm[:, n % 2, :].unsqueeze(1).to_broadcast([P, HPG, P]), ALU.mult).then_inc(S["scores"], 1)

            def gate(g, n):
                await_group(dve, S["chunk_state_sum"], g, NBLK, n + 1)
                if n == 0:
                    dve.wait_ge(S["gated_turned"], g * 8)
                    dve.wait_ge(s_cout, g * 96 + 96)
                    nc.vector.tensor_copy(state[:, 0, :], B.psum[:, 5, 0:256]).then_inc(S["state"], 1)
                else:
                    await_group(dve, S["state_decayed"], g, NBLK - 1, n)
                    nc.vector.tensor_tensor(state[:, n % 2, :], ste[:], B.psum[:, 5, 0:256], ALU.add).then_inc(S["state"], 1)
                await_group(dve, S["x_d"], g, NBLK, n + 1)
                y = yb[:]
                x_d = xd[:, n % 2, :]
                step(nc.vector.tensor_tensor(x_d, x_d, B.psum[:, 4, 0:256], ALU.add))
                if n >= 1:
                    step(nc.vector.tensor_tensor(y.rearrange("p (h q) -> p h q", h=HPG),
                                                 B.psum[:, 4, 256:512].rearrange("p (h q) -> p h q", h=HPG),
                                                 head_cols(B.eacs, g, n).unsqueeze(2).to_broadcast([P, HPG, PS]), ALU.mult))
                    step(nc.vector.tensor_tensor(y, y, x_d, ALU.add))
                    x_d = y
                nc.vector.tensor_tensor(gz[:, n, :], x_d, B.psum[:, 5, 256:512], ALU.mult).then_inc(S["gated"], 1)
                await_group(dve, S["gated"], g, NBLK, n + 1)

            xs = post[:, 0:2, SEQ:TOK]
            small = lambda i: sml[:, i, :].rearrange("p (c b) -> p c b", c=2)

            def outer(g):
                dve.wait_ge(S["conv_out"], g * 4 + 4)
                step(nc.vector.tensor_tensor(small(0), xs, B.chs[:, bass.ds(g * 2, 2), 0:NS], ALU.mult))
                await_group(dve, S["spread"], g, 2, 1)
                for c in range(2):
                    ins = nc.vector.tensor_tensor(tmp[:, c], B.psum[:, 6:8, :].rearrange("p a (b n) -> p (a b) n", b=4),
                                                  small(0)[:, c, :].unsqueeze(2).to_broadcast([P, NS, P]), ALU.mult)
                ins.then_inc(S["outer"], 1)

            def sample_y(g):
                await_group(dve, S["spread"], g, 2, 2)
                dve.wait_ge(S["sample_state"], g + 1)
                for c in range(2):
                    step(nc.vector.tensor_tensor(tmp[:, c], B.psum[:, 6:8, :].rearrange("p a (b n) -> p (a b) n", b=4),
                                                 st[:, :, c, :], ALU.mult))
                step(nc.vector.tensor_reduce(small(1), tmp, AX_X, ALU.add))
                step(nc.vector.tensor_tensor(small(0), xs, B.chs[:, bass.ds(g * 2, 2), 2 * NS:2 * NS + 1].to_broadcast([P, 2, NS]), ALU.mult))
                step(nc.vector.tensor_tensor(small(1), small(1), small(0), ALU.add))
                step(nc.vector.tensor_tensor(small(2), small(1), z[:, :, SEQ:TOK], ALU.mult))
                nc.vector.tensor_tensor(small(3), small(2), small(2), ALU.mult).then_inc(S["sample_gated"], 1)

            def sample_norm(g):
                dve.wait_ge(S["sample_sum"], g + 1)
                step(nc.vector.tensor_copy(sml[:, 5, :], B.psum[:, 6, 0:16]))
                nc.vector.tensor_tensor(sml[:, 4, 0:8], sml[:, 5, 0:8], sml[:, 5, 8:16], ALU.add).then_inc(S["sample_mean"], 1)
                dve.wait_ge(S["rstd"], g * 4 + 4)
                step(nc.vector.tensor_tensor(small(2), small(2), sml[:, 4, 0:8].unsqueeze(1).to_broadcast([P, 2, NS]), ALU.mult))
                dve.wait_ge(s_gout, g * 16)
                nc.vector.tensor_tensor(gst[:, :, SEQ:TOK], small(2), B.nw[:, bass.ds(g * 2, 2)].unsqueeze(2)
                                        .to_broadcast([P, 2, NS]), ALU.mult).then_inc(S["sample_scaled"], 1)
                dve.wait_ge(S["state_turned"], g + 1)
                dve.wait_ge(s_sout, g * 16)
                nc.vector.tensor_copy(sst, B.psum[:, 7, 0:256].rearrange("p (c n) -> p c n", c=2)).then_inc(S["state_rows"], 1)

            def channel(nx, j):
                return (nx * 2, nx * 2 + 1, nx + 16, nx + 24)[j]

            def convolve(nx, j):
                dve.wait_ge(B.s_tile_free, unit(nx, j) * 3 + 9)
                w = lambda i: B.cw[:, bass.ds(channel(nx, j), 1), i]
                a, s = acc[:, j % 2, 0:SEQ], acc[:, j % 2, SEQ:TOK]
                if not (isinstance(nx, int) and j < 2):
                    dve.wait_ge(S["conv_out"], nx * 4 + j - 1)
                step(nc.vector.tensor_scalar(a, pre[:, j, PAD:PAD + SEQ], w(PAD), w(CW), ALU.mult, ALU.add))
                step(nc.vector.tensor_scalar(s, pre[:, j, PAD + SEQ:PAD + TOK], w(PAD), w(CW), ALU.mult, ALU.add))
                for i in range(PAD):
                    step(nc.vector.scalar_tensor_tensor(out=a, in0=pre[:, j, i:i + SEQ], scalar=w(i), in1=a,
                                                        op0=ALU.mult, op1=ALU.add))
                    h = B.hist[:, bass.ds(channel(nx, j), 1), :].rearrange("p o (b i) -> p i (o b)", i=PAD)[:, i]
                    ins = nc.vector.scalar_tensor_tensor(out=s, in0=h, scalar=w(i), in1=s, op0=ALU.mult, op1=ALU.add)
                    if i < PAD - 1:
                        step(ins)
                ins.then_inc(S["conv_sum"], 1)

            def part(g, nx):
                if g is not None:
                    start(g, 0)
                    for k in range(9):
                        if k < NBLK:
                            if k + 1 < NBLK:
                                start(g, k + 1)
                            scores(g, k)
                        if k >= 1:
                            gate(g, k - 1)
                        if k == 2:
                            outer(g)
                        if k == 5:
                            sample_y(g)
                        if k >= 7 and nx is not None:
                            convolve(nx, k - 7)
                if g is not None:
                    sample_norm(g)
                    dve.wait_ge(S["sample_gated"], g + 1)
                    dve.wait_ge(S["sample_state"], g + 1)
                if nx is not None:
                    for j in range(0 if g is None else 2, 4):
                        convolve(nx, j)
                    dve.wait_ge(S["conv_rows_turned"], nx + 1)
                    if g is not None:
                        dve.wait_ge(S["gated_turned"], g * 8 + 8)
                    nc.vector.tensor_copy(cst, B.psum[0:PAD + NS, 5, :].rearrange("p (j c) -> p j c", j=4)).then_inc(S["conv_rows_kept"], 1)
                    dve.wait_ge(S["conv_rows_kept"], nx + 1)

            nc.vector.memset(pre[:, :, 0:PAD], 0.0).then_inc(S["pad_set"], 1)
            dve.wait_ge(S["pad_set"], 1)
            first = s_dv.count
            part(None, 0)
            n_first = s_dv.count - first
            CONV = 4 * (2 + 3 + 2)
            SCAN = (NBLK - 1) * 3 + 1 + 1 + 6 + 2
            assert n_first == CONV, (n_first, CONV)
            with counted(dve, G - 1, (s_dv, CONV + SCAN)) as g:
                part(g, g + 1)
            part(G - 1, None)
    B.unit += 6 * G
    B.top = mark


def load_operand(B, half):
    nc = B.nc
    mark = B.top
    g = B.take("gated_half_sb", [P, KT, TOK])
    s_g, s_high, s_low = B.sem("gated_loaded"), B.sem("gated_high"), B.sem("gated_low")
    with nc.Block() as block:
        @block.sync
        def _(sp):
            sp.dma_start(g[:], B.g_scratch[half * KT:(half + 1) * KT].rearrange("k p c -> p k c")).then_inc(s_g, 16)

        @block.scalar
        def _(act):
            act.wait_ge(s_g, 16)
            for k in range(KT):
                nc.scalar.copy(B.hh[:, k, :], g[:, k, :]).then_inc(s_high, 1)

        @block.vector
        def _(dve):
            for k in range(KT):
                dve.wait_ge(s_high, k + 1)
                nc.vector.tensor_tensor(B.hl[:, k, :], g[:, k, :], B.hh[:, k, :].bitcast(F32), ALU.subtract).then_inc(s_low, 1)
    B.top = mark


SHAPES_OUT = [
    ("y_prompt", (1, SEQ, D_MODEL)), ("y_sample", (NS, 1, D_MODEL)),
    ("k_prompt", (1, 1, SEQ, HA, DH)), ("v_prompt", (1, 1, SEQ, HA, DH)), ("idx_k_prompt", (1, 1, SEQ, DH)),
    ("k_sample", (1, NS, 1, HA, DH)), ("v_sample", (1, NS, 1, HA, DH)), ("idx_k_sample", (1, NS, 1, DH)),
    ("ret_prompt", (1, 1, HR, DKR, DVR)), ("ret_sample", (1, NS, HR, DKR, DVR)),
    ("conv_prompt", (1, 1, CW - 1, CONV_DIM)), ("conv_sample", (1, NS, CW - 1, CONV_DIM)),
    ("ssm_prompt", (1, 1, NH, PS, NST)), ("ssm_sample", (1, NS, NH, PS, NST)),
]


def build(nc, ins, outs, stop=None):
    with ExitStack() as ctx:
        B = Build(nc, ctx, ins, outs, stop)
        load_inputs(B)
        B.x_scratch = nc.dram_tensor("x_scratch", (P, KT, TOK), F32, kind="Internal").ap()
        if stop != "mlp":
            x_top = B.top
            normalize(B, 0, keep=B.x_scratch)
            B.top = B.x_base
            indexer(B)
            project_and_choose(B)
            keys_and_values(B)
            if stop == "kv":
                return
            attend(B)
            B.top = B.even_top
            attend_samples(B)
            B.recycle()
            B.top = B.retention_base
            retention(B)
            B.top = x_top
            project_add(B, B.i["w_out_even"][0].rearrange("(k p) (c m) -> c p k m", p=P, m=P))
            if stop == "mix0":
                write_outputs(B)
                return
            normalize(B, 1)
            mlp(B, 0)
            normalize(B, 2, keep=B.x_scratch)
            B.top = B.x_base
            time_steps(B)
            mamba_groups(B)
            B.top = x_top
            w_out = B.i["w_out_odd"][0].rearrange("(g k p) (c m) -> g c p k m", k=KT, p=P, m=P)
            load_operand(B, 0)
            project_add(B, w_out[0])
            load_operand(B, 1)
            project_add(B, w_out[1], load_x=False)
            normalize(B, 3)
            mlp(B, 1)
            normalize(B, 4, final=True)
            write_outputs(B)
            return
        if stop == "mlp":
            normalize(B, 1)
            mlp(B, 0)
            normalize(B, 4, final=True)
            write_outputs(B)
            return


INPUTS = ["x_prompt", "x_sample", "cache_k", "cache_v", "cache_idx_k", "state_ret", "state_conv", "state_ssm",
          "page_table", "rel_bias", "norm_mix", "norm_mlp", "norm_final", "w_in_even", "w_out_even", "w_in_odd",
          "conv_w", "conv_b", "dt_bias", "a_log", "d_skip", "ssm_norm", "w_out_odd", "w_up", "w_down"]


def kernel(**inputs):
    import numpy as _np
    import concourse.bacc as _bacc
    from concourse import mybir as _mybir
    from concourse.bass_utils import run_bass_kernel_spmd as _run

    nc = _bacc.Bacc("TRN2", target_bir_lowering=False, num_devices=1)
    arrays = {f"in_{n}": _np.ascontiguousarray(inputs[n]) for n in INPUTS}
    arrays.update({f"const_{n}": a for n, a in shape_constants().items()})
    ins = {n.split("_", 1)[1]: nc.dram_tensor(n, a.shape, _mybir.dt.from_np(a.dtype), kind="ExternalInput").ap()
           for n, a in arrays.items()}
    outs = {n: nc.dram_tensor(f"out_{n}", s, F32, kind="ExternalOutput").ap() for n, s in SHAPES_OUT}
    build(nc, ins, outs)
    r = _run(nc, [arrays], core_ids=[0])
    return tuple(r.results[0][f"out_{n}"] for n, _ in SHAPES_OUT)
```

```python
from contextlib import ExitStack, contextmanager

import numpy as np

import concourse.bass as bass
from concourse import mybir

F32 = mybir.dt.float32
F32R = mybir.dt.float32r
I32 = mybir.dt.int32
ALU = mybir.AluOpType
ACT = mybir.ActivationFunctionType
AX_X = mybir.AxisListType.X

P = 128
D_MODEL = 1024
KT = D_MODEL // P
SEQ = 1024
NBLK = SEQ // P
NS = 8
TOK = SEQ + NS
TT = 344
NT = TOK // TT
PAGES = 8
NPOOL = 80
DH = 64
HA = 8
HIDX = 8
TOPK = 256
NB = 32
HR = 4
DKR = 64
DVR = 128
D_INNER = 2048
PS = 64
NH = 32
G = 8
HPG = NH // G
NST = 128
CW = 4
CONV_DIM = 4096
EPS = 1e-6
BIG = 1e30
TAKEN = -3e38
COL_Q, COL_K, COL_V, COL_IQ, COL_IK, COL_IW, COL_R = 0, 512, 1024, 1536, 2048, 2112, 2120
COL_Z, COL_X, COL_B, COL_C, COL_DT = 0, 2048, 4096, 5120, 6144


class Tally:

    def __init__(self, sem, count=0):
        self.sem, self.count, self.reg = sem, count, None

    def value(self):
        return self.count if self.reg is None else self.reg + self.count

    def up(self, ins, by=1):
        ins.then_inc(self.sem, by)
        self.count += by


def done(eng, ins, tally):
    tally.up(ins)
    eng.wait_ge(tally.sem, tally.value())


@contextmanager
def counted(eng, trips, *tallies):
    kept = [(t, t.count, t.reg) for t, _ in tallies]
    with eng.Fori(0, trips) as i:
        for t, n in tallies:
            t.reg = i * n if t.reg is None else t.reg + i * n
        yield i
    for (t, n), (_, c0, r0) in zip(tallies, kept):
        assert t.count - c0 == n, (t.count - c0, n)
        t.count, t.reg = c0 + n * trips, r0


def shape_constants():
    f = np.float32
    c = {}
    c["ident"] = np.eye(P, dtype=f)
    k = np.arange(P)
    c["future"] = (k[None, :] > k[:, None]).astype(f)
    c["upto"] = (k[:, None] <= k[None, :]).astype(f)
    def bucket(d):
        d = np.maximum(d, 0)
        ratio = np.log(np.maximum(d, 16).astype(f) / f(16)) / f(np.log(8.0))
        large = 16 + (ratio * f(16)).astype(np.int32)
        return np.where(d < 16, d, np.minimum(large, 31))
    x = np.arange(384)
    oh = np.zeros((NB, 384 + P + NS), f)
    oh[bucket(255 - x), x] += 1
    oh[bucket(P - k), 384 + k] += 1
    oh[bucket(0), 384 + P:] += 1
    oh[NB - 1, :] -= 1
    c["buckets"] = oh
    inv = (f(10000.0) ** (-np.arange(32, dtype=f) / f(32))).astype(f)
    pos = np.concatenate([np.arange(SEQ), np.full(NS, SEQ)]).astype(f)
    ang = (pos[None, :] * inv[:, None]).astype(f)
    cos, sin = np.cos(ang).astype(f), np.sin(ang).astype(f)
    c["cos"] = np.tile(cos, (4, 1))
    c["sin"] = np.concatenate([-sin, sin, -sin, sin], 0)
    lg = np.log(1.0 - np.exp2(-5.0 - np.arange(HR, dtype=np.float64)))
    n = np.arange(P)
    dec = np.where(n[None, :] >= n[:, None], np.exp((n[None, :] - n[:, None])[None] * lg[:, None, None]), 0.0)
    c["decay"] = np.ascontiguousarray(dec.transpose(1, 0, 2)).reshape(P, HR * P).astype(f)
    head = lambda pair: np.repeat([2 * pair, 2 * pair + 1], 64)
    c["qdecay"] = np.concatenate([np.exp((n[None, :] + 1) * lg[head(p)][:, None]) for p in range(2)], 1).astype(f)
    c["kdecay"] = np.exp((P - 1 - n)[:, None] * lg[None, :]).astype(f)
    c["sdecay"] = np.concatenate([np.exp(P * lg[head(p)])[:, None] for p in range(2)]
                                 + [np.exp(lg[head(p)])[:, None] for p in range(2)], 1).astype(f)
    pick = np.zeros((NS, NS, P), f)
    for b in range(NS):
        pick[b, b] = 1
    c["pick"] = pick.reshape(NS, NS * P)
    expand = np.zeros((NH, 16, P), f)
    for h in range(NH):
        expand[h, h // 2, (h % 2) * 64:(h % 2) * 64 + 64] = 1
    c["expand"] = expand.reshape(NH, 16 * P)
    return c


CONSTS = {k: v.shape for k, v in shape_constants().items()}


class Build:

    def __init__(self, nc, ctx, ins, outs):
        self.nc, self.ctx = nc, ctx
        self.i, self.o = ins, outs
        self.top = (nc.sbuf_base + 63) // 64 * 64
        self.end = nc.sbuf_top
        self.names = 0
        self.stage_sems = []
        self.psum = ctx.enter_context(nc.psum_tensor("psum", [P, 8, 512], F32))
        self.ident = self.take("ident_sb", [P, P])
        self.upto = self.take("upto_sb", [P, P])
        self.ones = self.take("ones_sb", [P, P])
        self.gains = self.take("gains_sb", [P, 5, KT])
        self.eps = self.take("eps_sb", [P, 1])
        self.x = None
        self.wf = self.take("w_loaded_sb", [P, 2, KT, P])
        self.wh = self.take("w_high_sb", [P, 2, KT, P], F32R)
        self.wl = self.take("w_low_sb", [P, 2, KT, P], F32R)
        self.hh = self.take("act_high_sb", [P, KT, TOK], F32R)
        self.hl = self.take("act_low_sb", [P, KT, TOK], F32R)
        self.s_w_loaded = [self.sem("w_loaded_even"), self.sem("w_loaded_odd")]
        self.s_w_high = self.sem("w_high")
        self.s_w_low = self.sem("w_low")
        self.s_tile = self.sem("tile_summed")
        self.s_tile_free = self.sem("tile_free")
        self.s_held = {e.engine: self.sem(f"held_{n}") for n, e in
                       (("sync", nc.sync), ("act", nc.scalar), ("pool", nc.gpsimd))}
        self.stage_sems = []
        self.unit = 0

    def sem(self, name):
        self.names += 1
        sem = self.nc.alloc_semaphore(name=f"{name}_{self.names}")
        self.stage_sems.append(sem)
        return sem

    def recycle(self):
        self.nc.clear_and_free_semaphores(self.stage_sems)
        self.stage_sems = []
        self.nc.all_engine_barrier()

    def hold(self, eng):
        eng.sem_inc(self.s_held[eng.engine], 1)

    def tally(self, name):
        return Tally(self.sem(name))

    def take(self, name, shape, dt=F32):
        n = 4
        for s in shape[1:]:
            n *= s
        self.names += 1
        t = self.nc.alloc_sbuf_tensor_at(f"{name}_{self.names}", shape, dt, offset=self.top)
        self.top += (n + 31) // 32 * 32
        assert self.top <= self.end, (name, self.top, self.end)
        return t

    def bank(self, n, rows=P, cols=512):
        return self.psum[0:rows, n, 0:cols]


    def load_weights(self, sp, u, par, src, width=P, held=False):
        sp.wait_ge(self.s_w_low, u + 1)
        if held:
            self.hold(sp)
        sp.dma_start(self.wf[:, par, :, 0:width], src).then_inc(self.s_w_loaded[par], 16)

    def split_high(self, act, u, par, width=P):
        act.wait_ge(self.s_w_loaded[par], u * 8 + (16 - 8 * par))
        act.wait_ge(self.s_tile, u * 3 + 3)
        self.nc.scalar.copy(self.wh[:, par, :, 0:width], self.wf[:, par, :, 0:width]).then_inc(self.s_w_high, 1)

    def split_low(self, pool, u, par, width=P):
        pool.wait_ge(self.s_w_high, u + 1)
        pool.wait_ge(self.s_tile, u * 3 + 3)
        self.nc.gpsimd.tensor_tensor(self.wl[:, par, :, 0:width], self.wf[:, par, :, 0:width],
                                     self.wh[:, par, :, 0:width].bitcast(F32), ALU.subtract).then_inc(self.s_w_low, 1)

    def multiply(self, pe, u, par, high, low, width=P, last_k=None):
        nc = self.nc
        pe.wait_ge(self.s_w_high, u + 1)
        pe.wait_ge(self.s_w_low, u + 3)
        for t in range(NT):
            out = self.psum[0:width, 3 * par + t, 0:TT]
            pe.wait_ge(self.s_tile_free, u * 3 + t + 1)
            n = 0
            cols = slice(t * TT, (t + 1) * TT)
            for k in range(KT):
                if k == KT - 1 and t == 0 and last_k is not None:
                    last_k()
                for w, a in ((self.wh, high), (self.wh, low), (self.wl, high)):
                    ins = nc.tensor.matmul(out, w[:, par, k, 0:width], a[:, k, cols],
                                           start=n == 0, stop=n == 3 * KT - 1)
                    n += 1
            ins.then_inc(self.s_tile, 1)

    def await_tile(self, eng, u, t):
        eng.wait_ge(self.s_tile, u * 3 + t + 7)

    def tile(self, par, t, rows=P):
        return self.psum[0:rows, 3 * par + t, 0:TT]


def tcols(t):
    return slice(t * TT, (t + 1) * TT)


def load_inputs(B):
    nc = B.nc
    mark = B.top
    B.x_base = B.top
    B.x = B.take("x_sb", [P, KT, TOK])
    x_end = B.top
    nat = B.take("x_rows_sb", [P, NBLK, D_MODEL])
    nats = B.take("x_sample_rows_sb", [NS, D_MODEL])
    s_const, s_rows = B.sem("const_loaded"), B.sem("rows_loaded")
    s_turned, s_kept = B.sem("block_turned"), B.sem("block_kept")
    s_set = B.sem("constants_set")
    with nc.Block() as block:
        @block.sync
        def _(sp):
            sp.dma_start(nat[:], B.i["x_prompt"].rearrange("o (n p) d -> p (o n) d", p=P)).then_inc(s_rows, 16)
            sp.dma_start(nats[:], B.i["x_sample"].rearrange("b o d -> (b o) d")).then_inc(s_rows, 16)
            sp.dma_start(B.ident[:], B.i["ident"]).then_inc(s_const, 16)
            sp.dma_start(B.upto[:], B.i["upto"]).then_inc(s_const, 16)
            with nc.allow_non_contiguous_dma("norm gains, once"):
                for n, g in enumerate((B.i["norm_mix"][0], B.i["norm_mlp"][0], B.i["norm_mix"][1],
                                       B.i["norm_mlp"][1], B.i["norm_final"])):
                    sp.dma_start(B.gains[:, n, :], g.rearrange("(k p) -> p k", p=P)).then_inc(s_const, 16)
            sp.wait_ge(s_const, 7 * 16)

        @block.gpsimd
        def _(pool):
            nc.gpsimd.memset(B.ones[:], 1.0).then_inc(s_set, 1)
            nc.gpsimd.memset(B.eps[:], EPS).then_inc(s_set, 1)

        @block.tensor
        def _(pe):
            pe.sem_inc(B.s_w_low, 2)
            pe.sem_inc(B.s_tile, 6)
            pe.sem_inc(B.s_tile_free, 6)
            pe.wait_ge(s_const, 7 * 16)
            pe.wait_ge(s_rows, 32)
            for n in range(2 * (NBLK + 1)):
                blk, half = n // 2, n % 2
                if n >= 4:
                    pe.wait_ge(s_kept, n - 3)
                rows = P if blk < NBLK else NS
                src = nat[:, blk, :] if blk < NBLK else nats[:]
                for j in range(4):
                    k = 4 * half + j
                    ins = nc.tensor.transpose(B.psum[:, n % 4, j * P:j * P + rows], src[:, k * P:(k + 1) * P],
                                              B.ident[0:rows, 0:rows])
                ins.then_inc(s_turned, 1)

        @block.vector
        def _(dve):
            for n in range(2 * (NBLK + 1)):
                blk, half = n // 2, n % 2
                rows = P if blk < NBLK else NS
                dve.wait_ge(s_turned, n + 1)
                nc.vector.tensor_copy(
                    B.x[:, 4 * half:4 * half + 4, blk * P:blk * P + rows],
                    B.psum[:, n % 4, :].rearrange("p (j c) -> p j c", j=4)[:, :, 0:rows]).then_inc(s_kept, 1)
    B.top = x_end
    return mark


def normalize_final(B, gain):
    nc = B.nc
    mark = B.top
    sq = B.take("square_sb", [P, 4, TOK])
    acc = B.take("square_pairs_sb", [P, 2, TOK])
    rstd = B.take("rstd_sb", [P, TOK])
    s_sq, s_pair, s_added, s_sum, s_rstd, s_x = (B.sem(n) for n in (
        "squared", "squares_paired", "pair_summed", "squares_summed", "rstd", "x_normed"))
    with nc.Block() as block:
        @block.scalar
        def _(act):
            for k in range(KT):
                if k >= 4:
                    act.wait_ge(s_pair, (k - 4) // 2 + 1)
                nc.scalar.activation(sq[:, k % 4, :], B.x[:, k, :], ACT.Square).then_inc(s_sq, 1)
            for t in range(NT):
                act.wait_ge(s_sum, t + 1)
                nc.scalar.activation(rstd[:, tcols(t)], B.psum[:, t, 0:TT], ACT.Ln, bias=B.eps[:, 0:1],
                                     scale=1.0 / D_MODEL).then_inc(s_rstd, 1)
            act.wait_ge(s_rstd, NT)
            nc.scalar.activation(rstd[:], rstd[:], ACT.Exp, scale=-0.5).then_inc(s_rstd, 1)

        @block.tensor
        def _(pe):
            for m in range(KT // 2):
                pe.wait_ge(s_pair, m + 1)
                for t in range(NT):
                    ins = nc.tensor.matmul(B.psum[:, t, 0:TT], B.ones[:], acc[:, m % 2, tcols(t)],
                                           start=m == 0, stop=m == KT // 2 - 1)
                    if m == KT // 2 - 1:
                        ins.then_inc(s_sum, 1)
                if m < KT // 2 - 1:
                    ins.then_inc(s_added, 1)

        @block.vector
        def _(dve):
            for m in range(KT // 2):
                dve.wait_ge(s_sq, 2 * m + 2)
                if m >= 2:
                    dve.wait_ge(s_added, m - 1)
                s = 2 * m % 4
                nc.vector.tensor_tensor(acc[:, m % 2, :], sq[:, s, :], sq[:, s + 1, :], ALU.add).then_inc(s_pair, 1)
            dve.wait_ge(s_rstd, NT + 1)
            for k in range(KT):
                nc.vector.scalar_tensor_tensor(out=B.x[:, k, :], in0=B.x[:, k, :], scalar=B.gains[:, gain, k:k + 1],
                                               in1=rstd[:], op0=ALU.mult, op1=ALU.mult).then_inc(s_x, 1)
    B.top = mark


class Norm:
    SLOTS = 4
    POOL_K = (0, 2, 4, 6)

    def __init__(self, B, gain, width=P, keep=None):
        self.B, self.gain, self.width, self.keep = B, gain, width, keep
        self.u, self.par = B.unit, B.unit % 2
        mark = B.top
        self.buf = B.take("squares_and_normed_sb", [P, self.SLOTS, TOK])
        self.acc = B.take("square_pairs_sb", [P, 2, TOK])
        self.rstd = B.take("rstd_sb", [P, TOK])
        B.top = mark
        (self.s_sq, self.s_pair, self.s_added, self.s_sum, self.s_rstd, self.s_tmp, self.s_high, self.s_low_pool,
         self.s_low_dve) = (B.sem(n) for n in ("squared", "squares_paired", "pair_summed", "squares_summed", "rstd",
                                               "normed", "normed_high", "normed_low_pool", "normed_low_vector"))
        if keep is not None:
            self.s_keep = B.sem("x_kept")

    def sums(self, t):
        return self.B.psum[:, 3 * (1 - self.par) + t, 0:TT]

    def await_low(self, eng, k):
        if k in self.POOL_K:
            eng.wait_ge(self.s_low_pool, self.POOL_K.index(k) + 1)
        else:
            eng.wait_ge(self.s_low_dve, k + 1 - sum(p <= k for p in self.POOL_K))

    def await_done(self, eng):
        eng.wait_ge(self.s_high, KT)
        self.await_low(eng, KT - 2)
        self.await_low(eng, KT - 1)
        if self.keep is not None:
            eng.wait_ge(self.s_keep, 16)

    def store_x(self, sp):
        sp.dma_start(self.keep, self.B.x[:]).then_inc(self.s_keep, 16)

    def act(self, act):
        B, nc = self.B, self.B.nc
        for k in range(KT):
            if k >= self.SLOTS:
                act.wait_ge(self.s_pair, (k - self.SLOTS) // 2 + 1)
            nc.scalar.activation(self.buf[:, k % self.SLOTS, :], B.x[:, k, :], ACT.Square).then_inc(self.s_sq, 1)
        B.split_high(act, self.u, self.par, self.width)
        for t in range(NT):
            act.wait_ge(self.s_sum, t + 1)
            nc.scalar.activation(self.rstd[:, tcols(t)], self.sums(t), ACT.Ln, bias=B.eps[:, 0:1],
                                 scale=1.0 / D_MODEL).then_inc(self.s_rstd, 1)
        act.wait_ge(self.s_rstd, NT)
        nc.scalar.activation(self.rstd[:], self.rstd[:], ACT.Exp, scale=-0.5).then_inc(self.s_rstd, 1)
        for k in range(KT):
            act.wait_ge(self.s_tmp, k + 1)
            nc.scalar.copy(B.hh[:, k, :], self.buf[:, k % self.SLOTS, :]).then_inc(self.s_high, 1)

    def pe(self, pe):
        B, nc = self.B, self.B.nc
        for m in range(KT // 2):
            pe.wait_ge(self.s_pair, m + 1)
            for t in range(NT):
                ins = nc.tensor.matmul(self.sums(t), B.ones[:], self.acc[:, m % 2, tcols(t)],
                                       start=m == 0, stop=m == KT // 2 - 1)
                if m == KT // 2 - 1:
                    ins.then_inc(self.s_sum, 1)
            if m < KT // 2 - 1:
                ins.then_inc(self.s_added, 1)
        self.multiply_first(pe)

    def multiply_first(self, pe):
        B, nc = self.B, self.B.nc
        pe.wait_ge(B.s_w_high, self.u + 1)
        pe.wait_ge(B.s_w_low, self.u + 3)
        pe.wait_ge(B.s_tile_free, self.u * 3 + NT)
        for k in range(KT):
            pe.wait_ge(self.s_high, k + 1)
            self.await_low(pe, k)
            for t in range(NT):
                out = B.psum[0:self.width, 3 * self.par + t, 0:TT]
                for n, (w, a) in enumerate(((B.wh, B.hh), (B.wh, B.hl), (B.wl, B.hh))):
                    ins = nc.tensor.matmul(out, w[:, self.par, k, 0:self.width], a[:, k, tcols(t)],
                                           start=k == 0 and n == 0, stop=k == KT - 1 and n == 2)
                if k == KT - 1:
                    ins.then_inc(B.s_tile, 1)

    def dve(self, dve):
        B, nc = self.B, self.B.nc
        for m in range(KT // 2):
            dve.wait_ge(self.s_sq, 2 * m + 2)
            if m >= 2:
                dve.wait_ge(self.s_added, m - 1)
            s = 2 * m % self.SLOTS
            nc.vector.tensor_tensor(self.acc[:, m % 2, :], self.buf[:, s, :], self.buf[:, s + 1, :], ALU.add).then_inc(self.s_pair, 1)
        dve.wait_ge(self.s_rstd, NT + 1)
        dve.wait_ge(self.s_pair, KT // 2)

        def low(k):
            dve.wait_ge(self.s_high, k + 1)
            nc.vector.tensor_tensor(B.hl[:, k, :], self.buf[:, k % self.SLOTS, :], B.hh[:, k, :].bitcast(F32),
                                    ALU.subtract).then_inc(self.s_low_dve, 1)

        for k in range(KT):
            if k >= self.SLOTS:
                self.await_low(dve, k - self.SLOTS)
            nc.vector.scalar_tensor_tensor(out=self.buf[:, k % self.SLOTS, :], in0=B.x[:, k, :],
                                           scalar=B.gains[:, self.gain, k:k + 1], in1=self.rstd[:],
                                           op0=ALU.mult, op1=ALU.mult).then_inc(self.s_tmp, 1)
            if k >= 1 and k - 1 not in self.POOL_K:
                low(k - 1)
        low(KT - 1)

    def pool(self, pool):
        B, nc = self.B, self.B.nc
        B.split_low(pool, self.u, self.par, self.width)
        for k in self.POOL_K:
            pool.wait_ge(self.s_high, k + 1)
            nc.gpsimd.tensor_tensor(B.hl[:, k, :], self.buf[:, k % self.SLOTS, :], B.hh[:, k, :].bitcast(F32),
                                    ALU.subtract).then_inc(self.s_low_pool, 1)


def mlp(B, layer, norm):
    nc = B.nc
    mark = B.top
    uh = B.take("hidden_high_sb", [P, KT, TOK], F32R)
    ul = B.take("hidden_low_sb", [P, KT, TOK], F32R)
    relu = B.take("relu_sb", [P, 2, TT])
    sq = B.take("relu_square_sb", [P, 2, TT])
    GROUPS = 4
    U0 = B.unit
    w_up = B.i["w_up"][layer].rearrange("(k p) (c m) -> c p k m", p=P, m=P)
    w_down = B.i["w_down"][layer].rearrange("(g k p) (c m) -> g c p k m", k=KT, p=P, m=P)
    s_relu, s_square, s_high, s_low, s_added = (B.sem("relu"), B.sem("squared"), B.sem("hidden_high"),
                                                B.sem("hidden_low"), B.sem("down_added"))

    def up_unit(g, j, e):
        return g * 16 + j * 2 + (U0 + e)

    with nc.Block() as block:
        @block.sync
        def _(sp):
            with sp.Fori(0, GROUPS) as g:
                with sp.Fori(0, 4) as j:
                    for e in range(2):
                        B.load_weights(sp, up_unit(g, j, e), (U0 + e) % 2,
                                       w_up[bass.ds(g * 8 + j * 2 + e, 1)].rearrange("o p k m -> p (o k) m"))
                wd = w_down[bass.ds(g, 1)].rearrange("o c p k m -> (o c) p k m")
                with sp.Fori(0, 4) as j:
                    for e in range(2):
                        B.load_weights(sp, up_unit(g, j, 8 + e), (U0 + e) % 2,
                                       wd[bass.ds(j * 2 + e, 1)].rearrange("o p k m -> p (o k) m"))

        @block.gpsimd
        def _(pool):
            norm.pool(pool)
            B.split_low(pool, U0 + 1, (U0 + 1) % 2)
            with pool.Fori(1, GROUPS * 8) as j:
                for e in range(2):
                    B.split_low(pool, j * 2 + (U0 + e), (U0 + e) % 2)

        @block.tensor
        def _(pe):
            def down(g):
                pe.wait_ge(s_low, g * 24 + 21)
                for e in range(2):
                    B.multiply(pe, up_unit(g, 0, 8 + e), (U0 + e) % 2, uh, ul,
                               last_k=(lambda: pe.wait_ge(s_low, g * 24 + 24)) if e == 0 else None)
                with pe.Fori(1, 4) as j:
                    for e in range(2):
                        B.multiply(pe, up_unit(g, j, 8 + e), (U0 + e) % 2, uh, ul)

            norm.pe(pe)
            B.multiply(pe, U0 + 1, (U0 + 1) % 2, B.hh, B.hl)
            with pe.Fori(1, 4) as j:
                for e in range(2):
                    B.multiply(pe, up_unit(0, j, e), (U0 + e) % 2, B.hh, B.hl)
            down(0)
            with pe.Fori(1, GROUPS) as g:
                with pe.Fori(0, 4) as j:
                    for e in range(2):
                        B.multiply(pe, up_unit(g, j, e), (U0 + e) % 2, B.hh, B.hl)
                down(g)

        @block.scalar
        def _(act):
            def high(u, e):
                B.split_high(act, u, (U0 + e) % 2)

            def group(g):
                with act.Fori(0, 4) as j:
                    for e in range(2):
                        high(up_unit(g, j, e + 1), e + 1)
                        for t in range(NT):
                            n = g * 24 + j * 6 + (3 * e + t)
                            s = (3 * e + t) % 2
                            act.wait_ge(s_relu, n + 1)
                            nc.scalar.activation(sq[:, s, :], relu[:, s, :], ACT.Square).then_inc(s_square, 1)
                            act.wait_ge(s_square, n + 1)
                            nc.scalar.copy(uh[:, bass.ds(j * 2 + e, 1), tcols(t)].rearrange("p o c -> p (o c)"),
                                           sq[:, s, :]).then_inc(s_high, 1)
                with act.Fori(0, 3) as j:
                    for e in range(2):
                        high(up_unit(g, j, 9 + e), e + 1)
                high(up_unit(g, 3, 9), 1)

            norm.act(act)
            group(0)
            with act.Fori(1, GROUPS) as g:
                high(up_unit(g, 0, 0), 0)
                group(g)

        @block.vector
        def _(dve):
            norm.dve(dve)
            with dve.Fori(0, GROUPS) as g:
                with dve.Fori(0, 4) as j:
                    for e in range(2):
                        for t in range(NT):
                            n = g * 24 + j * 6 + (3 * e + t)
                            s = (3 * e + t) % 2
                            B.await_tile(dve, up_unit(g, j, e), t)
                            nc.vector.tensor_scalar(relu[:, s, :], B.tile((U0 + e) % 2, t), 0.0, None,
                                                    ALU.max).then_inc(s_relu, 1)
                            dve.wait_ge(s_high, n + 1)
                            nc.vector.tensor_tensor(
                                ul[:, bass.ds(j * 2 + e, 1), tcols(t)].rearrange("p o c -> p (o c)"), sq[:, s, :],
                                uh[:, bass.ds(j * 2 + e, 1), tcols(t)].rearrange("p o c -> p (o c)").bitcast(F32),
                                ALU.subtract).then_inc(s_low, 1)
                            dve.wait_ge(s_low, n + 1)
                            dve.sem_inc(B.s_tile_free, 1)
                with dve.Fori(0, 4) as j:
                    for e in range(2):
                        for t in range(NT):
                            B.await_tile(dve, up_unit(g, j, 8 + e), t)
                            xs = B.x[:, bass.ds(j * 2 + e, 1), tcols(t)].rearrange("p o c -> p (o c)")
                            nc.vector.tensor_tensor(xs, xs, B.tile((U0 + e) % 2, t), ALU.add).then_inc(B.s_tile_free, 1)
    B.unit += GROUPS * 16
    B.top = mark


def write_outputs(B):
    nc = B.nc
    rows_sb = B.take("y_rows_sb", [P, 2, D_MODEL])
    s_turned, s_kept, s_out = (B.sem("row_block_turned"), B.sem("row_block_kept"),
                               [B.sem("y_stored_even"), B.sem("y_stored_odd")])
    with nc.Block() as block:
        @block.tensor
        def _(pe):
            for n in range(2 * (NBLK + 1)):
                blk, half = n // 2, n % 2
                rows = P if blk < NBLK else NS
                if n >= 4:
                    pe.wait_ge(s_kept, n - 3)
                for j in range(4):
                    ins = nc.tensor.transpose(B.psum[0:rows, n % 4, j * P:(j + 1) * P],
                                              B.x[:, 4 * half + j, blk * P:blk * P + rows], B.ident[:])
                ins.then_inc(s_turned, 1)

        @block.vector
        def _(dve):
            for n in range(2 * (NBLK + 1)):
                blk, half = n // 2, n % 2
                rows = P if blk < NBLK else NS
                dve.wait_ge(s_turned, n + 1)
                if blk >= 2:
                    dve.wait_ge(s_out[blk % 2], 16 * (blk // 2))
                nc.vector.tensor_copy(rows_sb[0:rows, blk % 2, half * 512:half * 512 + 512],
                                      B.psum[0:rows, n % 4, :]).then_inc(s_kept, 1)

        @block.sync
        def _(sp):
            for blk in range(NBLK + 1):
                sp.wait_ge(s_kept, 2 * blk + 2)
                if blk < NBLK:
                    sp.dma_start(B.o["y_prompt"][0, blk * P:(blk + 1) * P, :], rows_sb[:, blk % 2, :]).then_inc(s_out[blk % 2], 16)
                else:
                    sp.dma_start(B.o["y_sample"].rearrange("b o d -> (b o) d"), rows_sb[0:NS, blk % 2, :]).then_inc(s_out[blk % 2], 16)
            sp.wait_ge(s_out[0], 16 * 5)
            sp.wait_ge(s_out[1], 16 * 4)



EARLY = 4
LATE = NBLK - 1
ROUNDS = TOPK // 8


def score_offset(i):
    return sum((j + 1) * P for j in range(2, i))


SCORE_COLS = score_offset(NBLK)
KEYS_S = PAGES * P + 1


def choose_step(dve, tally, S, W, m8, step):
    if tally.count:
        dve.wait_ge(tally.sem, tally.value())
    source = S if step < 2 else W
    if step % 2 == 0:
        tally.up(dve.max(m8, source))
    else:
        tally.up(dve.match_replace(W, m8, source, TAKEN))


def mark_left(dve, tally, S, W):
    dve.wait_ge(tally.sem, tally.value())
    tally.up(dve.scalar_tensor_tensor(out=S, in0=W, scalar=1.0, in1=S, op0=ALU.mult, op1=ALU.is_equal))


def indexer(B, norm):
    nc = B.nc
    B.retention_base = B.top
    B.scores_s = B.take("sample_scores_sb", [NS, KEYS_S + 7])
    B.pages = B.take("page_table_sb", [1, NS * PAGES], I32)
    B.qkv_s = B.take("sample_qkv_rows_sb", [NS, 3, 512])
    B.bias_s = B.take("sample_bias_sb", [P, 2, HA])
    B.even_top = B.top
    B.future = B.take("future_sb", [P, P])
    B.scores = B.take("scores_sb", [P, SCORE_COLS])
    mark = B.top
    iq = B.take("index_q_sb", [P, 4, TOK])
    ikw = B.take("index_k_w_sb", [P, TOK])
    ik2 = B.take("index_k_again_sb", [P, TOK])
    ikn = B.take("index_k_rows_sb", [P, NBLK + 1, DH + HIDX])
    iwn = B.take("index_w_rows_sb", [P, NBLK, HIDX])
    relu = B.take("relu_scores_sb", [P, 2, 1024])
    best = B.take("best_sb", [P, EARLY - 2, 8])
    iqs = B.take("sample_index_q_sb", [DH, NS, HIDX])
    iws = B.take("sample_index_w_sb", [HIDX, NS, NS])
    pk = B.take("index_pages_sb", [P, NS * PAGES, DH])
    ikt = B.take("index_pages_turned_sb", [DH, 2, KEYS_S + 7])
    rs = B.take("sample_relu_sb", [HIDX, 2, KEYS_S + 7])
    U0 = B.unit
    w_in = B.i["w_in_even"][0].rearrange("(k p) n -> p k n", p=P)
    WSCALE = HIDX ** -0.5 * DH ** -0.5
    N = (NBLK - 2) * HIDX
    s_table, s_page, s_out = B.sem("page_table_loaded"), B.sem("index_page_loaded"), B.sem("index_k_stored")
    s_turned, s_rows, s_w = B.sem("index_k_turned"), B.sem("index_k_rows"), B.sem("index_w_scaled")
    s_dot, s_relu, s_add = B.sem("index_products"), B.sem("index_relu"), B.sem("index_added")
    s_fut = B.sem("future_loaded")
    s_small = B.tally("sample_index_ready")
    s_pt, s_pc, s_sdot, s_srelu, s_sacc, s_fin = (B.sem("pages_turned"), B.sem("pages_copied"), B.sem("sample_products"),
                                                  B.sem("sample_relu"), B.sem("sample_weighted"), B.sem("sample_scores"))
    TILES_DONE = 6 + 3 * (U0 + 5)
    with nc.Block() as block:
        @block.sync
        def _(sp):
            for e in range(5):
                c0, w = (COL_IQ + e * P, P) if e < 4 else (COL_IK, DH + HIDX)
                B.load_weights(sp, U0 + e, (U0 + e) % 2, w_in[:, :, c0:c0 + w], w)
                if e == 1:
                    norm.store_x(sp)
            norm.await_done(sp)
            sp.dma_start(B.future[:], B.i["future"]).then_inc(s_fut, 16)
            sp.dma_start(B.pages[:], B.i["page_table"].rearrange("(o b) n -> o (b n)", o=1)).then_inc(s_table, 16)
            sp.wait_ge(s_table, 16)
            with sp.Fori(0, NS * PAGES) as n:
                page = sp.value_load(B.pages[0:1, bass.ds(n, 1)], min_val=0, max_val=NPOOL - 1)
                sp.dma_start(pk[:, bass.ds(n, 1), :],
                             B.i["cache_idx_k"][0][bass.ds(page, 1)].rearrange("o p d -> p o d")).then_inc(s_page, 16)
            sp.wait_ge(s_rows, 3)
            sp.dma_start(B.o["idx_k_prompt"][0, 0].rearrange("(n p) d -> p n d", p=P), ikn[:, 0:NBLK, 0:DH]).then_inc(s_out, 16)
            sp.dma_start(B.o["idx_k_sample"][0].rearrange("b o d -> (b o) d"), ikn[0:NS, NBLK, 0:DH]).then_inc(s_out, 16)
            sp.wait_ge(s_out, 32)

        @block.gpsimd
        def _(pool):
            norm.pool(pool)
            for e in range(1, 5):
                B.split_low(pool, U0 + e, (U0 + e) % 2, P if e < 4 else DH + HIDX)
            norm.await_done(pool)
            nc.gpsimd.memset(iws[:], 0.0).then_inc(s_w, 1)

        @block.tensor
        def _(pe):
            norm.pe(pe)
            for e in range(1, 5):
                B.multiply(pe, U0 + e, (U0 + e) % 2, B.hh, B.hl, P if e < 4 else DH + HIDX)
            pe.wait_ge(B.s_tile_free, TILES_DONE)
            for n in range(NBLK + 1):
                w = P if n < NBLK else NS
                ins = nc.tensor.transpose(B.psum[0:w, n // 4, (n % 4) * P:(n % 4) * P + DH + HIDX],
                                          ikw[0:DH + HIDX, n * P:n * P + w], B.ident[0:DH + HIDX, 0:DH + HIDX])
                if n % 4 == 3 or n == NBLK:
                    ins.then_inc(s_turned, 1)
            pe.wait_ge(s_rows, 3)
            n = 0
            for i in range(2, NBLK):
                L = (i + 1) * P
                for h in range(HIDX):
                    if n >= 3:
                        pe.wait_ge(s_relu, n - 2)
                    r = slice(64 * (h % 2), 64 * (h % 2) + 64)
                    keys = ikw if h % 2 == 0 else ik2
                    for c in range(0, L, 512):
                        w = min(512, L - c)
                        ins = nc.tensor.matmul(B.psum[:, 2 * (n % 3) + c // 512, 0:w], iq[r, h // 2, i * P:(i + 1) * P],
                                               keys[r, c:c + w], start=True, stop=True)
                    ins.then_inc(s_dot, 1)
                    n += 1
            pe.wait_ge(s_relu, N)
            pe.wait_ge(s_small.sem, 4)
            pe.wait_ge(s_page, 16 * NS * PAGES)

            def turn_pages(b):
                if b >= 1:
                    pe.wait_ge(s_pc, 2 * b)
                for j in range(PAGES):
                    ins = nc.tensor.transpose(B.psum[0:DH, 6 + j // 4, (j % 4) * P:(j % 4 + 1) * P],
                                              pk[:, b * PAGES + j, :], B.ident[:])
                ins.then_inc(s_pt, 1)

            turn_pages(0)
            for b in range(NS):
                if b + 1 < NS:
                    turn_pages(b + 1)
                pe.wait_ge(s_pc, 2 * b + 2)
                if b >= 1:
                    pe.wait_ge(s_srelu, 2 * b)
                for bank, c, w in ((0, 0, 512), (1, 512, 512), (2, 1024, 1)):
                    ins = nc.tensor.matmul(B.psum[0:HIDX, bank, 0:w], iqs[:, b, :], ikt[:, b % 2, c:c + w],
                                           start=True, stop=True)
                ins.then_inc(s_sdot, 1)
                pe.wait_ge(s_srelu, 2 * b + 2)
                for bank, c, w in ((3, 0, 512), (4, 512, 512), (5, 1024, 1)):
                    ins = nc.tensor.matmul(B.psum[0:NS, bank, 0:w], iws[:, b, :], rs[:, b % 2, c:c + w],
                                           start=b == 0, stop=b == NS - 1)
                ins.then_inc(s_sacc, 1)

        @block.scalar
        def _(act):
            norm.act(act)
            for e in range(1, 5):
                B.split_high(act, U0 + e, (U0 + e) % 2, P if e < 4 else DH + HIDX)
                if e == 1:
                    norm.await_done(act)
                if e >= 1:
                    for t in range(NT):
                        B.await_tile(act, U0 + e - 1, t)
                        nc.scalar.copy(iq[:, e - 1, tcols(t)], B.tile((U0 + e - 1) % 2, t)).then_inc(B.s_tile_free, 1)
            for t in range(NT):
                B.await_tile(act, U0 + 4, t)
                nc.scalar.copy(ikw[0:DH + HIDX, tcols(t)], B.tile((U0 + 4) % 2, t, DH + HIDX)).then_inc(s_small.sem, 1)
                nc.scalar.copy(ik2[64:128, tcols(t)], B.tile((U0 + 4) % 2, t, DH)).then_inc(B.s_tile_free, 1)
            act.wait_ge(s_small.sem, 3)
            act.wait_ge(B.s_tile_free, TILES_DONE)
            s_small.count = 3
            for par in range(2):
                nc.scalar.copy(iqs[:].rearrange("p b (c two) -> p two c b", two=2)[:, par],
                               iq[64 * par:64 * par + 64, :, SEQ:TOK]).then_inc(s_w, 1)
            act.wait_ge(s_w, 3)
            nc.scalar.mul(iws[:].rearrange("h a b -> h (a b)")[:, 0:NS * NS:NS + 1], ikw[64:64 + HIDX, SEQ:TOK],
                          WSCALE).then_inc(s_small.sem, 1)
            n = 0
            for i in range(2, NBLK):
                L = (i + 1) * P
                for h in range(HIDX):
                    act.wait_ge(s_dot, n + 1)
                    if n >= 2:
                        act.wait_ge(s_add, n - 1)
                    nc.scalar.activation(relu[:, n % 2, 0:L],
                                         B.psum[:, 2 * (n % 3):2 * (n % 3) + 2, :].rearrange("p b c -> p (b c)")[:, 0:L],
                                         ACT.Relu).then_inc(s_relu, 1)
                    n += 1
            for b in range(NS):
                act.wait_ge(s_sdot, b + 1)
                if b >= 2:
                    act.wait_ge(s_sacc, b - 1)
                nc.scalar.activation(rs[:, b % 2, 0:1024], B.psum[0:HIDX, 0:2, :].rearrange("p b c -> p (b c)"),
                                     ACT.Relu).then_inc(s_srelu, 1)
                nc.scalar.activation(rs[:, b % 2, 1024:1025], B.psum[0:HIDX, 2, 0:1], ACT.Relu).then_inc(s_srelu, 1)

        @block.vector
        def _(dve):
            norm.dve(dve)
            norm.await_done(dve)
            for n in range(3):
                dve.wait_ge(s_turned, n + 1)
                if n < 2:
                    nc.vector.tensor_copy(ikn[:, 4 * n:4 * n + 4, :],
                                          B.psum[:, n, :].rearrange("p (j c) -> p j c", j=4)[:, :, 0:DH + HIDX]).then_inc(s_rows, 1)
                else:
                    nc.vector.tensor_copy(ikn[0:NS, NBLK, :], B.psum[0:NS, 2, 0:DH + HIDX]).then_inc(s_rows, 1)
            dve.wait_ge(s_rows, 2)
            s_iw = B.sem("index_w_rows")
            nc.vector.tensor_scalar(iwn[:], ikn[:, 0:NBLK, DH:DH + HIDX], WSCALE, None, ALU.mult).then_inc(s_iw, 1)
            dve.wait_ge(s_iw, 1)
            dve.wait_ge(s_fut, 16)
            n = 0
            s_diag = B.sem("diagonal_masked")
            for i in range(2, NBLK):
                L = (i + 1) * P
                S = B.scores[:, score_offset(i):score_offset(i) + L]
                for h in range(HIDX):
                    dve.wait_ge(s_relu, n + 1)
                    w = iwn[:, i, h:h + 1]
                    if h == 0:
                        nc.vector.tensor_scalar(S, relu[:, n % 2, 0:L], w, None, ALU.mult).then_inc(s_add, 1)
                    else:
                        dve.wait_ge(s_add, n)
                        nc.vector.scalar_tensor_tensor(out=S, in0=relu[:, n % 2, 0:L], scalar=w, in1=S,
                                                       op0=ALU.mult, op1=ALU.add).then_inc(s_add, 1)
                    n += 1
                dve.wait_ge(s_add, n)
                D = S[:, i * P:L]
                nc.vector.scalar_tensor_tensor(out=D, in0=B.future[:], scalar=-BIG, in1=D,
                                               op0=ALU.mult, op1=ALU.add).then_inc(s_diag, 1)
            s_choice = [B.tally(f"choosing_step_{i}") for i in range(2, EARLY)]
            spare = relu[:].rearrange("p s c -> p (s c)")

            def choice(i):
                o = score_offset(i)
                return B.scores[:, o:o + (i + 1) * P], spare[:, o:o + (i + 1) * P], best[:, i - 2, :]

            dve.wait_ge(s_diag, NBLK - 2)
            for b in range(NS):
                dve.wait_ge(s_pt, b + 1)
                if b >= 2:
                    dve.wait_ge(s_sdot, b - 1)
                nc.vector.tensor_copy(ikt[:, b % 2, 0:1024],
                                      B.psum[0:DH, 6:8, :].rearrange("p b c -> p (b c)")).then_inc(s_pc, 1)
                nc.vector.tensor_copy(ikt[:, b % 2, 1024:1025], ikw[0:DH, SEQ + b:SEQ + b + 1]).then_inc(s_pc, 1)
                for step in range(b * 2 * ROUNDS // NS, (b + 1) * 2 * ROUNDS // NS):
                    for i in range(2, EARLY):
                        choose_step(dve, s_choice[i - 2], *choice(i), step)
            for i in range(2, EARLY):
                mark_left(dve, s_choice[i - 2], *choice(i)[0:2])
            dve.wait_ge(s_sacc, NS)
            nc.vector.tensor_copy(B.scores_s[:, 0:1024], B.psum[0:NS, 3:5, :].rearrange("p b c -> p (b c)")).then_inc(s_fin, 1)
            nc.vector.tensor_copy(B.scores_s[:, 1024:1025], B.psum[0:NS, 5, 0:1]).then_inc(s_fin, 1)
    B.unit += 5
    B.top = mark


def project_and_choose(B):
    nc = B.nc
    B.qkv = B.take("qkv_sb", [P, 12, TOK])
    mark = B.top
    stage = B.take("stage_sb", [P, 2, TOK])
    left = B.take("scores_left_sb", [P, 1 + LATE - EARLY, KEYS_S + 7])
    best = B.take("best_sb", [P, 1 + LATE - EARLY, 8])
    U0 = B.unit
    par = lambda e: (U0 + e) % 2
    B.r_scratch = nc.dram_tensor("retention_scratch", (12, P, TOK), F32, kind="Internal").ap()
    w_in = B.i["w_in_even"][0].rearrange("(k p) n -> p k n", p=P)
    w_qkv = w_in[:, :, 0:12 * P].rearrange("p k (c m) -> c p k m", m=P)
    w_r = w_in[:, :, COL_R:COL_R + 12 * P].rearrange("p k (c m) -> c p k m", m=P)
    s_spill = [B.sem("unit_spilled_even"), B.sem("unit_spilled_odd")]
    s_step = [B.tally(f"choosing_step_{c}") for c in range(1 + LATE - EARLY)]
    s_round = B.sem("choosing_round")
    with nc.Block() as block:
        @block.sync
        def _(sp):
            for base, src in ((0, w_qkv), (12, w_r)):
                with sp.Fori(0, 6) as j:
                    for e in range(2):
                        B.load_weights(sp, j * 2 + (U0 + base + e), par(e),
                                       src[bass.ds(j * 2 + e, 1)].rearrange("o p k m -> p (o k) m"))

        @block.gpsimd
        def _(pool):
            with pool.Fori(0, 12) as j:
                for e in range(2):
                    B.split_low(pool, j * 2 + (U0 + e), par(e))

        @block.tensor
        def _(pe):
            with pe.Fori(0, 12) as j:
                for e in range(2):
                    B.multiply(pe, j * 2 + (U0 + e), par(e), B.hh, B.hl)

        @block.scalar
        def _(act):
            B.split_high(act, U0, par(0))
            with act.Fori(0, 6) as j:
                for e in range(2):
                    B.split_high(act, j * 2 + (U0 + e + 1), par(e + 1))
                    for t in range(NT):
                        B.await_tile(act, j * 2 + (U0 + e), t)
                        nc.scalar.copy(B.qkv[:, bass.ds(j * 2 + e, 1), tcols(t)].rearrange("p o c -> p (o c)"),
                                       B.tile(par(e), t)).then_inc(B.s_tile_free, 1)

            def spill(j, last=False):
                for e in range(2):
                    u = j * 2 + (U0 + 12 + e)
                    if not (last and e == 1):
                        B.split_high(act, u + 1, par(e + 1))
                    act.wait_ge(s_spill[e], j * 16 + 16)
                    for t in range(NT):
                        B.await_tile(act, u, t)
                        nc.scalar.copy(stage[:, e, tcols(t)], B.tile(par(e), t)).then_inc(B.s_tile_free, 1)
                    act.wait_ge(B.s_tile_free, u * 3 + 9)
                    act.dma_start(B.r_scratch[bass.ds(j * 2 + e, 1)].rearrange("o p c -> p (o c)"),
                                  stage[:, e, :]).then_inc(s_spill[e], 16)

            for e in range(2):
                act.sem_inc(s_spill[e], 16)
            with act.Fori(0, 5) as j:
                spill(j)
            spill(5, last=True)
            for e in range(2):
                act.wait_ge(s_spill[e], 16 * 7)

        @block.vector
        def _(dve):
            chains = [(B.scores_s[:, 0:KEYS_S], NS, KEYS_S)]
            chains += [(B.scores[:, score_offset(i):score_offset(i) + (i + 1) * P], P, (i + 1) * P) for i in range(EARLY, LATE)]

            def each(step):
                for c, (S, rows, L) in enumerate(chains):
                    step(s_step[c], S, left[0:rows, c, 0:L], best[0:rows, c, :])

            def step_of(n):
                return lambda tally, S, W, m8: choose_step(dve, tally, S, W, m8, n)

            def largest(tally, S, W, m8):
                dve.wait_ge(tally.sem, tally.value())
                dve.sem_inc(s_round, 1)
                tally.up(nc.vector.max(m8, W))

            def take(tally, S, W, m8):
                dve.wait_ge(tally.sem, tally.value())
                dve.sem_inc(s_round, 1)
                tally.up(nc.vector.match_replace(W, m8, W, TAKEN))

            each(step_of(0))
            each(step_of(1))
            with counted(dve, ROUNDS - 1, *((t, 2) for t in s_step)):
                each(largest)
                each(take)
            each(lambda tally, S, W, m8: mark_left(dve, tally, S, W))
    B.unit += 24
    B.top = mark


def keys_and_values(B):
    nc = B.nc
    B.vn = B.take("v_rows_sb", [P, NBLK, 512])
    B.bias = B.take("bias_sb", [P, HA, 2 * P])
    mark = B.top
    kn = B.take("k_rows_sb", [P, 2, 512])
    buckets = B.take("buckets_sb", [NB, 384 + P + NS])
    rel = B.take("rel_bias_sb", [NB, HA])
    line = B.take("bias_line_sb", [HA, 384])
    b_scratch = nc.dram_tensor("bias_scratch", (HA, 384), F32, kind="Internal").ap()
    b_rows = nc.dram_tensor("bias_rows_scratch", (P, HA, 384), F32, kind="Internal").ap()
    s_in, s_bias, s_biasc = B.sem("bias_loaded"), B.sem("bias_products"), B.sem("bias_copied")
    s_line, s_biast = B.sem("bias_line_stored"), B.sem("bias_tiles_loaded")
    s_turned, s_kept = B.sem("rows_turned"), B.sem("rows_kept")
    s_k, s_v = [B.sem("k_stored_even"), B.sem("k_stored_odd")], B.sem("v_stored")
    steps = [(0, NBLK)] + [(1, b) for b in range(NBLK + 1)] + [(2, b) for b in range(NBLK + 1)]
    with nc.Block() as block:
        @block.sync
        def _(sp):
            sp.dma_start(buckets[:], B.i["buckets"]).then_inc(s_in, 16)
            sp.dma_start(rel[:], B.i["rel_bias"]).then_inc(s_in, 16)
            sp.wait_ge(s_biasc, 1)
            sp.dma_start(b_scratch, line[:]).then_inc(s_line, 16)
            sp.wait_ge(s_line, 16)
            sp.dma_start(b_rows, bass.AP(tensor=b_scratch.tensor, offset=0,
                                         ap=[[0, P], [384, HA], [1, 384]])).then_inc(s_line, 16)
            sp.wait_ge(s_line, 32)
            sp.dma_start(B.bias[:], bass.AP(tensor=b_rows.tensor, offset=P - 1,
                                            ap=[[HA * 384 - 1, P], [384, HA], [1, 2 * P]])).then_inc(s_biast, 16)
            for n, (part, b) in enumerate(steps):
                if part == 1 and b < NBLK:
                    sp.wait_ge(s_kept, n + 1)
                    sp.dma_start(B.o["k_prompt"][0, 0, b * P:(b + 1) * P].rearrange("p h d -> p (h d)"),
                                 kn[:, b % 2, :]).then_inc(s_k[b % 2], 16)
            sp.wait_ge(s_kept, len(steps))
            sp.dma_start(B.o["v_prompt"][0, 0].rearrange("(n p) h d -> p n (h d)", p=P), B.vn[:]).then_inc(s_v, 16)
            sp.dma_start(B.o["k_sample"][0].rearrange("b o h d -> (b o) (h d)"), B.qkv_s[:, 1, :]).then_inc(s_v, 16)
            sp.dma_start(B.o["v_sample"][0].rearrange("b o h d -> (b o) (h d)"), B.qkv_s[:, 2, :]).then_inc(s_v, 16)
            sp.wait_ge(s_v, 48)
            sp.wait_ge(s_biast, 16)
            for e in range(2):
                sp.wait_ge(s_k[e], 64)

        @block.tensor
        def _(pe):
            pe.wait_ge(s_in, 32)
            nc.tensor.matmul(B.psum[0:HA, 0, 0:384], rel[:], buckets[:, 0:384], start=True, stop=True)
            nc.tensor.matmul(B.psum[:, 1, 0:HA], buckets[:, 384:384 + P], rel[:], start=True, stop=True)
            nc.tensor.matmul(B.psum[0:NS, 2, 0:HA], buckets[:, 384 + P:384 + P + NS], rel[:], start=True,
                             stop=True).then_inc(s_bias, 1)
            for n, (part, b) in enumerate(steps):
                w = P if b < NBLK else NS
                if n >= 4:
                    pe.wait_ge(s_kept, n - 3)
                for j in range(4):
                    ins = nc.tensor.transpose(B.psum[0:w, 4 + n % 4, j * P:(j + 1) * P],
                                              B.qkv[:, 4 * part + j, b * P:b * P + w], B.ident[:])
                ins.then_inc(s_turned, 1)

        @block.vector
        def _(dve):
            dve.wait_ge(s_bias, 1)
            nc.vector.tensor_scalar(line[:], B.psum[0:HA, 0, 0:384], DH ** 0.5, None, ALU.mult).then_inc(s_biasc, 1)
            nc.vector.tensor_copy(B.bias_s[:, 0, :], B.psum[:, 1, 0:HA]).then_inc(s_biasc, 1)
            nc.vector.tensor_copy(B.bias_s[0:NS, 1, :], B.psum[0:NS, 2, 0:HA]).then_inc(s_biasc, 1)
            for n, (part, b) in enumerate(steps):
                dve.wait_ge(s_turned, n + 1)
                if b == NBLK:
                    out, rows = B.qkv_s[:, part, :], NS
                elif part == 1:
                    out, rows = kn[:, b % 2, :], P
                    if b >= 2:
                        dve.wait_ge(s_k[b % 2], 16 * (b // 2))
                else:
                    out, rows = B.vn[:, b, :], P
                nc.vector.tensor_copy(out, B.psum[0:rows, 4 + n % 4, :]).then_inc(s_kept, 1)
    B.top = mark


def attend(B):
    nc = B.nc
    mark = B.top
    spare = B.qkv[:, 8:12, :].rearrange("p k c -> p (k c)")
    logit = spare[:, 0:2048].rearrange("p (s c) -> p s c", s=2)
    pt = spare[:, 2048:4096].rearrange("p (s c) -> p s c", s=2)
    first = B.take("first_blocks_mask_sb", [P, 2 * P])
    near = B.take("near_mask_sb", [P, 2, 2 * P])
    mx = B.take("row_max_sb", [P, 2, 2])
    nm = B.take("minus_max_sb", [P, 2])
    total = B.take("prob_sum_sb", [P, 2, HA])
    rden = B.take("prob_sum_inverse_sb", [P, HA])
    o = B.take("att_rows_sb", [P, 512])
    left = B.take("scores_left_sb", [P, NBLK * P])
    best = B.take("best_sb", [P, 8])
    s_choice, s_chosen = B.tally("choosing_step"), B.sem("block_chosen")
    seq = [(i, h) for i in range(NBLK) for h in range(HA)]
    N = len(seq)
    (s_mask, s_near, s_dot, s_log, s_max, s_prob, s_turned, s_pt, s_pv, s_o, s_ot, s_hi, s_lo, s_far, s_rden) = (
        B.sem(x) for x in ("mask_scaled", "near_mask", "logit_products", "logits", "row_max", "probs", "probs_turned",
                           "probs_copied", "values_weighted", "att_rows", "att_turned", "att_high", "att_low",
                           "far_logits", "sum_inverse"))
    width = lambda i: (i + 1) * P

    def mask(i):
        if i == 0:
            return first[:, P:2 * P]
        if i == 1:
            return first[:]
        return B.scores[:, score_offset(i):score_offset(i) + width(i)]

    with nc.Block() as block:
        @block.gpsimd
        def _(pool):
            nc.gpsimd.memset(first[:, 0:P], 0.0).then_inc(s_mask, 1)
            nc.gpsimd.tensor_scalar(first[:, P:2 * P], B.future[:], -BIG, None, ALU.mult).then_inc(s_mask, 1)
            n = 0
            for i in range(NBLK):
                M, L = mask(i), width(i)
                if i >= 2:
                    if i >= LATE:
                        pool.wait_ge(s_chosen, i - LATE + 1)
                    nc.gpsimd.tensor_scalar(M, M, -BIG, None, ALU.mult).then_inc(s_mask, 1)
                pool.wait_ge(s_mask, max(2, i + 1))
                w = min(L, 2 * P)
                for h in range(HA):
                    if n >= 2:
                        pool.wait_ge(s_log, n - 1)
                    nc.gpsimd.tensor_tensor(near[:, n % 2, 0:w], M[:, L - w:L], B.bias[:, h, 2 * P - w:2 * P],
                                            ALU.add).then_inc(s_near, 1)
                    n += 1

        @block.tensor
        def _(pe):
            def dot(n):
                i, h = seq[n]
                L = width(i)
                if n >= 2:
                    pe.wait_ge(s_log, n - 1)
                r = slice(64 * (h % 2), 64 * (h % 2) + 64)
                for c in range(0, L, 512):
                    w = min(512, L - c)
                    ins = nc.tensor.matmul(B.psum[:, 2 * (n % 2) + c // 512, 0:w], B.qkv[r, h // 2, i * P:(i + 1) * P],
                                           B.qkv[r, 4 + h // 2, c:c + w], start=True, stop=True)
                ins.then_inc(s_dot, 1)

            def turn(n):
                i, h = seq[n]
                pe.wait_ge(s_prob, n + 1)
                if n >= 1:
                    pe.wait_ge(s_pt, n)
                for j in range(i + 1):
                    ins = nc.tensor.transpose(B.psum[:, 4 + j // 4, (j % 4) * P:(j % 4 + 1) * P],
                                              logit[:, n % 2, j * P:(j + 1) * P], B.ident[:])
                ins.then_inc(s_turned, 1)

            def weigh(n):
                i, h = seq[n]
                pe.wait_ge(s_pt, n + 1)
                if h == 0 and i >= 1:
                    pe.wait_ge(s_o, i)
                for j in range(i + 1):
                    ins = nc.tensor.matmul(B.psum[:, 6, h * DH:(h + 1) * DH], pt[:, n % 2, j * P:(j + 1) * P],
                                           B.vn[:, j, h * DH:(h + 1) * DH], start=j == 0, stop=j == i)
                ins.then_inc(s_pv, 1)

            def turn_rows(i):
                pe.wait_ge(s_o, i + 1)
                if i >= 1:
                    pe.wait_ge(s_lo, i)
                for j in range(4):
                    ins = nc.tensor.transpose(B.psum[:, 7, j * P:(j + 1) * P], o[:, j * P:(j + 1) * P], B.ident[:])
                ins.then_inc(s_ot, 1)

            dot(0)
            for n in range(N + 1):
                if n + 1 < N:
                    dot(n + 1)
                if n < N:
                    turn(n)
                if n >= 1:
                    weigh(n - 1)
                if n >= 1 and n % HA == 1 and n > 1:
                    turn_rows(n // HA - 1)
            turn_rows(NBLK - 1)

        @block.vector
        def _(dve):
            def logits(n):
                i, h = seq[n]
                L = width(i)
                w = min(L, 2 * P)
                far = L - w
                ps = B.psum[:, 2 * (n % 2):2 * (n % 2) + 2, :].rearrange("p b c -> p (b c)")
                dve.wait_ge(s_dot, n + 1)
                dve.wait_ge(s_near, n + 1)
                if n >= 2:
                    dve.wait_ge(s_turned, n - 1)
                    dve.wait_ge(s_prob, n - 1)
                start = TAKEN
                if far:
                    nc.vector.tensor_tensor_reduce(out=logit[:, n % 2, 0:far], in0=ps[:, 0:far], in1=mask(i)[:, 0:far],
                                                   scale=DH ** -0.5, scalar=TAKEN, op0=ALU.add, op1=ALU.max,
                                                   accum_out=mx[:, n % 2, 0:1]).then_inc(s_far, 1)
                    dve.wait_ge(s_far, n + 1 - 2 * HA)
                    start = mx[:, n % 2, 0:1]
                nc.vector.tensor_tensor_reduce(out=logit[:, n % 2, far:L], in0=ps[:, far:L], in1=near[:, n % 2, 0:w],
                                               scale=DH ** -0.5, scalar=start, op0=ALU.add, op1=ALU.max,
                                               accum_out=mx[:, n % 2, 1:2]).then_inc(s_log, 1)
                dve.wait_ge(s_log, n + 1)
                nc.vector.tensor_scalar(nm[:, n % 2:n % 2 + 1], mx[:, n % 2, 1:2], -1.0, None, ALU.mult).then_inc(s_max, 1)
                dve.wait_ge(s_max, n + 1)

            def rows(i):
                dve.wait_ge(s_pv, HA * (i + 1))
                dve.wait_ge(s_prob, HA * (i + 1))
                if i >= 1:
                    dve.wait_ge(s_ot, i)
                    dve.wait_ge(s_o, i)
                nc.vector.reciprocal(rden[:], total[:, i % 2, :]).then_inc(s_rden, 1)
                dve.wait_ge(s_rden, i + 1)
                nc.vector.tensor_tensor(o[:].rearrange("p (h d) -> p h d", h=HA),
                                        B.psum[:, 6, :].rearrange("p (h d) -> p h d", h=HA),
                                        rden[:].unsqueeze(2).to_broadcast([P, HA, DH]), ALU.mult).then_inc(s_o, 1)

            def low(i):
                dve.wait_ge(s_hi, i + 1)
                out = B.hl[:, 0:4, i * P:(i + 1) * P]
                nc.vector.tensor_tensor(out, B.psum[:, 7, :].rearrange("p (k c) -> p k c", k=4),
                                        B.hh[:, 0:4, i * P:(i + 1) * P].bitcast(F32), ALU.subtract).then_inc(s_lo, 1)

            def choose(step):
                i = LATE + step // (2 * ROUNDS)
                choose_step(dve, s_choice, mask(i), left[:, 0:width(i)], best[:], step % (2 * ROUNDS))
                if step % (2 * ROUNDS) == 2 * ROUNDS - 1:
                    mark_left(dve, s_choice, mask(i), left[:, 0:width(i)])
                    dve.wait_ge(s_choice.sem, s_choice.value())
                    dve.sem_inc(s_chosen, 1)

            steps, heads_work = 0, sum(width(i) for i, h in seq if i < NBLK - 1)
            all_steps = (NBLK - LATE) * ROUNDS * 2
            work = 0
            for n in range(N):
                logits(n)
                work += width(seq[n][0])
                while steps < all_steps and steps * heads_work < work * all_steps:
                    choose(steps)
                    steps += 1
                if n >= HA and n % HA == 1:
                    rows(n // HA - 1)
                if n >= HA and n % HA == 3:
                    low(n // HA - 1)
            rows(NBLK - 1)
            low(NBLK - 1)

        @block.scalar
        def _(act):
            def high(i):
                act.wait_ge(s_ot, i + 1)
                nc.scalar.copy(B.hh[:, 0:4, i * P:(i + 1) * P],
                               B.psum[:, 7, :].rearrange("p (k c) -> p k c", k=4)).then_inc(s_hi, 1)

            def copy_turned(n):
                i, h = seq[n]
                L = width(i)
                act.wait_ge(s_turned, n + 1)
                if n >= 2:
                    act.wait_ge(s_pv, n - 1)
                nc.scalar.copy(pt[:, n % 2, 0:L], B.psum[:, 4:6, :].rearrange("p b c -> p (b c)")[:, 0:L]).then_inc(s_pt, 1)

            for n in range(N):
                i, h = seq[n]
                L = width(i)
                act.wait_ge(s_max, n + 1)
                if h == 0 and i >= 2:
                    act.wait_ge(s_rden, i - 1)
                nc.scalar.activation(logit[:, n % 2, 0:L], logit[:, n % 2, 0:L], ACT.Exp, bias=nm[:, n % 2:n % 2 + 1],
                                     accum_out=total[:, i % 2, h:h + 1]).then_inc(s_prob, 1)
                if n >= 1:
                    copy_turned(n - 1)
                if n >= HA and n % HA == 2:
                    high(n // HA - 1)
            copy_turned(N - 1)
            high(NBLK - 1)
    B.top = mark


def attend_samples(B):
    nc = B.nc
    mark = B.top
    KS, VS = 3, 3
    kp = B.take("k_pages_sb", [P, KS, PAGES, 512])
    vp = B.take("v_pages_sb", [P, VS, PAGES, 512])
    pick = B.take("pick_sb", [NS, NS, P])
    maskt = B.take("sample_mask_sb", [P, PAGES, NS])
    logit = B.take("sample_logits_sb", [P, NS, PAGES, HA])
    own_prod = B.take("own_product_sb", [NS, 512])
    own = B.take("own_logit_sb", [NS, HA])
    owned = B.take("own_logit_diagonal_sb", [NS, NS, HA])
    pmax = B.take("page_max_sb", [P, NS * HA])
    hmax = B.take("head_max_sb", [NS * HA, 1])
    dmax = B.take("head_max_diagonal_sb", [NS * HA, NS * HA])
    pown = B.take("own_prob_sb", [P, NS * HA])
    pownd = B.take("own_prob_diagonal_sb", [NS, NS, HA])
    den = B.take("denominator_sb", [P, NS * HA])
    att = B.take("sample_att_sb", [P, 4, NS])
    kept = pick[:].rearrange("p (s b) c -> p s (b c)", s=2)
    s_kept, s_col = B.sem("own_columns_kept"), B.sem("columns_summed")
    s_k, s_v = [B.sem(f"k_pages_{b}") for b in range(NS)], [B.sem(f"v_pages_{b}") for b in range(NS)]
    s_pick = B.sem("pick_loaded")
    (s_mt, s_q, s_prod, s_dots, s_ob, s_mxt, s_mb, s_sub, s_exp, s_sum, s_pvd, s_fin, s_hi, s_owned, s_pmax,
     s_dmax, s_pownd) = (B.sem(x) for x in (
         "mask_turned", "q_spread", "k_times_q", "dots", "own_spread", "max_turned", "max_spread", "max_subtracted",
         "sample_probs", "probs_summed", "sample_values", "sample_att", "sample_att_high",
         "own_logits", "page_max", "max_diagonal", "own_probs_diagonal"))
    s_step = B.tally("sample_step")
    eye8 = B.ident[0:NS, 0:NS].unsqueeze(2).to_broadcast([NS, NS, HA])

    def load(eng, cache, place, b, sem):
        with eng.Fori(0, PAGES) as j:
            page = eng.value_load(B.pages[0:1, bass.ds(j + b * PAGES, 1)], min_val=0, max_val=NPOOL - 1)
            eng.dma_start(place[:, bass.ds(j, 1), :],
                          B.i[cache][0][bass.ds(page, 1)].rearrange("o p h d -> p o (h d)")).then_inc(sem, 16)

    def load_keys(eng, parity):
        for b in range(parity, NS, 2):
            if b >= KS:
                eng.wait_ge(s_dots, b - KS + 1)
            load(eng, "cache_k", kp[:, b % KS], b, s_k[b])

    def key_place(b):
        return (NS - KS + b - VS) % KS

    def v_place(b):
        return vp[:, b] if b < VS else kp[:, key_place(b)] if b < VS + KS else vp[:, b - VS - KS]

    with nc.Block() as block:
        @block.sync
        def _(sp):
            sp.dma_start(pick[:].rearrange("p b c -> p (b c)"), B.i["pick"]).then_inc(s_pick, 16)
            load_keys(sp, 0)

        @block.gpsimd
        def _(pool):
            load_keys(pool, 1)

        @block.tensor
        def _(pe):
            def to_columns(b):
                pe.wait_ge(s_kept, b + 1)
                for t in range(4):
                    ins = nc.tensor.matmul(B.psum[:, 7, b * 4 + t:b * 4 + t + 1], kept[:, b % 2, t * P:(t + 1) * P],
                                           B.ones[0:HA, 0:1], start=True, stop=True)
                ins.then_inc(s_col, 1)

            for j in range(PAGES):
                ins = nc.tensor.transpose(B.psum[:, 0, j * NS:(j + 1) * NS], B.scores_s[:, j * P:(j + 1) * P],
                                          B.ident[0:NS, 0:NS])
            ins.then_inc(s_mt, 1)
            pe.wait_ge(s_pick, 16)
            for b in range(NS):
                if b >= 2:
                    pe.wait_ge(s_prod, b - 1)
                nc.tensor.matmul(B.psum[:, 1 + b % 2, :], pick[:, b, :], B.qkv_s[:, 0, :], start=True, stop=True).then_inc(s_q, 1)
            pe.wait_ge(s_owned, 1)
            nc.tensor.matmul(B.psum[:, 3, 0:NS * HA], B.ones[0:NS, :], owned[:].rearrange("p b h -> p (b h)"),
                             start=True, stop=True).then_inc(s_ob, 1)
            pe.wait_ge(s_pmax, 2)
            nc.tensor.transpose(B.psum[0:NS * HA, 4, 0:P], pmax[:], B.ident[:]).then_inc(s_mxt, 1)
            pe.wait_ge(s_dmax, 1)
            nc.tensor.matmul(B.psum[:, 5, 0:NS * HA], B.ones[0:NS * HA, :], dmax[:], start=True, stop=True).then_inc(s_mb, 1)
            pe.wait_ge(s_exp, 2)
            nc.tensor.matmul(B.psum[:, 6, :], B.ones[:], logit[:].rearrange("p b g h -> p (b g h)"),
                             start=True, stop=True).then_inc(s_sum, 1)
            pe.wait_ge(s_pownd, 1)
            for b in range(NS):
                pe.wait_ge(s_v[b], 16 * PAGES)
                if b >= 2:
                    pe.wait_ge(s_kept, b - 1)
                out = B.psum[0:HA, 1 + b % 2, :]
                for j in range(PAGES):
                    nc.tensor.matmul(out, logit[:, b, j, :], v_place(b)[:, j, :], start=j == 0, stop=False)
                nc.tensor.matmul(out, pownd[:, b, :], B.qkv_s[:, 2, :], start=False, stop=True).then_inc(s_pvd, 1)
                if b >= 1:
                    to_columns(b - 1)
            to_columns(NS - 1)

        @block.vector
        def _(dve):
            def step(ins):
                done(dve, ins, s_step)

            dve.wait_ge(s_mt, 1)
            step(nc.vector.tensor_scalar(maskt[:].rearrange("p g b -> p (g b)"), B.psum[:, 0, 0:PAGES * NS], -BIG, None, ALU.mult))
            step(nc.vector.tensor_tensor(own_prod[:], B.qkv_s[:, 0, :], B.qkv_s[:, 1, :], ALU.mult))
            step(nc.vector.tensor_reduce(own[:], own_prod[:].rearrange("p (h d) -> p h d", h=HA), AX_X, ALU.add))
            step(nc.vector.scalar_tensor_tensor(out=own[:], in0=own[:], scalar=DH ** -0.5, in1=B.bias_s[0:NS, 1, :],
                                                op0=ALU.mult, op1=ALU.add))
            step(nc.vector.tensor_scalar(hmax[0:NS, :], B.scores_s[:, KEYS_S - 1:KEYS_S], -BIG, None, ALU.mult))
            step(nc.vector.tensor_scalar(own[:], own[:], hmax[0:NS, 0:1], None, ALU.add))
            nc.vector.tensor_tensor(owned[:], own[:].unsqueeze(1).to_broadcast([NS, NS, HA]), eye8,
                                    ALU.mult).then_inc(s_owned, 1)
            for b in range(NS):
                dve.wait_ge(s_k[b], 16 * PAGES)
                dve.wait_ge(s_q, b + 1)
                nc.vector.tensor_tensor(kp[:, b % KS], kp[:, b % KS],
                                        B.psum[:, 1 + b % 2, :].unsqueeze(1).to_broadcast([P, PAGES, 512]),
                                        ALU.mult).then_inc(s_prod, 1)
                dve.wait_ge(s_prod, b + 1)
                nc.vector.tensor_reduce(logit[:, b].rearrange("p g h -> p (g h)"),
                                        kp[:, b % KS].rearrange("p g (h d) -> p (g h) d", d=DH), AX_X, ALU.add).then_inc(s_dots, 1)
            dve.wait_ge(s_dots, NS)
            flat = logit[:].rearrange("p b g h -> p (b g h)")
            step(nc.vector.tensor_scalar(flat, flat, DH ** -0.5, None, ALU.mult))
            step(nc.vector.tensor_tensor(logit[:], logit[:],
                                         maskt[:].rearrange("p g b -> p b g").unsqueeze(3).to_broadcast([P, NS, PAGES, HA]), ALU.add))
            step(nc.vector.tensor_tensor(logit[:, :, PAGES - 1, :], logit[:, :, PAGES - 1, :],
                                         B.bias_s[:, 0, :].unsqueeze(1).to_broadcast([P, NS, HA]), ALU.add))
            nc.vector.tensor_reduce(pmax[:].rearrange("p (b h) -> p b h", b=NS),
                                    logit[:].rearrange("p b g h -> p b h g"), AX_X, ALU.max).then_inc(s_pmax, 1)
            dve.wait_ge(s_pmax, 1)
            dve.wait_ge(s_ob, 1)
            nc.vector.tensor_tensor(pmax[:], pmax[:], B.psum[:, 3, 0:NS * HA], ALU.max).then_inc(s_pmax, 1)
            dve.wait_ge(s_mxt, 1)
            step(nc.vector.tensor_reduce(hmax[:], B.psum[0:NS * HA, 4, 0:P], AX_X, ALU.max))
            nc.vector.tensor_scalar(dmax[:], B.ident[0:NS * HA, 0:NS * HA], hmax[:, 0:1], None, ALU.mult).then_inc(s_dmax, 1)
            dve.wait_ge(s_mb, 1)
            step(nc.vector.tensor_copy(den[:], B.psum[:, 5, 0:NS * HA]))
            nc.vector.tensor_tensor(logit[:], logit[:], den[:].rearrange("p (b h) -> p b h", b=NS).unsqueeze(2)
                                    .to_broadcast([P, NS, PAGES, HA]), ALU.subtract).then_inc(s_sub, 1)
            nc.vector.tensor_tensor(pown[:], B.psum[:, 3, 0:NS * HA], den[:], ALU.subtract).then_inc(s_sub, 1)
            dve.wait_ge(s_exp, 2)
            nc.vector.tensor_tensor(pownd[:], pown[0:NS, :].rearrange("p (b h) -> p b h", b=NS), eye8, ALU.mult).then_inc(s_pownd, 1)
            dve.wait_ge(s_sum, 1)
            dve.wait_ge(s_sub, 2)
            step(nc.vector.tensor_reduce(den[:].rearrange("p (b h) -> p b h", b=NS),
                                         B.psum[:, 6, :].rearrange("p (b g h) -> p b h g", b=NS, g=PAGES), AX_X, ALU.add))
            step(nc.vector.tensor_tensor(den[:], den[:], pown[:], ALU.add))
            step(nc.vector.reciprocal(den[:], den[:]))
            for b in range(NS):
                dve.wait_ge(s_pvd, b + 1)
                if b >= 2:
                    dve.wait_ge(s_col, b - 1)
                nc.vector.tensor_tensor(kept[:, b % 2, :].rearrange("h (g d) -> h g d", g=HA),
                                        B.psum[0:HA, 1 + b % 2, :].rearrange("h (g d) -> h g d", g=HA),
                                        B.ident[0:HA, 0:HA].unsqueeze(2).to_broadcast([HA, HA, DH]), ALU.mult).then_inc(s_kept, 1)
            dve.wait_ge(s_col, NS)
            for e in range(2):
                r = slice(64 * e, 64 * e + 64)
                nc.vector.tensor_tensor(
                    att[r, :, :], B.psum[r, 7, 0:NS * 4].rearrange("p (b t) -> p t b", b=NS),
                    den[r, :].rearrange("p (b t e) -> p e t b", b=NS, e=2)[:, e], ALU.mult).then_inc(s_fin, 1)
            dve.wait_ge(s_fin, 2)
            dve.wait_ge(s_hi, 1)
            step(nc.vector.tensor_tensor(B.hl[:, 0:4, SEQ:TOK], att[:], B.hh[:, 0:4, SEQ:TOK].bitcast(F32), ALU.subtract))

        @block.scalar
        def _(act):
            for b in range(VS + KS):
                act.wait_ge(s_dots, 2 * b + 1 if b < VS else NS - KS + 1 + b - VS)
                load(act, "cache_v", v_place(b), b, s_v[b])
            act.wait_ge(s_sub, 2)
            nc.scalar.activation(logit[:].rearrange("p b g h -> p (b g h)"), logit[:].rearrange("p b g h -> p (b g h)"),
                                 ACT.Exp).then_inc(s_exp, 1)
            nc.scalar.activation(pown[:], pown[:], ACT.Exp).then_inc(s_exp, 1)
            for b in range(VS + KS, NS):
                act.wait_ge(s_pvd, b - VS - KS + 1)
                load(act, "cache_v", v_place(b), b, s_v[b])
            act.wait_ge(s_fin, 2)
            nc.scalar.copy(B.hh[:, 0:4, SEQ:TOK], att[:]).then_inc(s_hi, 1)
    B.top = mark


def retention(B):
    nc = B.nc
    mark = B.top
    r = B.take("retention_parts_sb", [P, 12, TOK])
    o = B.take("retention_out_sb", [P, HR, TOK])
    sw = B.take("halves_swapped_sb", [P, 4, TOK])
    vrow = sw[:].rearrange("p k c -> p (k c)")[:, 0:4096].rearrange("p (n c) -> p n c", c=512)
    cs = B.take("cos_sin_sb", [P, 2, TOK])
    kdec = cs[:].rearrange("p k c -> p (k c)")[:, 0:2048].rearrange("p (n c) -> p n c", c=256)
    tab = B.take("retention_tables_sb", [P, HR * P + 2 * P + HR + 4])
    decay, qdecay = tab[:, 0:512].rearrange("p (h t) -> p h t", h=HR), tab[:, 512:768].rearrange("p (c t) -> p c t", c=2)
    kdecay, sdecay = tab[:, 768:772], tab[:, 772:776]
    srow = B.take("sample_kv_rows_sb", [NS, 256 + 512])
    scd = B.take("decayed_scores_sb", [P, 2, HR, P])
    by_parity = lambda a: a.rearrange("p (c two) t -> p two c t", two=2)
    pairs = lambda bank: B.psum[:, bank:bank + 2, 0:2 * P].rearrange("p two (c t) -> p two c t", c=2)
    state = B.take("retention_state_sb", [P, 2, 2, P])
    s_rest, s_keys = B.sem("values_gates_loaded"), B.sem("keys_rotated")
    s_load, s_tab = B.sem("parts_loaded"), B.sem("tables_loaded")
    s_swap, s_rot, s_sin, s_gate = B.sem("halves_swapped"), B.sem("rotated"), B.sem("sin_part"), B.sem("gates")
    s_turned, s_kept, s_qd = B.sem("kv_turned"), B.sem("kv_rows"), B.sem("q_decayed")
    s_sc, s_scd, s_o, s_okept, s_st, s_state = (B.sem(x) for x in (
        "chunk_scores", "chunk_scores_decayed", "chunk_out", "chunk_out_kept", "chunk_state", "state_updated"))
    s_out, s_kd = B.sem("prompt_state_stored"), B.sem("k_rows_decayed")
    qdb = B.take("q_decayed_sb", [P, 2, 2, P])
    with nc.Block() as block:
        @block.sync
        def _(sp):
            sp.dma_start(r[:, 0:4, :], B.r_scratch[0:4].rearrange("k p c -> p k c")).then_inc(s_load, 16)
            for dst, name in ((cs[:, 0, :], "cos"), (cs[:, 1, :], "sin"), (tab[:, 0:512], "decay"), (tab[:, 512:768], "qdecay"),
                              (kdecay, "kdecay"), (sdecay, "sdecay")):
                sp.dma_start(dst, B.i[name]).then_inc(s_tab, 16)
            sp.dma_start(r[:, 4:12, :], B.r_scratch[4:12].rearrange("k p c -> p k c")).then_inc(s_rest, 16)
            sp.wait_ge(s_state, 2 * NBLK)
            sp.dma_start(B.o["ret_prompt"][0, 0].rearrange("(c two) k v -> (two k) c v", two=2),
                         state[:, (NBLK - 1) % 2]).then_inc(s_out, 16)
            sp.wait_ge(s_out, 16)

        @block.scalar
        def _(act):
            for a in range(4):
                src = a ^ 1
                act.dma_start(sw[32 * a:32 * a + 32, :, :],
                              B.r_scratch[0:4, 32 * src:32 * src + 32].rearrange("k p c -> p k c")).then_inc(s_swap, 16)
            act.wait_ge(s_keys, 1)
            nc.scalar.mul(r[:, 2:4, :], r[:, 2:4, :], DKR ** -0.5).then_inc(s_keys, 1)
            act.wait_ge(s_rest, 16)
            nc.scalar.activation(r[:, 8:12, :], r[:, 8:12, :], ACT.Silu).then_inc(s_gate, 1)
            for n in range(NBLK + 1):
                act.wait_ge(s_turned, 2 * n + 1)
                if n < NBLK:
                    nc.scalar.copy(vrow[:, n, :], B.psum[:, 2 * (n % 2), :]).then_inc(s_kept, 1)
                else:
                    nc.scalar.copy(srow[:, 256:768], B.psum[0:NS, 2 * (n % 2), :]).then_inc(s_kept, 1)
                    act.wait_ge(s_turned, 2 * n + 2)
                    nc.scalar.copy(srow[:, 0:256], B.psum[0:NS, 2 * (n % 2) + 1, 0:256]).then_inc(s_kept, 1)
            for n in range(NBLK):
                act.wait_ge(s_o, n + 1)
                nc.scalar.copy(by_parity(o[:, :, n * P:(n + 1) * P]), pairs(2 + 2 * (n % 2))).then_inc(s_okept, 1)

        @block.gpsimd
        def _(pool):
            pool.wait_ge(s_tab, 16 * 6)
            pool.wait_ge(s_swap, 64)
            nc.gpsimd.tensor_tensor(sw[:, 2:4, :], sw[:, 2:4, :], cs[:, 1, :].unsqueeze(1).to_broadcast([P, 2, TOK]), ALU.mult).then_inc(s_sin, 1)
            for n in range(NBLK):
                if n == 0:
                    pool.wait_ge(s_rot, 3)
                if n >= 2:
                    pool.wait_ge(s_o, n - 1)
                nc.gpsimd.tensor_tensor(qdb[:, n % 2], r[:, 0:2, n * P:(n + 1) * P], qdecay, ALU.mult).then_inc(s_qd, 1)

        @block.vector
        def _(dve):
            dve.wait_ge(s_tab, 16 * 6)
            dve.wait_ge(s_load, 16)
            nc.vector.tensor_tensor(r[:, 0:4, :], r[:, 0:4, :], cs[:, 0, :].unsqueeze(1).to_broadcast([P, 4, TOK]),
                                    ALU.mult).then_inc(s_rot, 1)
            dve.wait_ge(s_swap, 64)
            nc.vector.tensor_tensor(sw[:, 0:2, :], sw[:, 0:2, :], cs[:, 1, :].unsqueeze(1).to_broadcast([P, 2, TOK]),
                                    ALU.mult).then_inc(s_rot, 1)
            dve.wait_ge(s_rot, 2)
            dve.wait_ge(s_sin, 1)
            nc.vector.tensor_tensor(r[:, 2:4, :], r[:, 2:4, :], sw[:, 2:4, :], ALU.add).then_inc(s_keys, 1)
            nc.vector.tensor_tensor(r[:, 0:2, :], r[:, 0:2, :], sw[:, 0:2, :], ALU.add).then_inc(s_rot, 1)
            dve.wait_ge(s_rot, 3)
            for n in range(NBLK):
                dve.wait_ge(s_turned, 2 * n + 2)
                nc.vector.tensor_tensor(kdec[:, n, :].rearrange("p (h d) -> p h d", h=HR),
                                        B.psum[:, 2 * (n % 2) + 1, 0:256].rearrange("p (h d) -> p h d", h=HR),
                                        kdecay.unsqueeze(2).to_broadcast([P, HR, DKR]), ALU.mult).then_inc(s_kd, 1)
            for n in range(NBLK):
                dve.wait_ge(s_sc, n + 1)
                if n >= 2:
                    dve.wait_ge(s_o, n - 1)
                nc.vector.tensor_tensor(by_parity(scd[:, n % 2]), pairs(0), by_parity(decay), ALU.mult).then_inc(s_scd, 1)
                dve.wait_ge(s_st, n + 1)
                for c in range(2):
                    ps = B.psum[:, 7, c * P:(c + 1) * P]
                    new = state[:, n % 2, c, :]
                    if n == 0:
                        nc.vector.tensor_copy(new, ps).then_inc(s_state, 1)
                    else:
                        dve.wait_ge(s_state, 2 * n)
                        nc.vector.scalar_tensor_tensor(out=new, in0=state[:, (n - 1) % 2, c, :], scalar=sdecay[:, c:c + 1],
                                                       in1=ps, op0=ALU.mult, op1=ALU.add).then_inc(s_state, 1)

        @block.tensor
        def _(pe):
            pe.wait_ge(s_keys, 2)
            pe.wait_ge(s_rest, 16)
            pe.wait_ge(s_rot, 3)
            for n in range(NBLK + 1):
                w = P if n < NBLK else NS
                if n >= 2:
                    pe.wait_ge(s_kept, n - 1)
                    pe.wait_ge(s_kd, n - 1)
                for j in range(4):
                    ins = nc.tensor.transpose(B.psum[0:w, 2 * (n % 2), j * P:(j + 1) * P], r[:, 4 + j, n * P:n * P + w], B.ident[:])
                ins.then_inc(s_turned, 1)
                for j in range(2):
                    ins = nc.tensor.transpose(B.psum[0:w, 2 * (n % 2) + 1, j * P:(j + 1) * P], r[:, 2 + j, n * P:n * P + w], B.ident[:])
                ins.then_inc(s_turned, 1)
            pe.wait_ge(s_kept, NBLK + 2)

            def scores(n):
                if n >= 1:
                    pe.wait_ge(s_scd, n)
                for h in range(HR):
                    q = slice(64 * (h % 2), 64 * (h % 2) + 64)
                    ins = nc.tensor.matmul(B.psum[:, h % 2, (h // 2) * P:(h // 2 + 1) * P], r[q, 2 + h // 2, n * P:(n + 1) * P],
                                           r[q, h // 2, n * P:(n + 1) * P], start=True, stop=True)
                ins.then_inc(s_sc, 1)

            for n in range(NBLK):
                scores(n)
                if n >= 1:
                    pe.wait_ge(s_state, 2 * n)
                for h in range(HR):
                    q = slice(64 * (h % 2), 64 * (h % 2) + 64)
                    ins = nc.tensor.matmul(B.psum[q, 7, (h // 2) * P:(h // 2 + 1) * P], kdec[:, n, h * DKR:(h + 1) * DKR],
                                           vrow[:, n, h * P:(h + 1) * P], start=True, stop=True)
                ins.then_inc(s_st, 1)
                pe.wait_ge(s_scd, n + 1)
                pe.wait_ge(s_qd, n + 1)
                if n >= 2:
                    pe.wait_ge(s_okept, n - 1)
                for h in range(HR):
                    q = slice(64 * (h % 2), 64 * (h % 2) + 64)
                    out = B.psum[:, 2 + 2 * (n % 2) + h % 2, (h // 2) * P:(h // 2 + 1) * P]
                    ins = nc.tensor.matmul(out, vrow[:, n, h * P:(h + 1) * P], scd[:, n % 2, h, :],
                                           start=True, stop=n == 0)
                    if n >= 1:
                        ins = nc.tensor.matmul(out, state[q, (n - 1) % 2, h // 2, :], qdb[q, n % 2, h // 2, :],
                                               start=False, stop=True)
                ins.then_inc(s_o, 1)

    flat = sw[:].rearrange("p k c -> p (k c)")
    st = flat[:, 0:2048].rearrange("p (b c v) -> p b c v", b=NS, c=2)
    kd = flat[0:NS, 2048:4096].rearrange("p (b n) -> p b n", b=NS)
    s_stl, s_sto = B.sem("sample_state_loaded"), B.sem("sample_state_stored")
    s_kd2, s_outer, s_new, s_os, s_ok = (B.sem(x) for x in ("sample_k_diagonal", "sample_outer", "sample_state_new",
                                                           "sample_out", "sample_out_kept"))
    with nc.Block() as block:
        @block.sync
        def _(sp):
            for b in range(NS):
                sp.dma_start(st[:, b], B.i["state_ret"][0, b].rearrange("(c two) k v -> (two k) c v", two=2)).then_inc(s_stl, 16)
            sp.wait_ge(s_new, 2)
            for b in range(NS):
                sp.dma_start(B.o["ret_sample"][0, b].rearrange("(c two) k v -> (two k) c v", two=2), st[:, b]).then_inc(s_sto, 16)
            sp.wait_ge(s_sto, 16 * NS)

        @block.vector
        def _(dve):
            nc.vector.tensor_tensor(kd, srow[:, 0:256].unsqueeze(1).to_broadcast([NS, NS, 256]),
                                    B.ident[0:NS, 0:NS].unsqueeze(2).to_broadcast([NS, NS, 256]), ALU.mult).then_inc(s_kd2, 1)
            dve.wait_ge(s_stl, 16 * NS)
            dve.wait_ge(s_outer, 1)
            for c in range(2):
                nc.vector.scalar_tensor_tensor(
                    out=st[:, :, c, :], in0=st[:, :, c, :], scalar=sdecay[:, 2 + c:3 + c],
                    in1=B.psum[:, 0:4, :].rearrange("p a (b c v) -> p c (a b) v", c=2, b=2)[:, c],
                    op0=ALU.mult, op1=ALU.add).then_inc(s_new, 1)
            dve.wait_ge(s_os, 1)
            nc.vector.tensor_copy(by_parity(o[:, :, SEQ:TOK]),
                                  B.psum[:, 4:6, 0:2 * NS].rearrange("p two (c b) -> p two c b", c=2)).then_inc(s_ok, 1)

        @block.tensor
        def _(pe):
            pe.wait_ge(s_kd2, 1)
            for b in range(NS):
                for h in range(HR):
                    q = slice(64 * (h % 2), 64 * (h % 2) + 64)
                    c0 = (b % 2) * 256 + (h // 2) * P
                    ins = nc.tensor.matmul(B.psum[q, b // 2, c0:c0 + P], kd[:, b, h * DKR:(h + 1) * DKR],
                                           srow[:, 256 + h * P:256 + (h + 1) * P], start=True, stop=True)
            ins.then_inc(s_outer, 1)
            pe.wait_ge(s_new, 2)
            for b in range(NS):
                for h in range(HR):
                    q = slice(64 * (h % 2), 64 * (h % 2) + 64)
                    ins = nc.tensor.matmul(B.psum[:, 4 + h % 2, (h // 2) * NS + b:(h // 2) * NS + b + 1], st[q, b, h // 2, :],
                                           r[q, h // 2, SEQ + b:SEQ + b + 1], start=True, stop=True)
            ins.then_inc(s_os, 1)

    oc = r[:, 0:4, :]
    sq = sw
    s_sum, s_oc, s_sq, s_sum2, s_rs, s_on, s_hi, s_lo = (B.sem(x) for x in (
        "head_summed", "centred", "centred_square", "square_summed", "inverse_deviation", "gated", "ret_high", "ret_low"))
    wide = lambda a: a.rearrange("p (t c) -> p t c", t=NT)
    with nc.Block() as block:
        @block.tensor
        def _(pe):
            def total(h):
                if h >= 1:
                    pe.wait_ge(s_oc, h)
                for t in range(NT):
                    ins = nc.tensor.matmul(B.psum[:, t, 0:TT], B.ones[:], o[:, h, tcols(t)], start=True, stop=True)
                ins.then_inc(s_sum, 1)

            total(0)
            for h in range(HR):
                if h + 1 < HR:
                    total(h + 1)
                pe.wait_ge(s_sq, h + 1)
                if h >= 1:
                    pe.wait_ge(s_rs, 2 * h - 1)
                for t in range(NT):
                    ins = nc.tensor.matmul(B.psum[:, 3 + t, 0:TT], B.ones[:], sq[:, h, tcols(t)], start=True, stop=True)
                ins.then_inc(s_sum2, 1)

        @block.vector
        def _(dve):
            for h in range(HR):
                dve.wait_ge(s_sum, h + 1)
                nc.vector.scalar_tensor_tensor(out=wide(oc[:, h, :]), in0=B.psum[:, 0:3, 0:TT], scalar=-1.0 / DVR,
                                               in1=wide(o[:, h, :]), op0=ALU.mult, op1=ALU.add).then_inc(s_oc, 1)
            for h in range(HR):
                dve.wait_ge(s_oc, h + 1)
                dve.wait_ge(s_rs, 2 * h + 2)
                nc.vector.tensor_tensor(o[:, h, :], oc[:, h, :], sq[:, h, :], ALU.mult).then_inc(s_on, 1)
                dve.wait_ge(s_on, 2 * h + 1)
                nc.vector.tensor_tensor(o[:, h, :], o[:, h, :], r[:, 8 + h, :], ALU.mult).then_inc(s_on, 1)

        @block.scalar
        def _(act):
            for h in range(HR):
                act.wait_ge(s_oc, h + 1)
                nc.scalar.activation(sq[:, h, :], oc[:, h, :], ACT.Square).then_inc(s_sq, 1)
                act.wait_ge(s_sum2, h + 1)
                nc.scalar.activation(wide(sq[:, h, :]), B.psum[:, 3:6, 0:TT], ACT.Ln, bias=B.eps[:, 0:1], scale=1.0 / DVR).then_inc(s_rs, 1)
                act.wait_ge(s_rs, 2 * h + 1)
                nc.scalar.activation(sq[:, h, :], sq[:, h, :], ACT.Exp, scale=-0.5).then_inc(s_rs, 1)
            for h in range(HR):
                act.wait_ge(s_on, 2 * h + 2)
                nc.scalar.copy(B.hh[:, 4 + h, :], o[:, h, :]).then_inc(s_hi, 1)

        @block.gpsimd
        def _(pool):
            for h in range(HR):
                pool.wait_ge(s_hi, h + 1)
                nc.gpsimd.tensor_tensor(B.hl[:, 4 + h, :], o[:, h, :], B.hh[:, 4 + h, :].bitcast(F32), ALU.subtract).then_inc(s_lo, 1)
    B.top = mark


def project_add(B, w):
    nc = B.nc
    U0 = B.unit
    par = lambda e: (U0 + e) % 2
    s_x = B.sem("x_loaded")
    with nc.Block() as block:
        @block.sync
        def _(sp):
            B.load_weights(sp, U0, par(0), w[0])
            B.load_weights(sp, U0 + 1, par(1), w[1])
            sp.dma_start(B.x[:], B.x_scratch).then_inc(s_x, 16)
            with sp.Fori(1, 4) as j:
                for e in range(2):
                    B.load_weights(sp, j * 2 + (U0 + e), par(e), w[bass.ds(j * 2 + e, 1)].rearrange("o p k m -> p (o k) m"))

        @block.gpsimd
        def _(pool):
            with pool.Fori(0, 4) as j:
                for e in range(2):
                    B.split_low(pool, j * 2 + (U0 + e), par(e))

        @block.scalar
        def _(act):
            with act.Fori(0, 4) as j:
                for e in range(2):
                    B.split_high(act, j * 2 + (U0 + e), par(e))

        @block.tensor
        def _(pe):
            with pe.Fori(0, 4) as j:
                for e in range(2):
                    B.multiply(pe, j * 2 + (U0 + e), par(e), B.hh, B.hl)

        @block.vector
        def _(dve):
            dve.wait_ge(s_x, 16)
            with dve.Fori(0, 4) as j:
                for e in range(2):
                    for t in range(NT):
                        B.await_tile(dve, j * 2 + (U0 + e), t)
                        xs = B.x[:, bass.ds(j * 2 + e, 1), tcols(t)].rearrange("p o c -> p (o c)")
                        nc.vector.tensor_tensor(xs, xs, B.tile(par(e), t), ALU.add).then_inc(B.s_tile_free, 1)
    B.unit += 8



def time_steps(B, norm):
    nc = B.nc
    HC = NBLK * NH
    B.cw = B.take("conv_weights_sb", [P, 32, CW + 1])
    B.nw = B.take("ssm_norm_sb", [P, 16])
    B.dskip = B.take("d_skip_sb", [P, NH])
    B.dt = B.take("dt_rows_sb", [P, HC])
    B.acs = B.take("decay_sum_rows_sb", [P, HC])
    B.eacs = B.take("decay_rows_sb", [P, HC])
    B.dend = B.take("decay_to_end_sb", [P, HC])
    B.etot = B.take("chunk_decay_sb", [P, HC])
    B.chs = B.take("sample_channel_values_sb", [P, 16, 2 * NS + 1])
    B.hist = B.take("conv_history_sb", [P, 32, NS * (CW - 1)])
    mark = B.top
    raw = B.take("dt_raw_sb", [NH, TOK])
    dtt = B.take("dt_sb", [NH, TOK])
    dta = B.take("dt_a_sb", [NH, TOK])
    sm = B.take("head_values_sb", [NH, 4])
    dar = B.take("dt_a_rows_sb", [P, HC])
    expand = B.take("expand_sb", [NH, 16, P])
    srhs = B.take("sample_head_values_sb", [NH, 2 * NS + 1])
    hrow = B.take("history_rows_sb", [NS * (CW - 1), CONV_DIM])
    acst = B.take("decay_sum_sb", [NH, SEQ])
    tot = B.take("chunk_sum_sb", [P, HC])
    B.acs_scratch = nc.dram_tensor("decay_sum_scratch", (NH, SEQ), F32, kind="Internal").ap()
    U0 = B.unit
    par = U0 % 2
    w_in = B.i["w_in_odd"][0].rearrange("(k p) n -> p k n", p=P)
    (s_raw, s_act, s_rows, s_t, s_sums, s_sumc, s_exp, s_h, s_hc, s_ch, s_chc) = (B.sem(x) for x in (
        "dt_copied", "dt_exp", "dt_rows", "dt_turned", "sums", "sums_kept", "decays", "history_turned", "history_kept",
        "channels", "channels_kept"))
    s_ld, s_hl, s_acst, s_dt = B.sem("head_values_loaded"), B.sem("history_loaded"), B.sem("decay_sum_stored"), B.tally("dt_step")
    with nc.Block() as block:
        @block.sync
        def _(sp):
            B.load_weights(sp, U0, par, w_in[:, :, COL_DT:COL_DT + NH], NH)
            norm.store_x(sp)
            norm.await_done(sp)
            with nc.allow_non_contiguous_dma("small per-head and per-channel values, once"):
                for n, name in enumerate(("dt_bias", "a_log", "d_skip")):
                    sp.dma_start(sm[:, n:n + 1], B.i[name].rearrange("o h -> h o")).then_inc(s_ld, 16)
                for j in range(CW):
                    sp.dma_start(B.cw[:, :, j], B.i["conv_w"][0, j].rearrange("(c p) -> p c", p=P)).then_inc(s_ld, 16)
                sp.dma_start(B.cw[:, :, CW], B.i["conv_b"][0].rearrange("(c p) -> p c", p=P)).then_inc(s_ld, 16)
                sp.dma_start(B.nw[:], B.i["ssm_norm"][0].rearrange("(c p) -> p c", p=P)).then_inc(s_ld, 16)
                sp.dma_start(B.dskip[:], B.i["d_skip"].to_broadcast([P, NH])).then_inc(s_ld, 16)
            sp.dma_start(expand[:].rearrange("h c p -> h (c p)"), B.i["expand"]).then_inc(s_ld, 16)
            sp.dma_start(hrow[:], B.i["state_conv"][0].rearrange("b j c -> (b j) c")).then_inc(s_hl, 16)
            sp.dma_start(B.o["conv_sample"][0, :, 0:CW - 2, :], B.i["state_conv"][0, :, 1:CW - 1, :]).then_inc(s_hl, 16)
            sp.wait_ge(s_sumc, 2)
            sp.dma_start(B.acs_scratch, acst[:]).then_inc(s_acst, 16)
            sp.wait_ge(s_acst, 16)
            sp.wait_ge(s_hl, 32)

        @block.gpsimd
        def _(pool):
            norm.pool(pool)

        @block.tensor
        def _(pe):
            norm.pe(pe)
            pe.wait_ge(s_ld, 16 * 11)
            pe.wait_ge(s_hl, 32)
            for n in range(8):
                if n >= 2:
                    pe.wait_ge(s_hc, n - 1)
                for j in range(4):
                    ins = nc.tensor.transpose(B.psum[:, 6 + n % 2, j * 24:(j + 1) * 24], hrow[:, (4 * n + j) * P:(4 * n + j + 1) * P],
                                              B.ident[0:24, 0:24])
                ins.then_inc(s_h, 1)
            pe.wait_ge(s_act, 3)
            for n in range(NBLK):
                nc.tensor.transpose(B.psum[:, 3, n * NH:(n + 1) * NH], dtt[:, n * P:(n + 1) * P], B.ident[0:NH, 0:NH])
                ins = nc.tensor.transpose(B.psum[:, 4, n * NH:(n + 1) * NH], dta[:, n * P:(n + 1) * P], B.ident[0:NH, 0:NH])
            ins.then_inc(s_t, 1)
            pe.wait_ge(s_rows, 2)
            nc.tensor.matmul(B.psum[:, 5, 0:HC], B.upto[:], dar[:], start=True, stop=True)
            nc.tensor.matmul(B.psum[:, 0, 0:HC], B.ones[:], dar[:], start=True, stop=True)
            for n in range(NBLK):
                ins = nc.tensor.matmul(B.psum[0:NH, 1 + n // 4, (n % 4) * P:(n % 4 + 1) * P], dar[:, n * NH:(n + 1) * NH],
                                       B.upto[:], start=True, stop=True)
            ins.then_inc(s_sums, 1)
            pe.wait_ge(s_chc, 1)
            for c in range(16):
                ins = nc.tensor.matmul(B.psum[:, 3, c * 17:c * 17 + 17], expand[:, c, :], srhs[:], start=True, stop=True)
            ins.then_inc(s_ch, 1)

        @block.scalar
        def _(act):
            norm.act(act)
            act.wait_ge(s_ld, 16 * 11)
            for t in range(NT):
                B.await_tile(act, U0, t)
                nc.scalar.activation(raw[:, tcols(t)], B.tile(par, t, NH), ACT.Identity, bias=sm[:, 0:1]).then_inc(B.s_tile_free, 1)
            act.wait_ge(B.s_tile_free, 6 + 3 * (U0 + 1))
            s_soft = B.sem("softplus_step")
            nc.scalar.activation(dtt[:], raw[:], ACT.Abs).then_inc(s_soft, 1)
            act.wait_ge(s_soft, 1)
            nc.scalar.activation(dtt[:], dtt[:], ACT.Exp, scale=-1.0).then_inc(s_soft, 1)
            nc.scalar.activation(sm[:, 3:4], sm[:, 1:2], ACT.Exp).then_inc(s_soft, 1)
            act.wait_ge(s_soft, 3)
            nc.scalar.activation(dtt[:], dtt[:], ACT.Ln, bias=B.ones[0:NH, 0:1]).then_inc(s_raw, 1)
            act.wait_ge(s_sumc, 5)
            nc.scalar.activation(B.eacs[:], B.acs[:], ACT.Exp).then_inc(s_exp, 1)
            nc.scalar.activation(B.etot[:], tot[:], ACT.Exp).then_inc(s_exp, 1)
            nc.scalar.activation(B.dend[:], B.dend[:], ACT.Exp).then_inc(s_exp, 1)
            act.wait_ge(s_chc, 2)
            nc.scalar.activation(B.chs[:, :, NS:2 * NS], B.chs[:, :, NS:2 * NS], ACT.Exp).then_inc(s_exp, 1)

        @block.vector
        def _(dve):
            norm.dve(dve)
            norm.await_done(dve)
            for n in range(8):
                dve.wait_ge(s_h, n + 1)
                nc.vector.tensor_copy(B.hist[:, 4 * n:4 * n + 4, :], B.psum[:, 6 + n % 2, 0:96].rearrange("p (j c) -> p j c", j=4)).then_inc(s_hc, 1)
            dve.wait_ge(s_raw, 1)
            done(dve, nc.vector.scalar_tensor_tensor(out=dtt[:], in0=raw[:], scalar=0.0, in1=dtt[:], op0=ALU.max, op1=ALU.add), s_dt)
            done(dve, nc.vector.tensor_scalar(dta[:], dtt[:], sm[:, 3:4], -1.0, ALU.mult, ALU.mult), s_dt)
            nc.vector.tensor_copy(srhs[:, 0:NS], dtt[:, SEQ:TOK]).then_inc(s_act, 1)
            nc.vector.tensor_copy(srhs[:, NS:2 * NS], dta[:, SEQ:TOK]).then_inc(s_act, 1)
            nc.vector.tensor_copy(srhs[:, 2 * NS:2 * NS + 1], sm[:, 2:3]).then_inc(s_act, 1)
            dve.wait_ge(s_act, 3)
            dve.sem_inc(s_chc, 1)
            dve.wait_ge(s_t, 1)
            nc.vector.tensor_copy(B.dt[:], B.psum[:, 3, 0:HC]).then_inc(s_rows, 1)
            nc.vector.tensor_copy(dar[:], B.psum[:, 4, 0:HC]).then_inc(s_rows, 1)
            dve.wait_ge(s_sums, 1)
            nc.vector.tensor_copy(acst[:, 0:512], B.psum[0:NH, 1, :]).then_inc(s_sumc, 1)
            nc.vector.tensor_copy(acst[:, 512:1024], B.psum[0:NH, 2, :]).then_inc(s_sumc, 1)
            nc.vector.tensor_copy(B.acs[:], B.psum[:, 5, 0:HC]).then_inc(s_sumc, 1)
            nc.vector.tensor_copy(tot[:], B.psum[:, 0, 0:HC]).then_inc(s_sumc, 1)
            dve.wait_ge(s_sumc, 4)
            nc.vector.tensor_tensor(B.dend[:], tot[:], B.acs[:], ALU.subtract).then_inc(s_sumc, 1)
            dve.wait_ge(s_ch, 1)
            nc.vector.tensor_copy(B.chs[:].rearrange("p c n -> p (c n)"), B.psum[:, 3, 0:16 * 17]).then_inc(s_chc, 1)
            dve.wait_ge(s_exp, 3)
            done(dve, nc.vector.tensor_tensor(B.dend[:], B.dend[:], B.dt[:], ALU.mult), s_dt)
    B.unit += 1
    B.top = mark


def mamba_groups(B):
    nc = B.nc
    mark = B.top
    PAD = CW - 1
    pre = B.take("conv_in_sb", [P, 4, PAD + TOK])
    post = B.take("conv_out_sb", [P, 4, TOK])
    z = B.take("z_sb", [P, 2, TOK])
    bc = B.take("decay_sum_spread_sb", [P, HPG, SEQ])
    acc = B.take("conv_sum_sb", [P, 2, TOK])
    tmp = acc[:].rearrange("p s c -> p (s c)")[:, 0:2048].rearrange("p (c b n) -> p c b n", c=2, b=NS)
    rows = B.take("x_b_rows_sb", [P, 2, 384])
    xdt = B.take("x_dt_sb", [P, 2, 256])
    xdec = B.take("x_decayed_sb", [P, 2, 256])
    xd = B.take("x_d_sb", [P, 2, 256])
    cbm = B.take("cb_masked_sb", [P, 2, P])
    state = B.take("scan_state_sb", [P, 2, 256])
    ste = B.take("scan_state_decayed_sb", [P, 256])
    yb = B.take("y_sb", [P, 256])
    gz = B.take("gated_rows_sb", [P, NBLK, 256])
    ss = B.take("square_sums_sb", [P, NBLK])
    st = B.take("sample_ssm_state_sb", [P, NS, 2, P])
    dg = B.take("diagonals_sb", [P, NS, P])
    gst = B.take("gated_sb", [P, 2, TOK])
    sml = B.take("sample_small_sb", [P, 8, 16])
    cst = gz[0:PAD + NS, 0:2, :].rearrange("p n (j c) -> p (n j) c", j=2)
    sst = xd[:, 0, :].rearrange("p (c n) -> p c n", c=2)
    B.g_scratch = nc.dram_tensor("gated_scratch", (16, P, TOK), F32, kind="Internal").ap()
    U0 = B.unit
    par = lambda e: (U0 + e) % 2
    w_in = B.i["w_in_odd"][0].rearrange("(k p) n -> p k n", p=P)
    w_pair = lambda c0: w_in[:, :, c0:c0 + G * 256].rearrange("p k (g e m) -> e g p k m", e=2, m=P)
    w_one = lambda c0: w_in[:, :, c0:c0 + G * P].rearrange("p k (g m) -> g p k m", m=P)
    w_of = [w_pair(COL_X)[0], w_pair(COL_X)[1], w_one(COL_B), w_one(COL_C), w_pair(COL_Z)[0], w_pair(COL_Z)[1]]
    names = ("conv_sum", "conv_out", "chunk_turned", "chunk_y", "chunk_state_sum", "rows_copied", "differences",
             "exps", "cb_masked", "scores", "x_dt", "x_decayed", "x_d", "state_decayed", "state", "gated",
             "square_sums", "rstd", "gated_scaled", "gated_turned", "gated_stored_col", "diagonal", "spread", "outer",
             "sample_state", "sample_gated", "sample_sum", "conv_rows_turned", "conv_rows_kept", "state_turned",
             "state_rows", "pad_set", "sample_scaled", "sample_decayed", "sample_mean", "column_half")
    S = {n: B.sem(n) for n in names}
    s_bc, s_st, s_sto = B.sem("spread_loaded"), B.sem("sample_ssm_loaded"), B.sem("sample_ssm_stored")
    s_gout, s_cout, s_sout = B.sem("gated_stored"), B.sem("conv_rows_stored"), B.sem("state_stored")
    s_dv = B.tally("vector_step")
    SLOT = {0: [0], 1: [1], 2: [2], 3: [3], 4: [4], 5: [5], 7: [6], 8: [7], 9: [8]}

    def unit(g, e):
        return g * 6 + (U0 + e)

    def await_group(eng, sem, g, per, n):
        eng.wait_ge(sem, g * per + n)

    def head_cols(a, g, n):
        return a[:, bass.ds(g * HPG + n * NH, HPG)]

    def rounds(eng, part, *tallies):
        part(None, 0)
        if tallies:
            with counted(eng, G - 1, *tallies) as g:
                part(g, g + 1)
        else:
            with eng.Fori(0, G - 1) as g:
                part(g, g + 1)
        part(G - 1, None)

    def rounds_ahead(eng, part):
        part(None, 0, True)
        with eng.Fori(0, G - 2) as g:
            part(g, g + 1, True)
        part(G - 2, G - 1, False)
        part(G - 1, None, False)

    with nc.Block() as block:
        @block.sync
        def _(sp):
            def load_unit(nx, e):
                B.load_weights(sp, unit(nx, e), par(e), w_of[e][bass.ds(nx, 1)].rearrange("o p k m -> p (o k) m"), held=True)

            def part(g, nx, more):
                if g is not None:
                    sp.wait_ge(S["chunk_y"], g * NBLK)
                    B.hold(sp)
                    sp.dma_start(bc[:], bass.AP(tensor=B.acs_scratch.tensor, offset=g * (HPG * SEQ),
                                                ap=[[0, P], [SEQ, HPG], [1, SEQ]])).then_inc(s_bc, 16)
                    sp.wait_ge(s_sto, g * (16 * NS))
                    sp.wait_ge(S["sample_gated"], g)
                    B.hold(sp)
                    for b in range(NS):
                        sp.dma_start(st[:, b], B.i["state_ssm"][0, b].rearrange("(g c two) q n -> g (two q) c n", g=G, two=2)
                                     [bass.ds(g, 1)].rearrange("o p c n -> p (o c) n")).then_inc(s_st, 16)
                if nx is not None:
                    for e in range(0 if g is None else 1, 6):
                        load_unit(nx, e)
                if more:
                    load_unit(nx + 1, 0)
            rounds_ahead(sp, part)

        @block.gpsimd
        def _(pool):
            def out_states(g):
                pool.wait_ge(S["sample_state"], g + 1)
                B.hold(pool)
                for b in range(NS):
                    pool.dma_start(B.o["ssm_sample"][0, b].rearrange("(g c two) q n -> g (two q) c n", g=G, two=2)
                                   [bass.ds(g, 1)].rearrange("o p c n -> p (o c) n"), st[:, b]).then_inc(s_sto, 16)

            def store_conv_rows(g):
                pool.wait_ge(S["conv_rows_kept"], g + 1)
                B.hold(pool)
                for j0, n, c0, w in ((0, 2, g * 256, 256), (2, 1, g * P + D_INNER, P), (3, 1, g * P + (D_INNER + G * NST), P)):
                    src = cst[:, j0:j0 + n, :].rearrange("p j c -> p (j c)")
                    pool.dma_start(B.o["conv_prompt"][0, 0][:, bass.ds(c0, w)], src[0:PAD]).then_inc(s_cout, 16)
                    pool.dma_start(B.o["conv_sample"][0, :, CW - 2, :][:, bass.ds(c0, w)], src[PAD:PAD + NS]).then_inc(s_cout, 16)

            def finish(g):
                pool.wait_ge(S["state_rows"], g + 1)
                B.hold(pool)
                pool.dma_start(B.o["ssm_prompt"][0, 0].rearrange("(g c two) q n -> g (two q) c n", g=G, two=2)
                               [bass.ds(g, 1)].rearrange("o p c n -> p (o c) n"), sst).then_inc(s_sout, 16)
                pool.wait_ge(S["gated_stored_col"], g * 8 + 8)
                pool.wait_ge(S["sample_scaled"], g + 1)
                B.hold(pool)
                pool.dma_start(B.g_scratch.rearrange("(g e) p c -> g p e c", e=2)[bass.ds(g, 1)].rearrange("o p e c -> p (o e) c"),
                               gst[:]).then_inc(s_gout, 16)

            def part(g, nx, more):
                splits = [] if nx is None else [0, 1, 2, 3] if g is None else [1, 2, 3]
                if g is not None:
                    pool.wait_ge(S["conv_out"], g * 4 + 4)
                    pool.wait_ge(S["sample_gated"], g)
                    nc.gpsimd.tensor_tensor(dg[:], B.ident[:].unsqueeze(1).to_broadcast([P, NS, P]),
                                            post[:, 2, SEQ:TOK].unsqueeze(2).to_broadcast([P, NS, P]), ALU.mult).then_inc(S["diagonal"], 1)
                for k in range(9):
                    if splits and k % 2 == 0 and (k > 0 or g is None):
                        e = splits.pop(0)
                        B.split_low(pool, unit(nx, e), par(e))
                    if g is None:
                        continue
                    if k == 0:
                        store_conv_rows(g)
                    if k < NBLK:
                        n = k
                        await_group(pool, S["rows_copied"], g, NBLK, n + 1)
                        await_group(pool, S["square_sums"], g, NBLK, max(n - 1, 0))
                        if n == 0:
                            pool.wait_ge(s_sout, g * 16)
                        B.hold(pool)
                        nc.gpsimd.tensor_tensor(xd[:, n % 2, :].rearrange("p (h q) -> p h q", h=HPG),
                                                rows[:, n % 2, 0:256].rearrange("p (h q) -> p h q", h=HPG),
                                                B.dskip[:, bass.ds(g * HPG, HPG)].unsqueeze(2).to_broadcast([P, HPG, PS]),
                                                ALU.mult).then_inc(S["x_d"], 1)
                        nc.gpsimd.tensor_tensor(xdec[:, n % 2, :].rearrange("p (h q) -> p h q", h=HPG),
                                                rows[:, n % 2, 0:256].rearrange("p (h q) -> p h q", h=HPG),
                                                head_cols(B.dend, g, n).unsqueeze(2).to_broadcast([P, HPG, PS]),
                                                ALU.mult).then_inc(S["x_decayed"], 1)
                        if n >= 1:
                            await_group(pool, S["state"], g, NBLK, n)
                            B.hold(pool)
                            nc.gpsimd.tensor_tensor(ste[:].rearrange("p (h q) -> p h q", h=HPG),
                                                    state[:, (n - 1) % 2, :].rearrange("p (h q) -> p h q", h=HPG),
                                                    head_cols(B.etot, g, n).unsqueeze(2).to_broadcast([P, HPG, PS]),
                                                    ALU.mult).then_inc(S["state_decayed"], 1)
                    if k == 1:
                        pool.wait_ge(s_st, g * (16 * NS) + 16 * NS)
                        B.hold(pool)
                        nc.gpsimd.tensor_tensor(st[:], st[:], B.chs[:, bass.ds(g * 2, 2), NS:2 * NS].rearrange("p c b -> p b c")
                                                .unsqueeze(3).to_broadcast([P, NS, 2, P]), ALU.mult).then_inc(S["sample_decayed"], 1)
                    if k == 3:
                        pool.wait_ge(S["outer"], g + 1)
                        pool.wait_ge(S["sample_decayed"], g + 1)
                        nc.gpsimd.tensor_tensor(dg[:], B.ident[:].unsqueeze(1).to_broadcast([P, NS, P]),
                                                post[:, 3, SEQ:TOK].unsqueeze(2).to_broadcast([P, NS, P]), ALU.mult).then_inc(S["diagonal"], 1)
                        nc.gpsimd.tensor_tensor(st[:], st[:], tmp.rearrange("p c b n -> p b c n"), ALU.add).then_inc(S["sample_state"], 1)
                    if k == 4:
                        out_states(g)
                if splits:
                    raise AssertionError(splits)
                for e in ((4, 5) if nx is not None else ()):
                    B.split_low(pool, unit(nx, e), par(e))
                if more:
                    B.split_low(pool, unit(nx + 1, 0), par(0))
                if g is not None:
                    finish(g)
            rounds_ahead(pool, part)
            pool.wait_ge(s_sto, 16 * NS * G)
            pool.wait_ge(s_gout, 16 * G)
            pool.wait_ge(s_sout, 16 * G)
            pool.wait_ge(s_cout, 16 * 6 * G)

        @block.tensor
        def _(pe):
            def tile(nx, e, t):
                u = unit(nx, e)
                if t == 0:
                    pe.wait_ge(B.s_w_high, u + 1)
                    pe.wait_ge(B.s_w_low, u + 3)
                pe.wait_ge(B.s_tile_free, u * 3 + t + 4)
                m = 0
                for k in range(KT):
                    for w, a in ((B.wh, B.hh), (B.wh, B.hl), (B.wl, B.hh)):
                        ins = nc.tensor.matmul(B.psum[:, t, 0:TT], w[:, par(e), k, :], a[:, k, tcols(t)], start=m == 0,
                                               stop=m == 3 * KT - 1)
                        m += 1
                ins.then_inc(B.s_tile, 1)

            def turn(g, n):
                if n == 0:
                    pe.wait_ge(S["conv_out"], g * 4 + 4)
                    pe.wait_ge(S["gated_stored_col"], g * 8)
                await_group(pe, S["rows_copied"], g, NBLK, n)
                await_group(pe, S["cb_masked"], g, NBLK, n)
                c = slice(n * P, (n + 1) * P)
                for j in range(3):
                    nc.tensor.transpose(B.psum[:, 3, j * P:(j + 1) * P], post[:, j, c], B.ident[:])
                nc.tensor.matmul(B.psum[:, 3, 384:512], post[:, 2, c], post[:, 3, c], start=True, stop=True).then_inc(S["chunk_turned"], 1)

            def scan(g, n):
                if n == 0:
                    pe.wait_ge(B.s_tile_free, unit(g, 5) * 3 + 9)
                    pe.wait_ge(S["conv_rows_kept"], g + 1)
                await_group(pe, S["scores"], g, NBLK, n + 1)
                await_group(pe, S["gated"], g, NBLK, n)
                await_group(pe, S["state"], g, NBLK, n)
                c = slice(n * P, (n + 1) * P)
                for j in range(2):
                    nc.tensor.transpose(B.psum[:, 5, 256 + j * P:256 + (j + 1) * P], z[:, j, c], B.ident[:])
                for h in range(HPG):
                    ins = nc.tensor.matmul(B.psum[:, 4, h * PS:(h + 1) * PS], bc[:, h, c], xdt[:, n % 2, h * PS:(h + 1) * PS],
                                           start=True, stop=True)
                if n >= 1:
                    ins = nc.tensor.matmul(B.psum[:, 4, 256:512], post[:, 3, c], state[:, (n - 1) % 2, :], start=True, stop=True)
                ins.then_inc(S["chunk_y"], 1)
                await_group(pe, S["x_decayed"], g, NBLK, n + 1)
                nc.tensor.matmul(B.psum[:, 5, 0:256], rows[:, n % 2, 256:384], xdec[:, n % 2, :], start=True,
                                 stop=True).then_inc(S["chunk_state_sum"], 1)

            def spread(g, m):
                await_group(pe, S["diagonal"], g, 2, m + 1)
                if m == 0:
                    pe.wait_ge(S["state_rows"], g)
                    pe.wait_ge(S["sample_scaled"], g)
                for a in range(2):
                    ins = nc.tensor.matmul(B.psum[:, 6 + a, :], B.ones[:],
                                           dg[:, 4 * a:4 * a + 4, :].rearrange("p b n -> p (b n)"), start=True, stop=True)
                ins.then_inc(S["spread"], 1)

            def slot(g, k):
                if k < NBLK:
                    turn(g, k)
                if k >= 1:
                    scan(g, k - 1)
                if k == 2:
                    spread(g, 0)
                if k == 5:
                    spread(g, 1)

            def sample_sum(g):
                pe.wait_ge(S["sample_gated"], g + 1)
                nc.tensor.matmul(B.psum[:, 6, 0:16], B.ones[:], sml[:, 3, :], start=True, stop=True).then_inc(S["sample_sum"], 1)

            def finish(g, n):
                pe.wait_ge(S["gated_scaled"], g * 8 + n + 1)
                if n >= 2:
                    pe.wait_ge(S["gated_stored_col"], g * 8 + n - 1)
                for j in range(2):
                    ins = nc.tensor.transpose(B.psum[:, 3 + n % 2, j * P:(j + 1) * P], gz[:, n, j * P:(j + 1) * P], B.ident[:])
                ins.then_inc(S["gated_turned"], 1)

            def part(g, nx):
                for i in range(12):
                    if nx is not None:
                        tile(nx, i // 3, i % 3)
                    if g is not None:
                        for k in SLOT.get(i, []):
                            slot(g, k)
                if nx is not None:
                    tile(nx, 4, 0)
                if g is not None:
                    sample_sum(g)
                for i in range(5):
                    if nx is not None:
                        tile(nx, 4 + (i + 1) // 3, (i + 1) % 3)
                    if g is not None and i == 0:
                        await_group(pe, S["state"], g, NBLK, NBLK)
                        for j in range(2):
                            ins = nc.tensor.transpose(B.psum[:, 7, j * P:(j + 1) * P], state[:, (NBLK - 1) % 2, j * P:(j + 1) * P], B.ident[:])
                        ins.then_inc(S["state_turned"], 1)
                        pe.wait_ge(S["gated"], g * 8 + 8)
                    if g is not None:
                        for n in ((0, 1), (2, 3), (4, 5), (6, 7), ())[i]:
                            finish(g, n)
                if nx is not None:
                    pe.wait_ge(B.s_tile_free, unit(nx, 3) * 3 + 9)
                    if g is not None:
                        pe.wait_ge(S["chunk_state_sum"], g * 8 + 8)
                        pe.wait_ge(S["gated"], g * 8 + 8)
                        pe.wait_ge(S["state"], g * 8 + 8)
                    for j in range(4):
                        ins = nc.tensor.transpose(B.psum[0:PAD + NS, 5, j * P:(j + 1) * P], pre[:, j, SEQ:SEQ + PAD + NS], B.ident[:])
                    ins.then_inc(S["conv_rows_turned"], 1)
            rounds(pe, part)

        @block.scalar
        def _(act):
            def evacuate(nx, e, t):
                B.await_tile(act, unit(nx, e), t)
                ps = B.psum[:, t, 0:TT]
                if e < 4:
                    nc.scalar.copy(pre[:, e, PAD + t * TT:PAD + (t + 1) * TT], ps).then_inc(B.s_tile_free, 1)
                else:
                    nc.scalar.activation(z[:, e - 4, tcols(t)], ps, ACT.Silu).then_inc(B.s_tile_free, 1)

            def slot(g, k):
                if k < NBLK:
                    n = k
                    await_group(act, S["chunk_turned"], g, NBLK, n + 1)
                    await_group(act, S["cb_masked"], g, NBLK, n + 1)
                    if n >= 2:
                        await_group(act, S["chunk_state_sum"], g, NBLK, n - 1)
                        await_group(act, S["x_dt"], g, NBLK, n - 1)
                        await_group(act, S["x_decayed"], g, NBLK, n - 1)
                    nc.scalar.copy(rows[:, n % 2, :], B.psum[:, 3, 0:384]).then_inc(S["rows_copied"], 1)
                    await_group(act, S["differences"], g, NBLK, n + 1)
                    e = bc[:, :, n * P:(n + 1) * P]
                    nc.scalar.activation(e, e, ACT.Exp).then_inc(S["exps"], 1)
                if k >= 2:
                    square(g, k - 2)

            def square(g, n):
                await_group(act, S["gated"], g, NBLK, n + 1)
                nc.scalar.activation(xd[:, n % 2, :], gz[:, n, :], ACT.Square, accum_out=ss[:, n:n + 1]).then_inc(S["square_sums"], 1)

            def finish(g, n):
                act.wait_ge(S["gated_turned"], g * 8 + n + 1)
                B.hold(act)
                for e in range(2):
                    nc.scalar.activation(gst[:, e, n * P:(n + 1) * P], B.psum[:, 3 + n % 2, e * P:(e + 1) * P], ACT.Copy,
                                         scale=B.nw[:, bass.ds(g * 2 + e, 1)]).then_inc(
                        S["gated_stored_col"] if e == 1 else S["column_half"], 1)

            def silu(nx, j):
                act.wait_ge(S["conv_sum"], nx * 4 + j + 1)
                nc.scalar.activation(post[:, j, :], acc[:, j % 2, :], ACT.Silu).then_inc(S["conv_out"], 1)

            def part(g, nx, more):
                if nx is not None:
                    if g is None:
                        B.split_high(act, unit(nx, 0), par(0))
                    if g is not None:
                        act.wait_ge(S["conv_sum"], g * 4 + 4)
                        act.wait_ge(S["conv_rows_turned"], g + 1)
                for i in range(12):
                    if nx is not None:
                        if i % 3 == 0:
                            B.split_high(act, unit(nx, i // 3 + 1), par(i // 3 + 1))
                        evacuate(nx, i // 3, i % 3)
                    if g is not None:
                        for k in SLOT.get(i, []):
                            slot(g, k)
                if g is not None:
                    square(g, NBLK - 1)
                    act.wait_ge(S["square_sums"], g * 8 + 8)
                    nc.scalar.activation(ss[:], ss[:], ACT.Ln, bias=B.eps[:, 0:1], scale=1.0 / 256).then_inc(S["rstd"], 1)
                    act.wait_ge(S["rstd"], g * 4 + 1)
                    nc.scalar.activation(ss[:], ss[:], ACT.Exp, scale=-0.5).then_inc(S["rstd"], 1)
                    act.wait_ge(S["rstd"], g * 4 + 2)
                    act.wait_ge(s_gout, g * 16)
                    for n in range(NBLK):
                        nc.scalar.activation(gz[:, n, :], gz[:, n, :], ACT.Copy, scale=ss[:, n:n + 1]).then_inc(S["gated_scaled"], 1)
                    act.wait_ge(S["sample_mean"], g + 1)
                    nc.scalar.activation(sml[:, 4, 0:8], sml[:, 4, 0:8], ACT.Ln, bias=B.eps[:, 0:1], scale=1.0 / 256).then_inc(S["rstd"], 1)
                    act.wait_ge(S["rstd"], g * 4 + 3)
                    nc.scalar.activation(sml[:, 4, 0:8], sml[:, 4, 0:8], ACT.Exp, scale=-0.5).then_inc(S["rstd"], 1)
                if nx is not None:
                    if g is not None:
                        act.wait_ge(S["chunk_turned"], g * 8 + 8)
                        act.wait_ge(S["sample_gated"], g + 1)
                    silu(nx, 0)
                for i in range(6):
                    if nx is not None:
                        if i == 0:
                            B.split_high(act, unit(nx, 5), par(5))
                        if i == 3 and more:
                            B.split_high(act, unit(nx + 1, 0), par(0))
                        evacuate(nx, 4 + i // 3, i % 3)
                    if g is not None and 1 <= i <= 4:
                        finish(g, 2 * i - 2)
                        finish(g, 2 * i - 1)
                    if nx is not None and i in (0, 3, 5):
                        if i == 3 and g is not None:
                            act.wait_ge(S["chunk_state_sum"], g * 8 + 8)
                        silu(nx, {0: 1, 3: 2, 5: 3}[i])
            rounds_ahead(act, part)

        @block.vector
        def _(dve):
            def step(ins):
                done(dve, ins, s_dv)

            def start(g, n):
                if n == 0:
                    dve.wait_ge(s_bc, g * 16 + 16)
                for h in range(HPG):
                    e = bc[:, h, n * P:(n + 1) * P]
                    ins = nc.vector.tensor_scalar(e, e, B.acs[:, bass.ds(g * HPG + (n * NH + h), 1)], 0.0, ALU.subtract, ALU.min)
                ins.then_inc(S["differences"], 1)

            def scores(g, n):
                await_group(dve, S["chunk_turned"], g, NBLK, n + 1)
                nc.vector.tensor_tensor(cbm[:, n % 2, :], B.psum[:, 3, 384:512], B.upto[:], ALU.mult).then_inc(S["cb_masked"], 1)
                await_group(dve, S["rows_copied"], g, NBLK, n + 1)
                nc.vector.tensor_tensor(xdt[:, n % 2, :].rearrange("p (h q) -> p h q", h=HPG),
                                        rows[:, n % 2, 0:256].rearrange("p (h q) -> p h q", h=HPG),
                                        head_cols(B.dt, g, n).unsqueeze(2).to_broadcast([P, HPG, PS]), ALU.mult).then_inc(S["x_dt"], 1)
                await_group(dve, S["exps"], g, NBLK, n + 1)
                await_group(dve, S["cb_masked"], g, NBLK, n + 1)
                e = bc[:, :, n * P:(n + 1) * P]
                await_group(dve, S["x_dt"], g, NBLK, n + 1)
                nc.vector.tensor_tensor(e, e, cbm[:, n % 2, :].unsqueeze(1).to_broadcast([P, HPG, P]), ALU.mult).then_inc(S["scores"], 1)

            def gate(g, n):
                await_group(dve, S["chunk_state_sum"], g, NBLK, n + 1)
                if n == 0:
                    dve.wait_ge(S["gated_turned"], g * 8)
                    dve.wait_ge(s_cout, g * 96 + 96)
                    nc.vector.tensor_copy(state[:, 0, :], B.psum[:, 5, 0:256]).then_inc(S["state"], 1)
                else:
                    await_group(dve, S["state_decayed"], g, NBLK - 1, n)
                    nc.vector.tensor_tensor(state[:, n % 2, :], ste[:], B.psum[:, 5, 0:256], ALU.add).then_inc(S["state"], 1)
                await_group(dve, S["x_d"], g, NBLK, n + 1)
                y = yb[:]
                x_d = xd[:, n % 2, :]
                step(nc.vector.tensor_tensor(x_d, x_d, B.psum[:, 4, 0:256], ALU.add))
                if n >= 1:
                    step(nc.vector.tensor_tensor(y.rearrange("p (h q) -> p h q", h=HPG),
                                                 B.psum[:, 4, 256:512].rearrange("p (h q) -> p h q", h=HPG),
                                                 head_cols(B.eacs, g, n).unsqueeze(2).to_broadcast([P, HPG, PS]), ALU.mult))
                    step(nc.vector.tensor_tensor(y, y, x_d, ALU.add))
                    x_d = y
                nc.vector.tensor_tensor(gz[:, n, :], x_d, B.psum[:, 5, 256:512], ALU.mult).then_inc(S["gated"], 1)
                await_group(dve, S["gated"], g, NBLK, n + 1)

            xs = post[:, 0:2, SEQ:TOK]
            small = lambda i: sml[:, i, :].rearrange("p (c b) -> p c b", c=2)

            def outer(g):
                dve.wait_ge(S["conv_out"], g * 4 + 4)
                step(nc.vector.tensor_tensor(small(0), xs, B.chs[:, bass.ds(g * 2, 2), 0:NS], ALU.mult))
                await_group(dve, S["spread"], g, 2, 1)
                for c in range(2):
                    ins = nc.vector.tensor_tensor(tmp[:, c], B.psum[:, 6:8, :].rearrange("p a (b n) -> p (a b) n", b=4),
                                                  small(0)[:, c, :].unsqueeze(2).to_broadcast([P, NS, P]), ALU.mult)
                ins.then_inc(S["outer"], 1)

            def sample_y(g):
                await_group(dve, S["spread"], g, 2, 2)
                dve.wait_ge(S["sample_state"], g + 1)
                for c in range(2):
                    step(nc.vector.tensor_tensor(tmp[:, c], B.psum[:, 6:8, :].rearrange("p a (b n) -> p (a b) n", b=4),
                                                 st[:, :, c, :], ALU.mult))
                step(nc.vector.tensor_reduce(small(1), tmp, AX_X, ALU.add))
                step(nc.vector.tensor_tensor(small(0), xs, B.chs[:, bass.ds(g * 2, 2), 2 * NS:2 * NS + 1].to_broadcast([P, 2, NS]), ALU.mult))
                step(nc.vector.tensor_tensor(small(1), small(1), small(0), ALU.add))
                step(nc.vector.tensor_tensor(small(2), small(1), z[:, :, SEQ:TOK], ALU.mult))
                nc.vector.tensor_tensor(small(3), small(2), small(2), ALU.mult).then_inc(S["sample_gated"], 1)

            def sample_norm(g):
                dve.wait_ge(S["sample_sum"], g + 1)
                step(nc.vector.tensor_copy(sml[:, 5, :], B.psum[:, 6, 0:16]))
                nc.vector.tensor_tensor(sml[:, 4, 0:8], sml[:, 5, 0:8], sml[:, 5, 8:16], ALU.add).then_inc(S["sample_mean"], 1)
                dve.wait_ge(S["rstd"], g * 4 + 4)
                step(nc.vector.tensor_tensor(small(2), small(2), sml[:, 4, 0:8].unsqueeze(1).to_broadcast([P, 2, NS]), ALU.mult))
                dve.wait_ge(s_gout, g * 16)
                nc.vector.tensor_tensor(gst[:, :, SEQ:TOK], small(2), B.nw[:, bass.ds(g * 2, 2)].unsqueeze(2)
                                        .to_broadcast([P, 2, NS]), ALU.mult).then_inc(S["sample_scaled"], 1)
                dve.wait_ge(S["state_turned"], g + 1)
                dve.wait_ge(s_sout, g * 16)
                nc.vector.tensor_copy(sst, B.psum[:, 7, 0:256].rearrange("p (c n) -> p c n", c=2)).then_inc(S["state_rows"], 1)

            def channel(nx, j):
                return (nx * 2, nx * 2 + 1, nx + 16, nx + 24)[j]

            def convolve(nx, j):
                dve.wait_ge(B.s_tile_free, unit(nx, j) * 3 + 9)
                w = lambda i: B.cw[:, bass.ds(channel(nx, j), 1), i]
                a, s = acc[:, j % 2, 0:SEQ], acc[:, j % 2, SEQ:TOK]
                if not (isinstance(nx, int) and j < 2):
                    dve.wait_ge(S["conv_out"], nx * 4 + j - 1)
                step(nc.vector.tensor_scalar(a, pre[:, j, PAD:PAD + SEQ], w(PAD), w(CW), ALU.mult, ALU.add))
                step(nc.vector.tensor_scalar(s, pre[:, j, PAD + SEQ:PAD + TOK], w(PAD), w(CW), ALU.mult, ALU.add))
                for i in range(PAD):
                    step(nc.vector.scalar_tensor_tensor(out=a, in0=pre[:, j, i:i + SEQ], scalar=w(i), in1=a,
                                                        op0=ALU.mult, op1=ALU.add))
                    h = B.hist[:, bass.ds(channel(nx, j), 1), :].rearrange("p o (b i) -> p i (o b)", i=PAD)[:, i]
                    ins = nc.vector.scalar_tensor_tensor(out=s, in0=h, scalar=w(i), in1=s, op0=ALU.mult, op1=ALU.add)
                    if i < PAD - 1:
                        step(ins)
                ins.then_inc(S["conv_sum"], 1)

            def part(g, nx):
                if g is not None:
                    start(g, 0)
                    for k in range(9):
                        if k < NBLK:
                            if k + 1 < NBLK:
                                start(g, k + 1)
                            scores(g, k)
                        if k >= 1:
                            gate(g, k - 1)
                        if k == 2:
                            outer(g)
                        if k == 5:
                            sample_y(g)
                        if k >= 7 and nx is not None:
                            convolve(nx, k - 7)
                if g is not None:
                    sample_norm(g)
                    dve.wait_ge(S["sample_gated"], g + 1)
                    dve.wait_ge(S["sample_state"], g + 1)
                if nx is not None:
                    for j in range(0 if g is None else 2, 4):
                        convolve(nx, j)
                    dve.wait_ge(S["conv_rows_turned"], nx + 1)
                    if g is not None:
                        dve.wait_ge(S["gated_turned"], g * 8 + 8)
                    nc.vector.tensor_copy(cst, B.psum[0:PAD + NS, 5, :].rearrange("p (j c) -> p j c", j=4)).then_inc(S["conv_rows_kept"], 1)
                    dve.wait_ge(S["conv_rows_kept"], nx + 1)

            nc.vector.memset(pre[:, :, 0:PAD], 0.0).then_inc(S["pad_set"], 1)
            dve.wait_ge(S["pad_set"], 1)
            first = s_dv.count
            part(None, 0)
            n_first = s_dv.count - first
            CONV = 4 * (2 + 3 + 2)
            SCAN = (NBLK - 1) * 3 + 1 + 1 + 6 + 2
            assert n_first == CONV, (n_first, CONV)
            with counted(dve, G - 1, (s_dv, CONV + SCAN)) as g:
                part(g, g + 1)
            part(G - 1, None)
    B.unit += 6 * G
    B.top = mark


class Gated(Norm):

    def __init__(self, B):
        self.B, self.width = B, P
        self.u, self.par = B.unit, B.unit % 2
        self.buf = B.take("gated_tiles_sb", [P, self.SLOTS, TOK])
        self.high = (B.hh, B.take("second_high_sb", [P, KT, TOK], F32R))
        self.low = (B.hl, B.take("second_low_sb", [P, KT, TOK], F32R))
        self.s_loaded = [B.sem(f"gated_loaded_{n}") for n in range(self.SLOTS)]
        self.s_high, self.s_low_pool, self.s_low_dve = B.sem("gated_high"), B.sem("gated_low_pool"), B.sem("gated_low_vector")

    def await_low(self, eng, k):
        if k < KT:
            super().await_low(eng, k)
        else:
            eng.wait_ge(self.s_low_pool, len(self.POOL_K) + k - KT + 1)

    def load(self, sp, k):
        if k >= self.SLOTS:
            sp.wait_ge(self.s_high, k - self.SLOTS + 1)
            self.await_low(sp, k - self.SLOTS)
        sp.dma_start(self.buf[:, k % self.SLOTS, :], self.B.g_scratch[k]).then_inc(self.s_loaded[k % self.SLOTS], 16)

    def make_high(self, act, k):
        act.wait_ge(self.s_loaded[k % self.SLOTS], 16 * (k // self.SLOTS + 1))
        self.B.nc.scalar.copy(self.high[k // KT][:, k % KT, :], self.buf[:, k % self.SLOTS, :]).then_inc(self.s_high, 1)

    def make_low(self, eng, k, sem):
        eng.wait_ge(self.s_high, k + 1)
        eng.tensor_tensor(self.low[k // KT][:, k % KT, :], self.buf[:, k % self.SLOTS, :],
                          self.high[k // KT][:, k % KT, :].bitcast(F32), ALU.subtract).then_inc(sem, 1)


def project_odd(B, w):
    nc = B.nc
    mark = B.top
    gated = Gated(B)
    U0 = B.unit
    par = lambda e: (U0 + e) % 2
    s_x = B.sem("x_loaded")
    w_of = lambda half, j, e: w[half][bass.ds(j * 2 + e, 1)].rearrange("o p k m -> p (o k) m")
    with nc.Block() as block:
        @block.sync
        def _(sp):
            B.load_weights(sp, U0, par(0), w[0][0])
            for k in range(gated.SLOTS):
                gated.load(sp, k)
            B.load_weights(sp, U0 + 1, par(1), w[0][1])
            for k in range(gated.SLOTS, KT):
                gated.load(sp, k)
            sp.dma_start(B.x[:], B.x_scratch).then_inc(s_x, 16)
            for j in range(1, 4):
                for e in range(2):
                    gated.load(sp, KT + 2 * (j - 1) + e)
                    B.load_weights(sp, j * 2 + (U0 + e), par(e), w_of(0, j, e))
            for e in range(2):
                gated.load(sp, KT + 6 + e)
            with sp.Fori(0, 4) as j:
                for e in range(2):
                    B.load_weights(sp, j * 2 + (U0 + 8 + e), par(e), w_of(1, j, e))

        @block.scalar
        def _(act):
            B.split_high(act, U0, par(0))
            for k in range(KT):
                gated.make_high(act, k)
            B.split_high(act, U0 + 1, par(1))
            for n in range(KT):
                gated.make_high(act, KT + n)
                B.split_high(act, U0 + 2 + n, par(n))
            with act.Fori(5, 8) as j:
                for e in range(2):
                    B.split_high(act, j * 2 + (U0 + e), par(e))

        @block.gpsimd
        def _(pool):
            B.split_low(pool, U0, par(0))
            for k in gated.POOL_K:
                gated.make_low(pool, k, gated.s_low_pool)
            B.split_low(pool, U0 + 1, par(1))
            for n in range(KT):
                gated.make_low(pool, KT + n, gated.s_low_pool)
                B.split_low(pool, U0 + 2 + n, par(n))
            with pool.Fori(5, 8) as j:
                for e in range(2):
                    B.split_low(pool, j * 2 + (U0 + e), par(e))

        @block.tensor
        def _(pe):
            gated.multiply_first(pe)
            B.multiply(pe, U0 + 1, par(1), B.hh, B.hl)
            with pe.Fori(1, 4) as j:
                for e in range(2):
                    B.multiply(pe, j * 2 + (U0 + e), par(e), B.hh, B.hl)
            pe.wait_ge(gated.s_high, 2 * KT)
            gated.await_low(pe, 2 * KT - 1)
            with pe.Fori(4, 8) as j:
                for e in range(2):
                    B.multiply(pe, j * 2 + (U0 + e), par(e), gated.high[1], gated.low[1])

        @block.vector
        def _(dve):
            for k in range(KT):
                if k not in gated.POOL_K:
                    gated.make_low(dve, k, gated.s_low_dve)
            dve.wait_ge(s_x, 16)
            for half in range(2):
                with dve.Fori(0, 4) as j:
                    for e in range(2):
                        for t in range(NT):
                            B.await_tile(dve, j * 2 + (U0 + 8 * half + e), t)
                            if half == 1:
                                dve.wait_ge(B.s_tile_free, j * 6 + ((U0 + e) * 3 + t + 7))
                            xs = B.x[:, bass.ds(j * 2 + e, 1), tcols(t)].rearrange("p o c -> p (o c)")
                            nc.vector.tensor_tensor(xs, xs, B.tile(par(e), t), ALU.add).then_inc(B.s_tile_free, 1)
    B.unit += 16
    B.top = mark


SHAPES_OUT = [
    ("y_prompt", (1, SEQ, D_MODEL)), ("y_sample", (NS, 1, D_MODEL)),
    ("k_prompt", (1, 1, SEQ, HA, DH)), ("v_prompt", (1, 1, SEQ, HA, DH)), ("idx_k_prompt", (1, 1, SEQ, DH)),
    ("k_sample", (1, NS, 1, HA, DH)), ("v_sample", (1, NS, 1, HA, DH)), ("idx_k_sample", (1, NS, 1, DH)),
    ("ret_prompt", (1, 1, HR, DKR, DVR)), ("ret_sample", (1, NS, HR, DKR, DVR)),
    ("conv_prompt", (1, 1, CW - 1, CONV_DIM)), ("conv_sample", (1, NS, CW - 1, CONV_DIM)),
    ("ssm_prompt", (1, 1, NH, PS, NST)), ("ssm_sample", (1, NS, NH, PS, NST)),
]


def build(nc, ins, outs):
    with ExitStack() as ctx:
        B = Build(nc, ctx, ins, outs)
        load_inputs(B)
        x_top = B.top
        B.x_scratch = nc.dram_tensor("x_scratch", (P, KT, TOK), F32, kind="Internal").ap()
        norm = Norm(B, 0, keep=B.x_scratch)
        B.top = B.x_base
        indexer(B, norm)
        project_and_choose(B)
        keys_and_values(B)
        attend(B)
        B.top = B.even_top
        attend_samples(B)
        B.top = B.retention_base
        retention(B)
        B.recycle()
        B.top = x_top
        project_add(B, B.i["w_out_even"][0].rearrange("(k p) (c m) -> c p k m", p=P, m=P))
        mlp(B, 0, Norm(B, 1))
        norm = Norm(B, 2, width=NH, keep=B.x_scratch)
        B.top = B.x_base
        time_steps(B, norm)
        mamba_groups(B)
        B.top = x_top
        w_out = B.i["w_out_odd"][0].rearrange("(g k p) (c m) -> g c p k m", k=KT, p=P, m=P)
        project_odd(B, w_out)
        mlp(B, 1, Norm(B, 3))
        normalize_final(B, 4)
        write_outputs(B)


INPUTS = ["x_prompt", "x_sample", "cache_k", "cache_v", "cache_idx_k", "state_ret", "state_conv", "state_ssm",
          "page_table", "rel_bias", "norm_mix", "norm_mlp", "norm_final", "w_in_even", "w_out_even", "w_in_odd",
          "conv_w", "conv_b", "dt_bias", "a_log", "d_skip", "ssm_norm", "w_out_odd", "w_up", "w_down"]


def kernel(**inputs):
    import numpy as _np
    import concourse.bacc as _bacc
    from concourse import mybir as _mybir
    from concourse.bass_utils import run_bass_kernel_spmd as _run

    nc = _bacc.Bacc("TRN2", target_bir_lowering=False, num_devices=1)
    arrays = {f"in_{n}": _np.ascontiguousarray(inputs[n]) for n in INPUTS}
    arrays.update({f"const_{n}": a for n, a in shape_constants().items()})
    ins = {n.split("_", 1)[1]: nc.dram_tensor(n, a.shape, _mybir.dt.from_np(a.dtype), kind="ExternalInput").ap()
           for n, a in arrays.items()}
    outs = {n: nc.dram_tensor(f"out_{n}", s, F32, kind="ExternalOutput").ap() for n, s in SHAPES_OUT}
    build(nc, ins, outs)
    r = _run(nc, [arrays], core_ids=[0])
    return tuple(r.results[0][f"out_{n}"] for n, _ in SHAPES_OUT)
```
